# Optimizing a Trainium2 kernel written in Bass

```python
import math
import jax, jax.numpy as jnp
from jax import lax
import numpy as np

D_MODEL = 1024
BATCH = 1
SEQ = 256
DEPTH = 1

ATT_HEADS = 8
ATT_KV_HEADS = 2
ATT_HEAD_DIM = 64
ATT_GROUP = ATT_HEADS // ATT_KV_HEADS
WINDOW = 128
BLOCK = 128
ML_HEADS = 4
ML_HEAD_DIM = 128
ML_CHUNK = 64
CONV_WIDTH = 4
MEM_LEN = 256
X_HEADS = 4
X_HEAD_DIM = 128
N_GROUPS = 4
EXPERTS_PER_GROUP = 8
N_EXPERTS = N_GROUPS * EXPERTS_PER_GROUP
TOP_K = 2
D_EXPERT = 512
MOE_BLOCK = 128
EPS = 1e-6

ATT_Q = ATT_HEADS * ATT_HEAD_DIM
ATT_KV = ATT_KV_HEADS * ATT_HEAD_DIM
ML_W = ML_HEADS * ML_HEAD_DIM
MIX_WIDTH = ATT_Q + ML_W
IN_SPLITS = [ATT_Q, ATT_KV, ATT_KV, 2 * ML_W, ML_W, ML_W, 2 * ML_HEADS]
IN_COLS = sum(IN_SPLITS)
IN_OFFSETS = [int(v) for v in np.cumsum(IN_SPLITS)[:-1]]


def rms_norm(x, g):
    xf = x.astype(jnp.float32)
    y = xf * lax.rsqrt(jnp.mean(xf * xf, axis=-1, keepdims=True) + EPS)
    return (y * g.astype(jnp.float32)).astype(x.dtype)

def alibi_slopes(n):
    return jnp.exp2(-8.0 * jnp.arange(1, n + 1, dtype=jnp.float32) / n)

def causal_depthwise_conv(x, w, b):
    c = x.shape[-1]
    y = lax.conv_general_dilated(x, w[:, None, :], window_strides=(1,),
                                 padding=[(CONV_WIDTH - 1, 0)],
                                 dimension_numbers=('NWC', 'WIO', 'NWC'),
                                 feature_group_count=c)
    return y + b

def sliding_window_gqa(q, k, v, sinks):
    bsz, s = q.shape[0], q.shape[1]
    nb = s // BLOCK
    qb = q.reshape(bsz, nb, BLOCK, ATT_KV_HEADS, ATT_GROUP, ATT_HEAD_DIM)

    def with_prev(t):
        t = t.reshape(bsz, nb, BLOCK, ATT_KV_HEADS, ATT_HEAD_DIM)
        prev = jnp.pad(t[:, :-1], ((0, 0), (1, 0), (0, 0), (0, 0), (0, 0)))
        return jnp.concatenate([prev, t], axis=2)

    kk, vv = with_prev(k), with_prev(v)
    scores = jnp.einsum('bnqkgd,bnskd->bkgnqs', qb, kk).astype(jnp.float32)
    scores = scores * (1.0 / math.sqrt(ATT_HEAD_DIM))
    dist = (jnp.arange(BLOCK)[:, None] + BLOCK) - jnp.arange(2 * BLOCK)[None, :]
    in_band = (dist >= 0) & (dist < WINDOW)
    pad_key = (jnp.arange(nb)[:, None, None] == 0) & (jnp.arange(2 * BLOCK)[None, None, :] < BLOCK)
    valid = in_band[None] & ~pad_key
    slopes = alibi_slopes(ATT_HEADS).reshape(ATT_KV_HEADS, ATT_GROUP)[:, :, None, None, None]
    logits = scores - slopes * dist.astype(jnp.float32)
    logits = jnp.where(valid, logits, -jnp.inf)
    sink = sinks.astype(jnp.float32).reshape(ATT_KV_HEADS, ATT_GROUP)[:, :, None, None, None]
    mx = jnp.maximum(logits.max(axis=-1, keepdims=True), sink)
    e = jnp.exp(logits - mx)
    p = e / (e.sum(axis=-1, keepdims=True) + jnp.exp(sink - mx))
    out = jnp.einsum('bkgnqs,bnskd->bnqkgd', p.astype(v.dtype), vv)
    return out.reshape(bsz, s, ATT_Q)

def mlstm_chunk_step(carry, inp):
    c_st, n_st, m_st = carry
    q, k, v, ig, lf = inp
    L = q.shape[2]
    b = jnp.cumsum(lf, axis=-1)
    causal = jnp.tril(jnp.ones((L, L), dtype=bool))
    log_d = jnp.where(causal, b[..., :, None] - b[..., None, :] + ig[..., None, :], -jnp.inf)
    m_inter = b + m_st[..., None]
    m_t = jnp.maximum(m_inter, log_d.max(axis=-1))
    s = jnp.einsum('bhtd,bhsd->bhts', q, k) * jnp.exp(log_d - m_t[..., None])
    a_inter = jnp.exp(m_inter - m_t)
    num = jnp.einsum('bhts,bhsd->bhtd', s, v) + a_inter[..., None] * jnp.einsum('bhtk,bhkv->bhtv', q, c_st)
    den = s.sum(axis=-1) + a_inter * jnp.einsum('bhtk,bhk->bht', q, n_st)
    h = num / jnp.maximum(jnp.abs(den), jnp.exp(-m_t))[..., None]
    b_last = b[..., -1]
    log_w = b_last[..., None] - b + ig
    m_new = jnp.maximum(b_last + m_st, log_w.max(axis=-1))
    w = jnp.exp(log_w - m_new[..., None])
    decay = jnp.exp(b_last + m_st - m_new)
    c_new = decay[..., None, None] * c_st + jnp.einsum('bhsk,bhsv->bhkv', k * w[..., None], v)
    n_new = decay[..., None] * n_st + jnp.einsum('bhs,bhsk->bhk', w, k)
    return (c_new, n_new, m_new), h

def mlstm(q, k, v, i_pre, f_pre):
    bsz, s, nh, dh = q.shape
    nc = s // ML_CHUNK
    f32 = jnp.float32
    def chunks(t):
        return t.astype(f32).reshape(bsz, nc, ML_CHUNK, nh, dh).transpose(1, 0, 3, 2, 4)
    def gchunks(t):
        return t.reshape(bsz, nc, ML_CHUNK, nh).transpose(1, 0, 3, 2)
    qc = chunks(q)
    kc = chunks(k) * (1.0 / math.sqrt(dh))
    vc = chunks(v)
    igc = gchunks(i_pre.astype(f32))
    lfc = gchunks(jax.nn.log_sigmoid(f_pre.astype(f32)))
    init = (jnp.zeros((bsz, nh, dh, dh), f32), jnp.zeros((bsz, nh, dh), f32), jnp.zeros((bsz, nh), f32))
    _, hs = lax.scan(mlstm_chunk_step, init, (qc, kc, vc, igc, lfc))
    return hs.transpose(1, 0, 3, 2, 4).reshape(bsz, s, nh, dh)

def memory_cross_attention(xn, memn, w_cq, w_ckv, w_co):
    bsz, s, _ = xn.shape
    q = (xn @ w_cq).reshape(bsz, s, X_HEADS, X_HEAD_DIM)
    kv = (memn @ w_ckv).reshape(bsz, memn.shape[1], 2, X_HEADS, X_HEAD_DIM)
    k, v = kv[:, :, 0], kv[:, :, 1]
    sc = jnp.einsum('bshd,bmhd->bhsm', q, k).astype(jnp.float32) * (1.0 / math.sqrt(X_HEAD_DIM))
    p = jax.nn.softmax(sc, axis=-1)
    o = jnp.einsum('bhsm,bmhd->bshd', p.astype(v.dtype), v).reshape(bsz, s, X_HEADS * X_HEAD_DIM)
    return o @ w_co

def hierarchical_moe(xn, w_rg, b_rg, w_re, b_re, w_g, w_u, w_d):
    bsz, s, d = xn.shape
    t = bsz * s
    xt = xn.reshape(t, d)
    g_logits = (xt @ w_rg).astype(jnp.float32) + b_rg.astype(jnp.float32)
    g_prob = jax.nn.softmax(g_logits, axis=-1)
    g_sel = jnp.argmax(g_logits, axis=-1)
    g_w = jnp.take_along_axis(g_prob, g_sel[:, None], axis=-1)
    e_logits = ((xt @ w_re).astype(jnp.float32) + b_re.astype(jnp.float32)).reshape(t, N_GROUPS, EXPERTS_PER_GROUP)
    e_in = jnp.take_along_axis(e_logits, g_sel[:, None, None], axis=1)[:, 0]
    top_v, top_i = lax.top_k(e_in, TOP_K)
    top_p = jax.nn.softmax(top_v, axis=-1) * g_w
    expert_idx = (g_sel[:, None] * EXPERTS_PER_GROUP + top_i).reshape(-1)
    gates = top_p.reshape(-1)
    n_assign = t * TOP_K
    token_idx = jnp.arange(n_assign) // TOP_K
    order = jnp.argsort(expert_idx)
    sorted_e = expert_idx[order]
    counts = jnp.bincount(expert_idx, length=N_EXPERTS)
    padded = (counts + MOE_BLOCK - 1) // MOE_BLOCK * MOE_BLOCK
    pad_end = jnp.cumsum(padded)
    pad_start = pad_end - padded
    start = jnp.cumsum(counts) - counts
    dest = pad_start[sorted_e] + (jnp.arange(n_assign) - start[sorted_e])
    n_blocks = -(-n_assign // MOE_BLOCK) + N_EXPERTS
    x_pad = jnp.zeros((n_blocks * MOE_BLOCK, d), xt.dtype).at[dest].set(xt[token_idx[order]])
    block_e = jnp.minimum(jnp.searchsorted(pad_end, jnp.arange(n_blocks) * MOE_BLOCK, side='right'), N_EXPERTS - 1)

    def expert_block(args):
        xb, e = args
        hb = jax.nn.silu(xb @ w_g[e]) * (xb @ w_u[e])
        return hb @ w_d[e]

    y_pad = lax.map(expert_block, (x_pad.reshape(n_blocks, MOE_BLOCK, d), block_e)).reshape(-1, d)
    y = y_pad[dest] * gates[order][:, None].astype(y_pad.dtype)
    out = jnp.zeros((t, d), xt.dtype).at[token_idx[order]].add(y)
    return out.reshape(bsz, s, d)

def first_inputs(seed: int = 0) -> dict:
    key = jax.random.key(seed)
    ks = iter(jax.random.split(key, 40))
    f32 = jnp.float32

    def nrm(shape, scale):
        return jax.random.normal(next(ks), shape, f32) * scale

    def gain(shape):
        return 1.0 + nrm(shape, 0.02)

    L = DEPTH
    x = nrm((BATCH, SEQ, D_MODEL), 1.0)
    mem = nrm((BATCH, MEM_LEN, D_MODEL), 1.0)
    b_i = nrm((L, ML_HEADS), 0.1)
    b_f = jnp.linspace(3.0, 6.0, ML_HEADS, dtype=f32)[None, :] + nrm((L, ML_HEADS), 0.01)
    return {
        'x': x,
        'mem': mem,
        'norm_mix': gain((L, D_MODEL)),
        'w_in': nrm((L, D_MODEL, IN_COLS), D_MODEL ** -0.5),
        'b_gates': jnp.concatenate([b_i, b_f], axis=-1),
        'conv_w': nrm((L, CONV_WIDTH, 2 * ML_W), CONV_WIDTH ** -0.5),
        'conv_b': nrm((L, 2 * ML_W), 0.01),
        'att_sinks': nrm((L, ATT_HEADS), 0.5),
        'norm_att_out': gain((L, ATT_Q)),
        'norm_ml_out': gain((L, ML_W)),
        'w_out': nrm((L, MIX_WIDTH, D_MODEL), MIX_WIDTH ** -0.5),
        'norm_cross': gain((L, D_MODEL)),
        'norm_mem': gain((L, D_MODEL)),
        'w_cq': nrm((L, D_MODEL, X_HEADS * X_HEAD_DIM), D_MODEL ** -0.5),
        'w_ckv': nrm((L, D_MODEL, 2 * X_HEADS * X_HEAD_DIM), D_MODEL ** -0.5),
        'w_co': nrm((L, X_HEADS * X_HEAD_DIM, D_MODEL), (X_HEADS * X_HEAD_DIM) ** -0.5),
        'norm_ffn': gain((L, D_MODEL)),
        'w_router_group': nrm((L, D_MODEL, N_GROUPS), D_MODEL ** -0.5),
        'b_router_group': nrm((L, N_GROUPS), 0.01),
        'w_router_expert': nrm((L, D_MODEL, N_EXPERTS), D_MODEL ** -0.5),
        'b_router_expert': nrm((L, N_EXPERTS), 0.01),
        'w_e_gate': nrm((L, N_EXPERTS, D_MODEL, D_EXPERT), D_MODEL ** -0.5),
        'w_e_up': nrm((L, N_EXPERTS, D_MODEL, D_EXPERT), D_MODEL ** -0.5),
        'w_e_down': nrm((L, N_EXPERTS, D_EXPERT, D_MODEL), D_EXPERT ** -0.5),
        'norm_final': gain((D_MODEL,)),
    }

def first_block(x, mem, norm_mix, w_in, b_gates, conv_w, conv_b, att_sinks, norm_att_out,
              norm_ml_out, w_out, norm_cross, norm_mem, w_cq, w_ckv, w_co, norm_ffn,
              w_router_group, b_router_group, w_router_expert, b_router_expert,
              w_e_gate, w_e_up, w_e_down, norm_final):
    bsz, s, _ = x.shape
    for l in range(DEPTH):
        h = rms_norm(x, norm_mix[l])
        proj = h @ w_in[l]
        q_a, k_a, v_a, qk_m, v_m, o_m, g_m = jnp.split(proj, IN_OFFSETS, axis=-1)
        att = sliding_window_gqa(q_a.reshape(bsz, s, ATT_HEADS, ATT_HEAD_DIM),
                                 k_a.reshape(bsz, s, ATT_KV_HEADS, ATT_HEAD_DIM),
                                 v_a.reshape(bsz, s, ATT_KV_HEADS, ATT_HEAD_DIM),
                                 att_sinks[l])
        att = rms_norm(att, norm_att_out[l])
        qk_m = jax.nn.silu(causal_depthwise_conv(qk_m, conv_w[l], conv_b[l]))
        q_m, k_m = jnp.split(qk_m, 2, axis=-1)
        g_m = g_m + b_gates[l]
        i_pre, f_pre = g_m[..., :ML_HEADS], g_m[..., ML_HEADS:]
        hm = mlstm(q_m.reshape(bsz, s, ML_HEADS, ML_HEAD_DIM),
                   k_m.reshape(bsz, s, ML_HEADS, ML_HEAD_DIM),
                   v_m.reshape(bsz, s, ML_HEADS, ML_HEAD_DIM), i_pre, f_pre)
        hm = jax.nn.sigmoid(o_m.astype(jnp.float32)).reshape(bsz, s, ML_HEADS, ML_HEAD_DIM) * hm
        hm = rms_norm(hm.astype(x.dtype), norm_ml_out[l].reshape(ML_HEADS, ML_HEAD_DIM)).reshape(bsz, s, ML_W)
        x = x + jnp.concatenate([att, hm], axis=-1) @ w_out[l]
        x = x + memory_cross_attention(rms_norm(x, norm_cross[l]), rms_norm(mem, norm_mem[l]),
                                       w_cq[l], w_ckv[l], w_co[l])
        x = x + hierarchical_moe(rms_norm(x, norm_ffn[l]), w_router_group[l], b_router_group[l],
                                 w_router_expert[l], b_router_expert[l],
                                 w_e_gate[l], w_e_up[l], w_e_down[l])
    return rms_norm(x, norm_final)


DEPTH_2 = 2

N_MIXERS = 4
D_FF = 2816
REL_BUCKETS = 32
REL_MAX_DIST = 2048
REL_HEADS = 8
A_HEADS = 8
A_HEAD_DIM = D_MODEL // A_HEADS
IDX_HEADS = 8
IDX_DIM = 64
TOPK_MAX = 256
Q_BLOCK = 128
A_SPLITS = (D_MODEL, 2 * D_MODEL, 3 * D_MODEL,
            3 * D_MODEL + IDX_HEADS * IDX_DIM,
            3 * D_MODEL + IDX_HEADS * IDX_DIM + IDX_DIM)
A_IN = 3 * D_MODEL + IDX_HEADS * IDX_DIM + IDX_DIM + IDX_HEADS
B_CHUNK = 128
B_HALF = 3 * D_MODEL
B_GROUPS = 8
C_KERNEL = 31
D_PAIRS = ((128, 1), (512, 4), (2048, 16))
D_NGROUPS = len(D_PAIRS)
D_HEADS = 8
D_HEAD_DIM = 64
D_BLOCK = 128
D_SPAN = D_BLOCK * max(dil for _, dil in D_PAIRS)
D_IN = 3 * D_NGROUPS * D_HEADS * D_HEAD_DIM
D_OUT = D_HEADS * D_HEAD_DIM

def n_uses(m):
    return (DEPTH_2 - m + N_MIXERS - 1) // N_MIXERS


def rmsnorm(x, g):
    xf = x.astype(jnp.float32)
    y = xf * lax.rsqrt(jnp.mean(xf * xf, axis=-1, keepdims=True) + EPS)
    return (y * g.astype(jnp.float32)).astype(x.dtype)

def layernorm(x, g, b):
    xf = x.astype(jnp.float32)
    mu = jnp.mean(xf, axis=-1, keepdims=True)
    var = jnp.mean(jnp.square(xf - mu), axis=-1, keepdims=True)
    y = (xf - mu) * lax.rsqrt(var + EPS)
    return (y * g.astype(jnp.float32) + b.astype(jnp.float32)).astype(x.dtype)

def swiglu(x, w_in, w_out):
    gate, up = jnp.split(x @ w_in, 2, axis=-1)
    return (jax.nn.silu(gate) * up) @ w_out

def rel_bucket(dist):
    max_exact = REL_BUCKETS // 2
    d = jnp.maximum(dist, 0)
    df = jnp.maximum(d, 1).astype(jnp.float32)
    large = max_exact + (jnp.log(df / max_exact) / math.log(REL_MAX_DIST / max_exact)
                         * (REL_BUCKETS - max_exact)).astype(jnp.int32)
    large = jnp.minimum(large, REL_BUCKETS - 1)
    return jnp.where(d < max_exact, d, large)

def mixer_a(h, w_in, w_out, rel_table):
    B_, S, _ = h.shape
    q, k, v, qi, ki, wi = jnp.split(h @ w_in, A_SPLITS, axis=-1)
    q = q.reshape(B_, S, A_HEADS, A_HEAD_DIM)
    k = k.reshape(B_, S, A_HEADS, A_HEAD_DIM)
    v = v.reshape(B_, S, A_HEADS, A_HEAD_DIM)
    qi = qi.reshape(B_, S, IDX_HEADS, IDX_DIM)
    wi = wi * (IDX_HEADS ** -0.5)
    top_k = min(TOPK_MAX, S // 4)
    nb = S // Q_BLOCK
    key_pos = jnp.arange(S)
    scale = A_HEAD_DIM ** -0.5
    gather = jax.vmap(lambda arr, ix: arr[ix])

    def block(i):
        start = i * Q_BLOCK
        q_pos = start + jnp.arange(Q_BLOCK)
        qb = lax.dynamic_slice_in_dim(q, start, Q_BLOCK, axis=1)
        qib = lax.dynamic_slice_in_dim(qi, start, Q_BLOCK, axis=1)
        wib = lax.dynamic_slice_in_dim(wi, start, Q_BLOCK, axis=1)
        rel = jax.nn.relu(jnp.einsum('bthd,bsd->bths', qib, ki).astype(jnp.float32) * (IDX_DIM ** -0.5))
        score = jnp.einsum('bth,bths->bts', wib.astype(jnp.float32), rel)
        causal = key_pos[None, :] <= q_pos[:, None]
        score = jnp.where(causal[None], score, -jnp.inf)
        _, idx = lax.top_k(score, top_k)
        valid = idx <= q_pos[None, :, None]
        kg = gather(k, idx)
        vg = gather(v, idx)
        bias = rel_table[rel_bucket(q_pos[None, :, None] - idx)]
        logits = (jnp.einsum('bthe,btkhe->bhtk', qb, kg).astype(jnp.float32) * scale
                  + jnp.transpose(bias, (0, 3, 1, 2)).astype(jnp.float32))
        logits = jnp.where(valid[:, None], logits, -jnp.inf)
        p = jax.nn.softmax(logits, axis=-1)
        o = jnp.einsum('bhtk,btkhe->bthe', p, vg)
        return o.reshape(B_, Q_BLOCK, D_MODEL)

    out = lax.map(block, jnp.arange(nb))
    out = jnp.transpose(out, (1, 0, 2, 3)).reshape(B_, S, D_MODEL).astype(h.dtype)
    return out @ w_out

def mixer_b(h, w_in, b_in, ln_g, ln_b, w_sp, b_sp, w_out):
    B_, S, _ = h.shape
    z = jax.nn.gelu(h @ w_in + b_in)
    u, v = jnp.split(z, 2, axis=-1)
    v = layernorm(v, ln_g, ln_b)
    nc = S // B_CHUNK
    v = v.reshape(B_, nc, B_CHUNK, B_GROUPS, B_HALF // B_GROUPS)
    tri = jnp.tril(jnp.ones((B_CHUNK, B_CHUNK), dtype=bool))
    w = jnp.where(tri[None], w_sp, jnp.zeros((), w_sp.dtype))
    sv = jnp.einsum('gts,bcsgd->bctgd', w, v) + jnp.transpose(b_sp)[None, None, :, :, None]
    y = u * sv.reshape(B_, S, B_HALF)
    return y @ w_out

def mixer_c(h, w_pw1, b_pw1, w_dw, b_dw, ln_g, ln_b, w_pw2, b_pw2):
    a, g = jnp.split(h @ w_pw1 + b_pw1, 2, axis=-1)
    y = a * jax.nn.sigmoid(g)
    y = lax.conv_general_dilated(y, w_dw[:, None, :], window_strides=(1,),
                                 padding=((C_KERNEL - 1, 0),),
                                 dimension_numbers=('NWC', 'WIO', 'NWC'),
                                 feature_group_count=D_MODEL) + b_dw
    y = jax.nn.silu(layernorm(y, ln_g, ln_b))
    return y @ w_pw2 + b_pw2

def dilated_group(q, k, v, window, dil, rel_table):
    B_, Sp, H, E = q.shape
    n = Sp // dil
    nb = n // D_BLOCK

    def to_sub(t):
        t = jnp.swapaxes(t.reshape(B_, n, dil, H, E), 1, 2)
        return t.reshape(B_, dil, nb, D_BLOCK, H, E)

    def band(t):
        prev = jnp.pad(t, ((0, 0), (0, 0), (1, 0), (0, 0), (0, 0), (0, 0)))[:, :, :-1]
        return jnp.concatenate([prev, t], axis=3)

    qs = to_sub(q)
    kb = band(to_sub(k))
    vb = band(to_sub(v))
    steps = window // dil
    p_loc = jnp.arange(D_BLOCK)[:, None]
    j_loc = jnp.arange(2 * D_BLOCK)[None, :]
    m = p_loc + D_BLOCK - j_loc
    in_win = (m >= 0) & (m <= steps)
    first = (jnp.arange(nb) == 0)[:, None, None] & (j_loc < D_BLOCK)[None]
    mask = in_win[None] & ~first
    bias = jnp.transpose(rel_table[rel_bucket(m * dil)], (2, 0, 1)).astype(jnp.float32)
    logits = jnp.einsum('brnqhe,brnkhe->brnhqk', qs, kb).astype(jnp.float32) * (E ** -0.5) + bias
    logits = jnp.where(mask[None, None, :, None], logits, -jnp.inf)
    mx = jnp.max(logits, axis=-1, keepdims=True)
    e = jnp.exp(logits - mx)
    l = jnp.sum(e, axis=-1, keepdims=True)
    o = jnp.einsum('brnhqk,brnkhe->brnqhe', e / l, vb)
    lse = jnp.swapaxes((mx + jnp.log(l))[..., 0], -1, -2)

    def from_sub(t):
        rest = t.shape[4:]
        t = t.reshape((B_, dil, n) + rest)
        return jnp.swapaxes(t, 1, 2).reshape((B_, Sp) + rest)

    return from_sub(o), from_sub(lse)

def mixer_d(h, w_in, w_out, rel_table):
    B_, S, _ = h.shape
    Sp = -(-S // D_SPAN) * D_SPAN
    proj = jnp.pad(h @ w_in, ((0, 0), (0, Sp - S), (0, 0)))
    proj = proj.reshape(B_, Sp, 3, D_NGROUPS, D_HEADS, D_HEAD_DIM)
    outs, lses = [], []
    for g, (window, dil) in enumerate(D_PAIRS):
        o, lse = dilated_group(proj[:, :, 0, g], proj[:, :, 1, g], proj[:, :, 2, g],
                               window, dil, rel_table)
        outs.append(o)
        lses.append(lse)
    alpha = jax.nn.softmax(jnp.stack(lses, 0), axis=0)
    y = jnp.sum(alpha[..., None] * jnp.stack(outs, 0), axis=0)
    y = y[:, :S].reshape(B_, S, D_OUT).astype(h.dtype)
    return y @ w_out

def second_inputs(seed: int = 0) -> dict:
    key = jax.random.key(seed)
    ks = jax.random.split(key, 32)
    nrm = lambda k, shape, s: jax.random.normal(k, shape, jnp.float32) * s
    nA, nB, nC, nD = n_uses(0), n_uses(1), n_uses(2), n_uses(3)
    D = D_MODEL
    return {
        "x": nrm(ks[0], (BATCH, SEQ, D), 1.0),
        "norm_g": 1.0 + nrm(ks[1], (DEPTH_2, 3, D), 0.05),
        "final_g": 1.0 + nrm(ks[2], (D,), 0.05),
        "ffn_w_in": nrm(ks[3], (DEPTH_2, 2, D, 2 * D_FF), D ** -0.5),
        "ffn_w_out": nrm(ks[4], (DEPTH_2, 2, D_FF, D), D_FF ** -0.5),
        "rel_table": nrm(ks[5], (REL_BUCKETS, REL_HEADS), 0.5),
        "a_w_in": nrm(ks[6], (nA, D, A_IN), D ** -0.5),
        "a_w_out": nrm(ks[7], (nA, D, D), D ** -0.5),
        "b_w_in": nrm(ks[8], (nB, D, 2 * B_HALF), D ** -0.5),
        "b_b_in": nrm(ks[9], (nB, 2 * B_HALF), 0.02),
        "b_ln_g": 1.0 + nrm(ks[10], (nB, B_HALF), 0.05),
        "b_ln_b": nrm(ks[11], (nB, B_HALF), 0.02),
        "b_w_sp": nrm(ks[12], (nB, B_GROUPS, B_CHUNK, B_CHUNK), B_CHUNK ** -0.5),
        "b_b_sp": 1.0 + nrm(ks[13], (nB, B_GROUPS, B_CHUNK), 0.05),
        "b_w_out": nrm(ks[14], (nB, B_HALF, D), B_HALF ** -0.5),
        "c_w_pw1": nrm(ks[15], (nC, D, 2 * D), D ** -0.5),
        "c_b_pw1": nrm(ks[16], (nC, 2 * D), 0.02),
        "c_w_dw": nrm(ks[17], (nC, C_KERNEL, D), C_KERNEL ** -0.5),
        "c_b_dw": nrm(ks[18], (nC, D), 0.02),
        "c_ln_g": 1.0 + nrm(ks[19], (nC, D), 0.05),
        "c_ln_b": nrm(ks[20], (nC, D), 0.02),
        "c_w_pw2": nrm(ks[21], (nC, D, D), D ** -0.5),
        "c_b_pw2": nrm(ks[22], (nC, D), 0.02),
        "d_w_in": nrm(ks[23], (nD, D, D_IN), D ** -0.5),
        "d_w_out": nrm(ks[24], (nD, D_OUT, D), D_OUT ** -0.5),
    }

def second_block(x, norm_g, final_g, ffn_w_in, ffn_w_out, rel_table,
              a_w_in, a_w_out,
              b_w_in, b_b_in, b_ln_g, b_ln_b, b_w_sp, b_b_sp, b_w_out,
              c_w_pw1, c_b_pw1, c_w_dw, c_b_dw, c_ln_g, c_ln_b, c_w_pw2, c_b_pw2,
              d_w_in, d_w_out):
    h = x
    for i in range(DEPTH_2):
        kind, j = i % N_MIXERS, i // N_MIXERS
        h = h + 0.5 * swiglu(rmsnorm(h, norm_g[i, 0]), ffn_w_in[i, 0], ffn_w_out[i, 0])
        hn = rmsnorm(h, norm_g[i, 1])
        if kind == 0:
            y = mixer_a(hn, a_w_in[j], a_w_out[j], rel_table)
        elif kind == 1:
            y = mixer_b(hn, b_w_in[j], b_b_in[j], b_ln_g[j], b_ln_b[j], b_w_sp[j], b_b_sp[j], b_w_out[j])
        elif kind == 2:
            y = mixer_c(hn, c_w_pw1[j], c_b_pw1[j], c_w_dw[j], c_b_dw[j], c_ln_g[j], c_ln_b[j],
                        c_w_pw2[j], c_b_pw2[j])
        else:
            y = mixer_d(hn, d_w_in[j], d_w_out[j], rel_table)
        h = h + y
        h = h + 0.5 * swiglu(rmsnorm(h, norm_g[i, 2]), ffn_w_in[i, 1], ffn_w_out[i, 1])
    return rmsnorm(h, final_g)


def setup_inputs(seed=0):
    out = dict(first_inputs(seed))
    for name, value in second_inputs(seed + 1).items():
        if name != "x":
            out[name + "_2"] = value
    return out


def reference(
    x, mem, norm_mix, w_in, b_gates, conv_w, conv_b, att_sinks, norm_att_out, norm_ml_out,
    w_out, norm_cross, norm_mem, w_cq, w_ckv, w_co, norm_ffn, w_router_group, b_router_group,
    w_router_expert, b_router_expert, w_e_gate, w_e_up, w_e_down, norm_final, norm_g_2,
    final_g_2, ffn_w_in_2, ffn_w_out_2, rel_table_2, a_w_in_2, a_w_out_2, b_w_in_2, b_b_in_2,
    b_ln_g_2, b_ln_b_2, b_w_sp_2, b_b_sp_2, b_w_out_2, c_w_pw1_2, c_b_pw1_2, c_w_dw_2, c_b_dw_2,
    c_ln_g_2, c_ln_b_2, c_w_pw2_2, c_b_pw2_2, d_w_in_2, d_w_out_2,
):
    x = first_block(
        x, mem, norm_mix, w_in, b_gates, conv_w, conv_b, att_sinks, norm_att_out, norm_ml_out,
        w_out, norm_cross, norm_mem, w_cq, w_ckv, w_co, norm_ffn, w_router_group,
        b_router_group, w_router_expert, b_router_expert, w_e_gate, w_e_up, w_e_down,
        norm_final,
    )
    return second_block(
        x, norm_g_2, final_g_2, ffn_w_in_2, ffn_w_out_2, rel_table_2, a_w_in_2, a_w_out_2,
        b_w_in_2, b_b_in_2, b_ln_g_2, b_ln_b_2, b_w_sp_2, b_b_sp_2, b_w_out_2, c_w_pw1_2,
        c_b_pw1_2, c_w_dw_2, c_b_dw_2, c_ln_g_2, c_ln_b_2, c_w_pw2_2, c_b_pw2_2, d_w_in_2,
        d_w_out_2,
    )


_drawn_inputs = setup_inputs


def setup_inputs(seed=0):
    import zlib

    import numpy as np

    out = dict(_drawn_inputs(seed))
    spreads = {}
    factors = {'norm_cross': 8.0,
     'norm_mem': 4.162,
     'b_router_group': 16.131,
     'b_router_expert': 4.452,
     'b_b_in_2': 4.06,
     'b_ln_g_2': 3.416,
     'b_ln_b_2': 8.0,
     'norm_ffn': 3.106,
     'b_b_sp_2': 3.334}
    for name, (base, spread) in spreads.items():
        noise = np.random.default_rng([zlib.crc32(name.encode()), seed]).standard_normal(out[name].shape)
        drawn = base * np.exp(spread * noise) if base else spread * noise
        out[name] = __import__('jax').numpy.asarray(drawn.astype(out[name].dtype))
    for name, factor in factors.items():
        out[name] = (out[name] * factor).astype(out[name].dtype)
    return out
```

```python
import numpy as np
import concourse.bass as bass
from concourse import mybir
from contextlib import ExitStack

F32 = mybir.dt.float32
ALU = mybir.AluOpType
ACT = mybir.ActivationFunctionType
AX = mybir.AxisListType

NEG = -1.0e30
GONE = -3.0e38
RING = 5
CONST_AT = {"ident": (0, 128), "upper": (128, 512), "eye": (640, 512), "alibi": (1152, 2048),
            "causal": (3200, 512), "iota": (3712, 32), "ones": (3744, 128)}
CONST_W = 3872


def head_at(n):
    return 2 * (n % 4) + n // 4


def shape_constants():
    p = np.arange(128)[:, None]
    s = np.arange(256)[None, :]
    c = np.zeros((128, CONST_W), np.float32)

    def put(name, a):
        o, n = CONST_AT[name]
        c[:, o:o + n] = a.reshape(128, n)

    put("ident", np.eye(128))
    put("upper", np.stack([(p + 128 * j) <= s for j in range(2)], 1).astype(np.float32))
    put("eye", np.stack([(p + 128 * j) == s for j in range(2)], 1).astype(np.float32))
    dist = p + 128 - s
    ok = (dist >= 0) & (dist < 128)
    put("alibi", np.stack([np.where(ok, -(2.0 ** -(head_at(n) + 1)) * dist, NEG) for n in range(8)], 1))
    put("causal", np.stack([np.where(s <= p + 128 * t, 0.0, NEG) for t in range(2)], 1))
    put("iota", np.broadcast_to(np.arange(32), (128, 32)))
    put("ones", np.ones((128, 128)))
    hot = np.zeros((32, 512), np.float32)
    for j in range(256):
        d = 255 - j
        b = d if d < 16 else min(31, 16 + int(np.log(d / 16.0) / np.log(128.0) * 16))
        hot[b, j] = 1.0
    return c, hot


class Lane:

    def __init__(self, eng, sem):
        self.eng, self.sem, self.n, self.last, self.seen = eng, sem, 0, None, {}

    def wait(self, *tokens):
        for sem, value in tokens:
            if value > self.seen.get(sem.name, 0):
                self.seen[sem.name] = value
                self.eng.wait_ge(sem, value)

    def mark(self):
        if self.last is not None:
            self.last.then_inc(self.sem, 1)
            self.last = None
            self.n += 1
        return (self.sem, self.n)

    def put(self, fn):
        self.last = fn(self.eng)

    def step(self, fn, *tokens):
        self.wait((self.sem, self.n), *tokens)
        fn(self.eng).then_inc(self.sem, 1)
        self.n += 1
        return (self.sem, self.n)


def build(nc, a, out):
    with ExitStack() as ctx:
        assemble(nc, a, out, ctx)


def assemble(nc, a, out, ctx):
    def sem(name):
        return ctx.enter_context(nc.semaphore(name))

    def sb(name, shape):
        return ctx.enter_context(nc.sbuf_tensor(name, shape, F32))

    PE, V, S = Lane(nc.tensor, sem("s_pe")), Lane(nc.vector, sem("s_v")), Lane(nc.scalar, sem("s_s"))
    G, SP = Lane(nc.gpsimd, sem("s_g")), Lane(nc.sync, sem("s_sp"))
    dma_count = {}

    def dma(lane, name, dst, src, *tokens):
        if name not in dma_count:
            dma_count[name] = [sem("d_" + name), 0]
        lane.wait(*tokens)
        d = dma_count[name]
        d[1] += 16
        lane.eng.dma_start(dst, src).then_inc(d[0], 16)
        return (d[0], d[1])

    def fence(*tokens):
        marks = [(V.sem, V.n), (S.sem, S.n), (G.sem, G.n), PE.mark()]
        for lane in (PE, V, S, G):
            lane.wait(*marks, *tokens)
        return marks

    cst = sb("cst", [128, CONST_W])
    hot = sb("hot", [32, 512])
    gc = sb("gc", [128, 128])
    rows = sb("rows", [128, 128])
    X = sb("X", [128, 2, 1024])
    XT = sb("XT", [128, 8, 256])
    gfin = sb("gfin", [128, 2, 1024])
    small = sb("small", [128, 512])
    ring = sb("ring", [128, RING, 4096])
    arena = sb("arena", [128, 20400])
    PS = ctx.enter_context(nc.psum_tensor("PS", [128, 4096], F32))
    toep = nc.dram_tensor("toep", (8, 128, 512), F32, kind="Internal").ap()

    def C(name):
        o, n = CONST_AT[name]
        return cst[:, o:o + n]

    ident = C("ident")
    upper = C("upper").rearrange("p (j s) -> p j s", j=2)
    eye = C("eye").rearrange("p (j s) -> p j s", j=2)
    alibi = C("alibi").rearrange("p (h s) -> p h s", h=8)
    causal = C("causal").rearrange("p (t s) -> p t s", t=2)
    iota = C("iota")
    ones = C("ones")

    top = [0]

    def room(*dims):
        n = 1
        for d in dims:
            n *= d
        o = top[0]
        top[0] += n
        assert top[0] <= 20400, top[0]
        v = arena[:, o:o + n]
        if len(dims) == 2:
            v = v.rearrange("p (a b) -> p a b", a=dims[0])
        if len(dims) == 3:
            v = v.rearrange("p (a b c) -> p a b c", a=dims[0], b=dims[1])
        return v

    used = [0]

    def tiny(n):
        o = used[0]
        used[0] += n
        assert used[0] <= 512, used[0]
        return small[:, o:o + n]

    rel = [(PE.sem, 0)] * 8

    def bank(b, n=512, o=0):
        return PS[:, b * 512 + o:b * 512 + o + n]

    def take(*banks):
        for b in banks:
            PE.wait(rel[b])

    def give(token, *banks):
        for b in banks:
            rel[b] = token

    units = []

    def cols(w, c0, c1):
        src = w.rearrange("(k p) n -> p k n", p=128)[:, :, c0:c1]
        units.append([(0, 8, 0, c1 - c0, c1 - c0, src)])

    def pair(w, c0, u0, n):
        r = w.rearrange("(k p) n -> p k n", p=128)
        units.append([(0, 8, 0, n, 2 * n, r[:, :, c0:c0 + n]), (0, 8, n, 2 * n, 2 * n, r[:, :, u0:u0 + n])])

    def deep(w, r0, nk):
        src = w[r0:r0 + nk * 128, :].rearrange("(k p) n -> p k n", p=128)
        units.append([(0, nk, 0, 1024, 1024, src)])

    w_in = a["w_in"][0]
    for c in range(0, 2824, 512):
        cols(w_in, c, min(c + 512, 2824))
    cols(a["w_ckv"][0], 0, 512)
    cols(a["w_ckv"][0], 512, 1024)
    cols(a["w_out"][0], 0, 512)
    cols(a["w_out"][0], 512, 1024)
    cols(a["w_cq"][0], 0, 512)
    deep(a["w_co"][0], 0, 4)
    for e in range(32):
        cols(a["w_e_gate"][0, e], 0, 512)
        cols(a["w_e_up"][0, e], 0, 512)
        if e:
            deep(a["w_e_down"][0, e - 1], 0, 4)
    deep(a["w_e_down"][0, 31], 0, 4)

    def ffn_units(i, j):
        for c in range(11):
            pair(a["ffn_w_in_2"][i, j], 256 * c, 2816 + 256 * c, 256)
        for c in range(6):
            deep(a["ffn_w_out_2"][i, j], 512 * c, min(4, 22 - 4 * c))

    ffn_units(0, 0)
    for c in range(0, 3656, 512):
        cols(a["a_w_in_2"][0], c, min(c + 512, 3656))
    cols(a["a_w_out_2"][0], 0, 512)
    cols(a["a_w_out_2"][0], 512, 1024)
    ffn_units(0, 1)
    ffn_units(1, 0)
    for c in range(6):
        cols(a["b_w_in_2"][0], 3072 + 512 * c, 3584 + 512 * c)
    for c in range(6):
        cols(a["b_w_in_2"][0], 512 * c, 512 * c + 512)
    for c in range(6):
        deep(a["b_w_out_2"][0], 512 * c, 4)
    ffn_units(1, 1)

    loaded = {}
    at = {"next": 0, "load": 0}

    def load_next(*tokens):
        i = at["load"]
        if i >= len(units):
            return
        at["load"] += 1
        slot = i % RING
        for k0, k1, c0, c1, w, src in units[i]:
            dst = ring[:, slot, 0:(k1 - k0) * w].rearrange("p (k n) -> p k n", n=w)[:, :, c0:c1]
            loaded[i] = dma(SP, f"w{slot}", dst, src, *tokens)

    def unit():
        i = at["next"]
        at["next"] += 1
        PE.wait(loaded[i])
        k1, w = units[i][0][1], units[i][0][4]
        return i, ring[:, i % RING, 0:k1 * w].rearrange("p (k n) -> p k n", n=w)

    freed = {}

    def done(i):
        freed[i] = PE.mark()
        while at["load"] < len(units) and at["load"] - RING in freed:
            load_next(freed[at["load"] - RING])

    mem = room(2, 1024)
    t_x = dma(SP, "x", X[:, :, :], a["x"][0].rearrange("(t p) n -> p t n", p=128))
    t_c = dma(SP, "c", cst[:, :], a["cst"])
    t_mem = dma(SP, "m", mem, a["mem"][0].rearrange("(t p) n -> p t n", p=128))

    GAIN = {}
    row_at = 0
    t_r = None
    for name, src, n in (("mix", a["norm_mix"][0], 8), ("att", a["norm_att_out"][0], 4),
                         ("ml", a["norm_ml_out"][0], 4), ("cross", a["norm_cross"][0], 8),
                         ("mem", a["norm_mem"][0], 8), ("ffn", a["norm_ffn"][0], 8),
                         ("convb", a["conv_b"][0], 8)):
        t_r = dma(S, "r", rows[row_at:row_at + n, :], src.rearrange("(k p) -> k p", p=128))
        GAIN[name] = row_at
        row_at += n
    t_r = dma(S, "r", rows[row_at:row_at + 32, :], a["conv_w"][0].rearrange("w (k p) -> (w k) p", p=128))
    GAIN["convw"] = row_at
    row_at += 32
    t_r = dma(S, "r", rows[row_at:row_at + 48, :], a["norm_g_2"].rearrange("i j (k p) -> (i j k) p", p=128))
    GAIN["g2"] = row_at
    row_at += 48
    assert row_at == 128
    for _ in range(RING):
        load_next()

    sink = tiny(8)
    bgate = tiny(8)
    brout = tiny(36)
    sink_in = tiny(8)
    t_b = dma(S, "b", sink_in, a["att_sinks"].broadcast_to([128, 8]))
    t_b = dma(S, "b", bgate, a["b_gates"].broadcast_to([128, 8]))
    t_b = dma(S, "b", brout[:, 0:4], a["b_router_group"].broadcast_to([128, 4]))
    t_b = dma(S, "b", brout[:, 4:36], a["b_router_expert"].broadcast_to([128, 32]))
    t_b = dma(S, "b", gfin[:, 0, :], a["norm_final"].rearrange("(a n) -> a n", a=1).broadcast_to([128, 1024]))
    t_b = dma(S, "b", gfin[:, 1, :], a["final_g_2"].rearrange("(a n) -> a n", a=1).broadcast_to([128, 1024]))
    rtab = tiny(8)
    t_b = dma(S, "b", hot[:, :], a["hot"])
    t_b = dma(S, "b", rtab[0:32, :], a["rel_table_2"])

    PE.wait(t_c, t_r)
    PE.put(lambda e: e.transpose(bank(7, 128), rows[:, :], ident))
    t_gc = V.step(lambda e: e.tensor_copy(gc[:, :], bank(7, 128)), PE.mark())
    give(t_gc, 7)

    def col(name, k=0, n=1):
        o = GAIN[name] + k
        return gc[:, o:o + n]

    mhalf = tiny(8)
    V.step(lambda e: e.memset(mhalf, -0.5))

    def rsqrt(x, n):
        t_g = G.step(lambda e: e.tensor_tensor(x, x, mhalf[:, 0:n], ALU.pow), (V.sem, V.n))
        V.wait(t_g)

    ss = tiny(2)
    rstd = tiny(2)

    def rms_scale(src, dst, junk, *tokens, width=1024):
        for t in range(2):
            t_ss = S.step(lambda e, t=t: e.activation(junk[:, 0:width], src[:, t, :], ACT.Square,
                                                      accum_out=ss[:, t:t + 1]), *tokens)
        V.step(lambda e: e.tensor_scalar(rstd, ss, 1.0 / width, 1e-6, ALU.mult, ALU.add), t_ss, *tokens)
        rsqrt(rstd, 2)
        for t in range(2):
            t_v = V.step(lambda e, t=t: e.tensor_scalar(dst[:, t, :], src[:, t, :], rstd[:, t:t + 1], None, ALU.mult))
        return t_v

    def flip(src, nk, dst, gain, *tokens, banks=(0, 1, 2, 3)):
        PE.wait(*tokens)
        n = 0
        t_v = None
        for t in range(2):
            for k0 in range(0, nk, 4):
                b = banks[n % len(banks)]
                n += 1
                m = min(4, nk - k0)
                take(b)
                for k in range(m):
                    PE.put(lambda e, b=b, k=k, t=t, k0=k0: e.transpose(
                        bank(b, 128, 128 * k), src[:, t, 128 * (k0 + k):128 * (k0 + k + 1)], ident))
                view = bank(b, 128 * m).rearrange("p (k i) -> p k i", k=m)
                d = dst[:, k0:k0 + m, 128 * t:128 * t + 128]
                if gain is None:
                    t_v = V.step(lambda e, d=d, view=view: e.tensor_copy(d, view), PE.mark())
                else:
                    g = gain[:, k0:k0 + m].unsqueeze(2).broadcast_to([128, m, 128])
                    t_v = V.step(lambda e, d=d, view=view, g=g: e.tensor_tensor(d, view, g, ALU.mult), PE.mark())
                give(t_v, b)
        return t_v

    def mm(o, l, r, first, last):
        PE.put(lambda e: e.matmul(o, lhsT=l, rhs=r, start=first, stop=last))

    def mm_rows(b, xt, t, w, c0, c1, nk=8, o=0):
        for k in range(nk):
            mm(bank(b, c1 - c0, o), xt[:, k, 128 * t:128 * t + 128], w[:, k, c0:c1], k == 0, k == nk - 1)

    def mm_cols(b, o, xt, w, c0, m=128, nk=8):
        for k in range(nk):
            mm(PS[0:m, b * 512 + o:b * 512 + o + 256], w[:, k, c0:c0 + m], xt[:, k, :], k == 0, k == nk - 1)

    def bc(x, n, m):
        return x.unsqueeze(2).broadcast_to([128, n, m])

    xs = room(2, 1024)
    junk = room(1024)
    qT = room(4, 256)
    kT = room(256)
    kT2 = room(256)
    va = room(2, 128)
    qkT = room(8, 260)
    vm = room(2, 512)
    om = room(2, 512)
    gr = room(2, 8)
    memT = room(8, 256)
    mark_a = top[0]
    for o in range(2):
        V.step(lambda e: e.tensor_copy(sink[:, 4 * o:4 * o + 4],
                                       sink_in.rearrange("p (x o) -> p o x", o=2)[:, o, :]), t_b)
    t_z = V.step(lambda e: e.memset(qkT[:, :, 0:4], 0.0))

    t_v = rms_scale(X[:, :, :], xs, junk, t_x)
    t_xt = flip(xs, 8, XT[:, :, :], col("mix", 0, 8), t_v)
    t_v = rms_scale(mem, xs, junk, t_mem, PE.mark(), t_xt)
    t_mt = flip(xs, 8, memT, col("mem", 0, 8), t_v, banks=(4, 5, 6, 7))

    rot = [0]

    def nextbank():
        b = rot[0] % 8
        rot[0] += 1
        take(b)
        return b

    def to(dst, b, n, o=0, fn=None):
        t = V.step(fn or (lambda e: e.tensor_copy(dst, bank(b, n, o))), PE.mark())
        give(t, b)
        return t

    def qcols(lst, w, xt):
        for dst, c0 in lst:
            b = nextbank()
            mm_cols(b, 0, xt, w, c0)
            to(dst, b, 256)

    def qrows(dst, w, xt, c0, c1):
        for t in range(2):
            b = nextbank()
            mm_rows(b, xt, t, w, c0, c1)
            to(dst(t), b, c1 - c0)

    PE.wait(t_xt)
    XTv = XT[:, :, :]
    i, w = unit()
    qcols([(qT[:, c, :], 128 * c) for c in range(4)], w, XTv)
    done(i)
    i, w = unit()
    qcols([(kT, 0)], w, XTv)
    t_k = (V.sem, V.n)
    t_k2 = dma(G, "k2", kT2[0:64, :], kT[64:128, :], t_k)
    t_k2 = dma(G, "k2", kT2[64:128, :], kT[0:64, :])
    qrows(lambda t: va[:, t, :], w, XTv, 128, 256)
    qcols([(qkT[:, c, 4:260], 256 + 128 * c) for c in range(2)], w, XTv)
    done(i)
    i, w = unit()
    qcols([(qkT[:, 2 + c, 4:260], 128 * c) for c in range(4)], w, XTv)
    done(i)
    i, w = unit()
    qcols([(qkT[:, 6 + c, 4:260], 128 * c) for c in range(2)], w, XTv)
    qrows(lambda t: vm[:, t, 0:256], w, XTv, 256, 512)
    done(i)
    i, w = unit()
    qrows(lambda t: vm[:, t, 256:512], w, XTv, 0, 256)
    qrows(lambda t: om[:, t, 0:256], w, XTv, 256, 512)
    done(i)
    i, w = unit()
    qrows(lambda t: om[:, t, 256:512], w, XTv, 0, 256)
    qrows(lambda t: gr[:, t, :], w, XTv, 256, 264)
    done(i)
    fence(t_k2, t_b)

    L1 = arena[:, 0:2048].rearrange("p (h s) -> p h s", h=8)
    L0 = room(8, 128)
    pT = room(24, 128)
    att = room(2, 512)
    for n in range(8):
        h = head_at(n)
        lo = 64 * (h % 2)
        kk = kT if (h // 4) == (h % 2) else kT2
        mm(PS[:, 256 * n:256 * n + 256], qT[lo:lo + 64, h // 2, 128:256], kk[lo:lo + 64, :], True, True)
        mm(PS[:, 2048 + 128 * n:2048 + 128 * n + 128], qT[lo:lo + 64, h // 2, 0:128], kk[lo:lo + 64, 0:128], True, True)
    t_sc = PE.mark()

    kcT = room(4, 256)
    vc = room(2, 512)
    PE.wait(t_mt)
    i, w = unit()
    for c in range(4):
        b = 6 + c % 2
        take(b)
        mm_cols(b, 0, memT, w, 128 * c)
        t = S.step(lambda e, c=c, b=b: e.activation(kcT[:, c, :], bank(b, 256), ACT.Copy), PE.mark())
        give(t, b)
    done(i)
    i, w = unit()
    for t in range(2):
        b = 6 + t
        take(b)
        mm_rows(b, memT, t, w, 0, 512)
        tk = S.step(lambda e, t=t, b=b: e.activation(vc[:, t, :], bank(b), ACT.Copy), PE.mark())
        give(tk, b)
    done(i)

    mx = tiny(16)
    dn = tiny(16)
    esk = tiny(16)
    LL = (L0, L1)
    SC = (PS[:, 2048:3072].rearrange("p (h s) -> p h s", h=8), PS[:, 0:2048].rearrange("p (h s) -> p h s", h=8))
    AB = (alibi[:, :, 128:256], alibi)
    for t in range(2):
        m8 = mx[:, 8 * t:8 * t + 8]
        tv = V.step(lambda e, t=t: e.scalar_tensor_tensor(LL[t], SC[t], 0.125, AB[t], ALU.mult, ALU.add), t_sc)
        V.step(lambda e, t=t, m8=m8: e.tensor_reduce(m8, LL[t], AX.X, ALU.max))
        V.step(lambda e, m8=m8: e.tensor_tensor(m8, m8, sink, ALU.max))
        V.step(lambda e, t=t, m8=m8: e.tensor_tensor(esk[:, 8 * t:8 * t + 8], sink, m8, ALU.subtract))
        tv = V.step(lambda e, t=t, m8=m8: e.tensor_tensor(LL[t], LL[t], bc(m8, 8, 128 * (t + 1)), ALU.subtract))
        S.step(lambda e, t=t: e.activation(LL[t], LL[t], ACT.Exp), tv)
        ts = S.step(lambda e, t=t: e.activation(esk[:, 8 * t:8 * t + 8], esk[:, 8 * t:8 * t + 8], ACT.Exp))
        d8 = dn[:, 8 * t:8 * t + 8]
        V.step(lambda e, t=t, d8=d8: e.tensor_reduce(d8, LL[t], AX.X, ALU.add), ts)
        V.step(lambda e, t=t, d8=d8: e.tensor_tensor(d8, d8, esk[:, 8 * t:8 * t + 8], ALU.add))
        V.step(lambda e, d8=d8: e.reciprocal(d8, d8))
    fence()
    n = 0
    for t in range(2):
        for h in range(8):
            for j in range(t + 1):
                PE.put(lambda e, n=n, t=t, h=h, j=j: e.transpose(PS[:, 128 * n:128 * n + 128],
                                                                 LL[t][:, h, 128 * j:128 * j + 128], ident))
                n += 1
                if n % 4 == 0:
                    b = n // 4 - 1
                    V.step(lambda e, b=b: e.tensor_copy(pT[:, 4 * b:4 * b + 4, :].rearrange("p a b -> p (a b)"), bank(b)),
                           PE.mark())
    PE.wait((V.sem, V.n))
    n = 0
    for t in range(2):
        for m in range(8):
            kv = 64 * (head_at(m) // 4)
            for j in range(t + 1):
                mm(bank(6 + t, 64, 64 * m), pT[:, n, :], va[:, j, kv:kv + 64], j == 0, j == t)
                n += 1
    for t in range(2):
        for o in range(2):
            V.step(lambda e: e.tensor_tensor(att[:, t, :].rearrange("p (x o d) -> p x o d", o=2, d=64)[:, :, o, :],
                                             bank(6 + t, 256, 256 * o).rearrange("p (h d) -> p h d", h=4),
                                             bc(dn[:, 8 * t + 4 * o:8 * t + 4 * o + 4], 4, 64), ALU.mult), PE.mark())
    t_v = rms_scale(att, att, junk, (V.sem, V.n), width=512)
    mixT = XT
    flip(att, 4, XT[:, :, :], col("att", 0, 4), t_v)
    fence()

    top[0] = 0
    cv = room(8, 256)
    top[0] = mark_a
    R = room(2, 4, 256)
    tmp = room(256)
    AM0 = room(4, 128)
    AM1 = arena[:, 2048:3072].rearrange("p (h s) -> p h s", h=4)
    sT = room(12, 128)
    hm = arena[:, 3072:4096].rearrange("p (t n) -> p t n", t=2)
    assert top[0] <= mark_a + 5120
    lf = tiny(16)
    gi = tiny(16)
    ga = tiny(16)
    for c in range(8):
        V.step(lambda e, c=c: e.tensor_scalar(cv[:, c, :], qkT[:, c, 1:257], col("convw", c), col("convb", c),
                                              ALU.mult, ALU.add))
        for j in range(1, 4):
            V.step(lambda e, c=c, j=j: e.scalar_tensor_tensor(cv[:, c, :], qkT[:, c, 1 + j:257 + j],
                                                              col("convw", 8 * j + c), cv[:, c, :], ALU.mult, ALU.add))
    t_cv = S.step(lambda e: e.activation(cv, cv, ACT.Silu), (V.sem, V.n))
    for t in range(2):
        V.step(lambda e, t=t: e.tensor_tensor(gi[:, 8 * t:8 * t + 8], gr[:, t, :], bgate, ALU.add))
    gi3 = gi.rearrange("p (t g) -> p t g", t=2)
    ipre = gi3[:, :, 0:4]
    fpre = gi3[:, :, 4:8]
    lf3 = lf[:, 0:8].rearrange("p (t g) -> p t g", t=2)
    nlf = lf[:, 8:16].rearrange("p (t g) -> p t g", t=2)
    ga3 = ga[:, 0:8].rearrange("p (t g) -> p t g", t=2)
    t_v = V.step(lambda e: e.scalar_tensor_tensor(ga3, fpre, -1.0, fpre, ALU.mult, ALU.max))
    S.step(lambda e: e.activation(ga3, ga3, ACT.Exp, scale=-1.0), t_v)
    t_s = S.step(lambda e: e.activation(ga3, ga3, ACT.Ln, bias=1.0))
    V.step(lambda e: e.tensor_scalar(lf3, fpre, 0.0, None, ALU.min))
    V.step(lambda e: e.tensor_tensor(lf3, lf3, ga3, ALU.subtract), t_s)
    V.step(lambda e: e.tensor_scalar(nlf, lf3, -1.0, None, ALU.mult))
    for j in range(2):
        for h in range(4):
            V.step(lambda e, j=j, h=h: e.tensor_scalar(tmp, eye[:, j, :], ipre[:, j, h:h + 1], None, ALU.mult))
            V.step(lambda e, j=j, h=h: e.scalar_tensor_tensor(R[:, j, h, :], upper[:, j, :], nlf[:, j, h:h + 1], tmp,
                                                              ALU.mult, ALU.add))
    PE.wait((V.sem, V.n))
    for hh in range(2):
        for j in range(2):
            mm(bank(hh), ones, R[:, j, 2 * hh:2 * hh + 2, :].rearrange("p a b -> p (a b)"), j == 0, j == 1)
    for t in range(2):
        for j in range(t + 1):
            mm(bank(2, 4, 4 * t), upper[:, j, 128 * t:128 * t + 128], lf3[:, j, :], j == 0, j == t)
    t_a = PE.mark()
    PE.wait(t_cv)
    for h in range(4):
        mm(bank(3, 128, 128 * h), cv[:, h, 0:128], cv[:, 4 + h, 0:128], True, True)
    for h in range(4):
        mm(PS[:, 2048 + 256 * h:2048 + 256 * h + 256], cv[:, h, 128:256], cv[:, 4 + h, :], True, True)
    t_q = PE.mark()
    A3 = PS[:, 0:1024].rearrange("p (h s) -> p h s", h=4)
    QK = (bank(3).rearrange("p (h s) -> p h s", h=4), PS[:, 2048:3072].rearrange("p (h s) -> p h s", h=4))
    AM = (AM0, AM1)
    M = tiny(8)
    em = tiny(8)
    for t in range(2):
        w1 = 128 * (t + 1)
        m4, e4, d4 = M[:, 4 * t:4 * t + 4], em[:, 4 * t:4 * t + 4], dn[:, 4 * t:4 * t + 4]
        V.step(lambda e, t=t, w1=w1: e.tensor_tensor(AM[t], A3[:, :, 0:w1],
                                                     causal[:, t, 0:w1].unsqueeze(1).broadcast_to([128, 4, w1]), ALU.add), t_a)
        V.step(lambda e, t=t, m4=m4: e.tensor_reduce(m4, AM[t], AX.X, ALU.max))
        V.step(lambda e, m4=m4: e.tensor_scalar(m4, m4, 0.0, None, ALU.max))
        V.step(lambda e, t=t, m4=m4, w1=w1: e.tensor_tensor(AM[t], AM[t], bc(m4, 4, w1), ALU.subtract))
        t_v = V.step(lambda e, t=t, m4=m4, e4=e4: e.tensor_tensor(e4, bank(2, 4, 4 * t), m4, ALU.add))
        S.step(lambda e, t=t: e.activation(AM[t], AM[t], ACT.Exp), t_v)
        t_s = S.step(lambda e, e4=e4: e.activation(e4, e4, ACT.Exp, scale=-1.0))
        V.step(lambda e, t=t: e.scalar_tensor_tensor(AM[t], QK[t], 128 ** -0.5, AM[t], ALU.mult, ALU.mult), t_s, t_q)
        V.step(lambda e, t=t, d4=d4: e.tensor_reduce(d4, AM[t], AX.X, ALU.add))
        V.step(lambda e, d4=d4: e.scalar_tensor_tensor(d4, d4, -1.0, d4, ALU.mult, ALU.max))
        V.step(lambda e, d4=d4, e4=e4: e.tensor_tensor(d4, d4, e4, ALU.max))
        V.step(lambda e, d4=d4: e.reciprocal(d4, d4))
    t_s = S.step(lambda e: e.activation(om, om, ACT.Tanh, scale=0.5))
    V.step(lambda e: e.tensor_scalar(om, om, 0.5, 0.5, ALU.mult, ALU.add), t_s)
    fence()
    n = 0
    for t in range(2):
        for h in range(4):
            for j in range(t + 1):
                PE.put(lambda e, n=n, t=t, h=h, j=j: e.transpose(PS[:, 128 * n:128 * n + 128],
                                                                 AM[t][:, h, 128 * j:128 * j + 128], ident))
                n += 1
                if n % 4 == 0:
                    b = n // 4 - 1
                    V.step(lambda e, b=b: e.tensor_copy(sT[:, 4 * b:4 * b + 4, :].rearrange("p a b -> p (a b)"), bank(b)),
                           PE.mark())
    PE.wait((V.sem, V.n))
    n = 0
    for t in range(2):
        for h in range(4):
            for j in range(t + 1):
                mm(bank(6 + t, 128, 128 * h), sT[:, n, :], vm[:, j, 128 * h:128 * h + 128], j == 0, j == t)
                n += 1
    sq = tiny(8)
    for t in range(2):
        hv = hm[:, t, :].rearrange("p (h d) -> p h d", h=4)
        s4 = sq[:, 4 * t:4 * t + 4]
        V.step(lambda e, t=t, hv=hv: e.tensor_tensor(hv, bank(6 + t).rearrange("p (h d) -> p h d", h=4),
                                                     bc(dn[:, 4 * t:4 * t + 4], 4, 128), ALU.mult), PE.mark())
        V.step(lambda e, t=t: e.tensor_tensor(hm[:, t, :], hm[:, t, :], om[:, t, :], ALU.mult))
        jv = junk[:, 0:512].rearrange("p (h d) -> p h d", h=4)
        V.step(lambda e, jv=jv, hv=hv: e.tensor_tensor(jv, hv, hv, ALU.mult))
        V.step(lambda e, jv=jv, s4=s4: e.tensor_reduce(s4, jv, AX.X, ALU.add))
        V.step(lambda e, s4=s4: e.tensor_scalar(s4, s4, 1.0 / 128, 1e-6, ALU.mult, ALU.add))
        rsqrt(s4, 4)
        V.step(lambda e, hv=hv, s4=s4: e.tensor_tensor(hv, hv, bc(s4, 4, 128), ALU.mult))
    t_v = flip(hm, 4, XT[:, 4:8, :], col("ml", 0, 4), (V.sem, V.n))
    PE.wait(t_v)

    def add_out(nparts=2):
        for nn in range(2):
            i, w = unit()
            for t in range(2):
                b = nextbank()
                mm_rows(b, XT[:, :, :], t, w, 0, 512)
                xv = X[:, t, 512 * nn:512 * nn + 512]
                to(None, b, 512, fn=lambda e, xv=xv, b=b: e.tensor_tensor(xv, bank(b), xv, ALU.add))
            done(i)

    add_out()
    fence()

    top[0] = 0
    xs = room(2, 1024)
    junk = room(1024)
    top[0] = mark_a
    Lc = room(4, 256)
    pcT = room(8, 128)
    qcT = room(4, 256)
    oT = room(4, 256)
    assert top[0] <= mark_a + 5120
    t_v = rms_scale(X[:, :, :], xs, junk)
    t_v = flip(xs, 8, XT[:, :, :], col("cross", 0, 8), t_v)
    PE.wait(t_v)
    i, w = unit()
    qcols([(qcT[:, c, :], 128 * c) for c in range(4)], w, XTv)
    done(i)
    for t in range(2):
        fence()
        for h in range(4):
            mm(PS[:, 256 * h:256 * h + 256], qcT[:, h, 128 * t:128 * t + 128], kcT[:, h, :], True, True)
        sc3 = PS[:, 0:1024].rearrange("p (h s) -> p h s", h=4)
        m4, d4 = mx[:, 0:4], dn[:, 0:4]
        V.step(lambda e, sc3=sc3, m4=m4: e.tensor_reduce(m4, sc3, AX.X, ALU.max), PE.mark())
        t_v = V.step(lambda e, sc3=sc3, m4=m4: e.tensor_tensor(Lc, sc3, bc(m4, 4, 256), ALU.subtract))
        t_s = S.step(lambda e: e.activation(Lc, Lc, ACT.Exp, scale=128 ** -0.5), t_v)
        V.step(lambda e, d4=d4: e.tensor_reduce(d4, Lc, AX.X, ALU.add), t_s)
        V.step(lambda e, d4=d4: e.reciprocal(d4, d4))
        t_v = V.step(lambda e, d4=d4: e.tensor_tensor(Lc, Lc, bc(d4, 4, 256), ALU.mult))
        PE.wait(t_v)
        for n in range(8):
            PE.put(lambda e, n=n: e.transpose(PS[:, 1024 + 128 * n:1152 + 128 * n],
                                              Lc[:, n // 2, 128 * (n % 2):128 * (n % 2) + 128], ident))
        t_v = V.step(lambda e: e.tensor_copy(pcT.rearrange("p a b -> p (a b)"), PS[:, 1024:2048]), PE.mark())
        PE.wait(t_v)
        for h in range(4):
            for j in range(2):
                mm(bank(4, 128, 128 * h), vc[:, j, 128 * h:128 * h + 128], pcT[:, 2 * h + j, :], j == 0, j == 1)
        V.step(lambda e, t=t: e.tensor_copy(oT[:, :, 128 * t:128 * t + 128],
                                            bank(4).rearrange("p (h s) -> p h s", h=4)), PE.mark())
    fence()
    i, w = unit()
    for nn in range(2):
        for t in range(2):
            b = nextbank()
            mm_rows(b, oT, t, w, 512 * nn, 512 * nn + 512, nk=4)
            xv = X[:, t, 512 * nn:512 * nn + 512]
            to(None, b, 512, fn=lambda e, xv=xv, b=b: e.tensor_tensor(xv, bank(b), xv, ALU.add))
    done(i)
    fence()

    top[0] = 0
    xs = room(2, 1024)
    junk = room(1024)
    wr = room(8, 36)
    rt = room(2, 36)
    gates = room(2, 32)
    wk = room(4, 2, 32)
    t_wr = dma(S, "wr", wr[:, :, 0:4], a["w_router_group"][0].rearrange("(k p) n -> p k n", p=128))
    t_wr = dma(S, "wr", wr[:, :, 4:36], a["w_router_expert"][0].rearrange("(k p) n -> p k n", p=128))
    t_v = rms_scale(X[:, :, :], xs, junk)
    t_v = flip(xs, 8, XT[:, :, :], col("ffn", 0, 8), t_v)
    PE.wait(t_v, t_wr)
    for t in range(2):
        b = nextbank()
        mm_rows(b, XTv, t, wr, 0, 36)
        to(None, b, 36, fn=lambda e, t=t, b=b: e.tensor_tensor(rt[:, t, :], bank(b, 36), brout, ALU.add))
    st = tiny(16)
    g1, e1, g2_ = st[:, 0:2], st[:, 2:4], st[:, 4:6]
    gl = rt[:, :, 0:4]
    oh, ex = wk[:, 0, :, 0:4], wk[:, 1, :, 0:4]

    def first_hit(vals, n, hit, best, where):
        V.step(lambda e: e.tensor_reduce(best, vals, AX.X, ALU.max))
        V.step(lambda e: e.tensor_tensor(hit, vals, bc(best, 2, n), ALU.is_equal))
        io = iota[:, 0:n].unsqueeze(1).broadcast_to([128, 2, n])
        V.step(lambda e: e.tensor_scalar(hit, hit, -64.0, 64.0, ALU.mult, ALU.add))
        V.step(lambda e: e.tensor_tensor(hit, hit, io, ALU.add))
        V.step(lambda e: e.tensor_reduce(where, hit, AX.X, ALU.min))
        V.step(lambda e: e.tensor_tensor(hit, bc(where, 2, n), io, ALU.is_equal))

    idx = st[:, 6:8]
    first_hit(gl, 4, oh, g1, idx)
    t_v = V.step(lambda e: e.tensor_tensor(ex, gl, bc(g1, 2, 4), ALU.subtract))
    t_s = S.step(lambda e: e.activation(ex, ex, ACT.Exp), t_v)
    V.step(lambda e: e.tensor_reduce(g2_, ex, AX.X, ALU.add), t_s)
    V.step(lambda e: e.reciprocal(g2_, g2_))
    el = wk[:, 1, :, :]
    o1, o2 = wk[:, 2, :, :], wk[:, 3, :, :]
    off = wk[:, 0, :, 4:8]
    V.step(lambda e: e.tensor_scalar(off, oh, -NEG, NEG, ALU.mult, ALU.add))
    for t in range(2):
        e3 = el[:, t, :].rearrange("p (g x) -> p g x", g=4)
        r3 = rt[:, t, 4:36].rearrange("p (g x) -> p g x", g=4)
        V.step(lambda e, t=t, e3=e3, r3=r3: e.tensor_tensor(e3, r3, bc(oh[:, t, :], 4, 8), ALU.mult))
        V.step(lambda e, t=t, e3=e3: e.tensor_tensor(e3, e3, bc(off[:, t, :], 4, 8), ALU.add))
    first_hit(el, 32, o1, g1, idx)
    V.step(lambda e: e.scalar_tensor_tensor(el, o1, NEG, el, ALU.mult, ALU.add))
    first_hit(el, 32, o2, e1, idx)
    t_v = V.step(lambda e: e.tensor_tensor(e1, e1, g1, ALU.subtract))
    t_s = S.step(lambda e: e.activation(e1, e1, ACT.Exp), t_v)
    V.step(lambda e: e.tensor_scalar(g1, e1, 1.0, None, ALU.add), t_s)
    V.step(lambda e: e.reciprocal(g1, g1))
    V.step(lambda e: e.tensor_tensor(g1, g1, g2_, ALU.mult))
    V.step(lambda e: e.tensor_tensor(e1, e1, g1, ALU.mult))
    V.step(lambda e: e.tensor_tensor(o1, o1, bc(g1, 2, 32), ALU.mult))
    V.step(lambda e: e.tensor_tensor(o2, o2, bc(e1, 2, 32), ALU.mult))
    V.step(lambda e: e.tensor_tensor(gates, o1, o2, ALU.add))
    fence()

    hs = room(2, 512)
    hr = room(4, 512)
    hT = room(2, 4, 256)
    rot4 = [0]

    def rbank():
        b = rot4[0] % 4
        rot4[0] += 1
        take(b)
        return b

    hs_read = [(V.sem, 0)] * 2
    hr_read = [(PE.sem, 0)] * 4

    def gate_up(e_, t, wg, wu):
        bg = rbank()
        mm_rows(bg, XTv, t, wg, 0, 512)
        tg = PE.mark()
        bu = rbank()
        mm_rows(bu, XTv, t, wu, 0, 512)
        tu = PE.mark()
        ts = S.step(lambda e: e.activation(hs[:, t, :], bank(bg), ACT.Silu), tg, hs_read[t])
        give(ts, bg)
        slot = 2 * (e_ % 2) + t
        tv = V.step(lambda e: e.scalar_tensor_tensor(hr[:, slot, :], hs[:, t, :], gates[:, t, e_:e_ + 1], bank(bu),
                                                     ALU.mult, ALU.mult), ts, tu, hr_read[slot])
        give(tv, bu)
        hs_read[t] = tv
        return tv

    def down(e_, tv, first, last):
        PE.wait(tv)
        for t in range(2):
            b = rbank()
            slot = 2 * (e_ % 2) + t
            for k in range(4):
                PE.put(lambda e, b=b, k=k, slot=slot: e.transpose(bank(b, 128, 128 * k),
                                                                  hr[:, slot, 128 * k:128 * k + 128], ident))
            tp = PE.mark()
            hr_read[slot] = tp
            tc = V.step(lambda e, b=b, t=t: e.tensor_copy(hT[:, e_ % 2, :, 128 * t:128 * t + 128],
                                                          bank(b).rearrange("p (k i) -> p k i", k=4)), tp)
            give(tc, b)
        i, w = unit()
        PE.wait(tc)
        for t in range(2):
            for nn in range(2):
                for k in range(4):
                    mm(bank(4 + 2 * t + nn), hT[:, e_ % 2, k, 128 * t:128 * t + 128],
                       w[:, k, 512 * nn:512 * nn + 512], first and k == 0, last and k == 3)
        done(i)

    prev = None
    for e_ in range(32):
        ig, wg = unit()
        iu, wu = unit()
        gate_up(e_, 0, wg, wu)
        if e_:
            down(e_ - 1, prev, e_ == 1, False)
        prev = gate_up(e_, 1, wg, wu)
        done(ig)
        done(iu)
    down(31, prev, False, True)
    for t in range(2):
        for nn in range(2):
            xv = X[:, t, 512 * nn:512 * nn + 512]
            b = 4 + 2 * t + nn
            to(None, b, 512, fn=lambda e, xv=xv, b=b: e.tensor_tensor(xv, bank(b), xv, ALU.add))
    t_v = rms_scale(X[:, :, :], X[:, :, :], junk, (V.sem, V.n))
    for t in range(2):
        V.step(lambda e, t=t: e.tensor_tensor(X[:, t, :], X[:, t, :], gfin[:, 0, :], ALU.mult))
    fence()

    def swiglu(gain_row):
        top[0] = 0
        xs = room(2, 1024)
        junk = room(1024)
        hs = room(4, 256)
        hr = room(4, 256)
        hT = room(22, 256)
        t_v = rms_scale(X[:, :, :], xs, junk)
        t_v = flip(xs, 8, XT[:, :, :], gc[:, gain_row:gain_row + 8], t_v)
        PE.wait(t_v)
        hsr = [(V.sem, 0)] * 4
        hrr = [(PE.sem, 0)] * 4
        ready = {}

        def turn(c):
            for t in range(2):
                b = rbank()
                slot = 2 * (c % 2) + t
                PE.wait(ready[(c, t)])
                for k in range(2):
                    PE.put(lambda e, b=b, k=k, slot=slot: e.transpose(bank(b, 128, 128 * k),
                                                                      hr[:, slot, 128 * k:128 * k + 128], ident))
                tp = PE.mark()
                hrr[slot] = tp
                tc = V.step(lambda e, b=b, t=t: e.tensor_copy(hT[:, 2 * c:2 * c + 2, 128 * t:128 * t + 128],
                                                              bank(b, 256).rearrange("p (k i) -> p k i", k=2)), tp)
                give(tc, b)
            return tc

        for c in range(11):
            i, w = unit()
            for t in range(2):
                b = rbank()
                mm_rows(b, XTv, t, w, 0, 512)
                tp = PE.mark()
                slot = 2 * (c % 2) + t
                ts = S.step(lambda e, b=b, slot=slot: e.activation(hs[:, slot, :], bank(b, 256), ACT.Silu),
                            tp, hsr[slot])
                tv = V.step(lambda e, b=b, slot=slot: e.tensor_tensor(hr[:, slot, :], hs[:, slot, :],
                                                                      bank(b, 256, 256), ALU.mult),
                            ts, tp, hrr[slot])
                give(tv, b)
                hsr[slot] = tv
                ready[(c, t)] = tv
            done(i)
            if c:
                turn(c - 1)
        tc = turn(10)
        take(4, 5, 6, 7)
        PE.wait(tc)
        for c in range(6):
            i, w = unit()
            nk = min(4, 22 - 4 * c)
            for t in range(2):
                for nn in range(2):
                    for k in range(nk):
                        kk = 4 * c + k
                        mm(bank(4 + 2 * t + nn), hT[:, kk, 128 * t:128 * t + 128],
                           w[:, k, 512 * nn:512 * nn + 512], kk == 0, kk == 21)
            done(i)
        for t in range(2):
            for nn in range(2):
                xv = X[:, t, 512 * nn:512 * nn + 512]
                b = 4 + 2 * t + nn
                to(None, b, 512, fn=lambda e, xv=xv, b=b: e.scalar_tensor_tensor(xv, bank(b), 0.5, xv, ALU.mult, ALU.add))
        fence()

    g2 = GAIN["g2"]
    PE.wait(t_b)
    take(7)
    PE.put(lambda e: e.matmul(PS[0:8, 3584:4096], lhsT=rtab[0:32, :], rhs=hot[:, :], start=True, stop=True))
    frow = sb("frow", [8, 512])
    t_f = S.step(lambda e: e.activation(frow[:, :], PS[0:8, 3584:4096], ACT.Copy), PE.mark())
    give(t_f, 7)
    t_toep = dma(G, "toep", toep, frow[:, :].unsqueeze(1).broadcast_to([8, 128, 512]), t_f)

    swiglu(g2)

    top[0] = 0
    qT = room(8, 256)
    kT = room(8, 256)
    va = room(2, 1024)
    qi = room(4, 256)
    ki = room(256)
    BT = room(2, 8, 256)
    la = top[0]
    xs = room(2, 1024)
    junk = room(1024)
    top[0] = la
    sc = room(256)
    w0 = room(256)
    w1_ = room(256)
    La = room(8, 256)
    pa = room(16, 128)
    oT = XT
    wi = tiny(16)
    for t in range(2):
        src = bass.AP(tensor=toep.tensor, offset=255 - 128 * t, ap=[[511, 128], [65536, 8], [1, 256]])
        t_bt = dma(G, "bt", BT[:, t, :, :], src, t_toep)
    t_v = rms_scale(X[:, :, :], xs, junk)
    t_v = flip(xs, 8, XT[:, :, :], gc[:, g2 + 8:g2 + 16], t_v)
    PE.wait(t_v)
    for half, dst in ((0, qT), (0, kT)):
        for u in range(2):
            i, w = unit()
            qcols([(dst[:, 4 * u + c, :], 128 * c) for c in range(4)], w, XTv)
            done(i)
    for u in range(2):
        i, w = unit()
        qrows(lambda t, u=u: va[:, t, 512 * u:512 * u + 512], w, XTv, 0, 512)
        done(i)
    i, w = unit()
    qcols([(qi[:, c, :], 128 * c) for c in range(4)], w, XTv)
    done(i)
    i, w = unit()
    b = nextbank()
    mm_cols(b, 0, XTv, w, 0, m=64)
    t_ki = to(None, b, 256, fn=lambda e, b=b: e.tensor_copy(ki[0:64, :], PS[0:64, b * 512:b * 512 + 256]))
    t_ki = dma(G, "ki", ki[64:128, :], ki[0:64, :], t_ki)
    for t in range(2):
        b = nextbank()
        mm_rows(b, XTv, t, w, 64, 72)
        to(None, b, 8, fn=lambda e, b=b, t=t: e.tensor_scalar(wi[:, 8 * t:8 * t + 8], bank(b, 8), 8 ** -0.5 / 8,
                                                              None, ALU.mult))
    done(i)
    fence(t_ki, t_bt)
    best = tiny(8)
    for t in range(2):
        for n in range(8):
            h = head_at(n)
            lo = 64 * (h % 2)
            mm(PS[:, 256 * n:256 * n + 256], qi[lo:lo + 64, h // 2, 128 * t:128 * t + 128], ki[lo:lo + 64, :], True, True)
        t_i = PE.mark()
        for h in range(8):
            mm(PS[:, 2048 + 256 * h:2304 + 256 * h], qT[:, h, 128 * t:128 * t + 128], kT[:, h, :], True, True)
        t_q = PE.mark()
        for n in range(8):
            wcol = wi[:, 8 * t + head_at(n):8 * t + head_at(n) + 1]
            V.step(lambda e: e.tensor_scalar(w0, PS[:, 256 * n:256 * n + 256], 0.0, wcol, ALU.max, ALU.mult), t_i)
            if n == 0:
                V.step(lambda e, t=t: e.tensor_copy(sc, w0))
            else:
                V.step(lambda e: e.tensor_tensor(sc, sc, w0, ALU.add))
        V.step(lambda e, t=t: e.tensor_tensor(sc, sc, causal[:, t, :], ALU.add))
        cur = sc
        for r in range(8):
            nxt = w0 if r % 2 == 0 else w1_
            V.step(lambda e, cur=cur: e.max(best, cur))
            V.step(lambda e, cur=cur, nxt=nxt: e.match_replace(nxt, best, cur, GONE))
            cur = nxt
        V.step(lambda e, cur=cur: e.tensor_scalar(cur, cur, -2.0e38, None, ALU.is_gt))
        V.step(lambda e, cur=cur, t=t: e.scalar_tensor_tensor(cur, cur, NEG, causal[:, t, :], ALU.mult, ALU.add))
        V.step(lambda e, t=t: e.scalar_tensor_tensor(La, PS[:, 2048:4096].rearrange("p (h s) -> p h s", h=8),
                                                     128 ** -0.5, BT[:, t, :, :], ALU.mult, ALU.add), t_q)
        V.step(lambda e, cur=cur: e.tensor_tensor(La, La, cur.unsqueeze(1).broadcast_to([128, 8, 256]), ALU.add))
        m8, d8 = mx[:, 0:8], dn[:, 0:8]
        V.step(lambda e, m8=m8: e.tensor_reduce(m8, La, AX.X, ALU.max))
        t_v = V.step(lambda e, m8=m8: e.tensor_tensor(La, La, bc(m8, 8, 256), ALU.subtract))
        t_s = S.step(lambda e: e.activation(La, La, ACT.Exp), t_v)
        V.step(lambda e, d8=d8: e.tensor_reduce(d8, La, AX.X, ALU.add), t_s)
        V.step(lambda e, d8=d8: e.reciprocal(d8, d8))
        t_v = V.step(lambda e, d8=d8: e.tensor_tensor(La, La, bc(d8, 8, 256), ALU.mult))
        PE.wait(t_v)
        for n in range(16):
            PE.put(lambda e, n=n: e.transpose(PS[:, 128 * n:128 * n + 128],
                                              La[:, n // 2, 128 * (n % 2):128 * (n % 2) + 128], ident))
        t_v = V.step(lambda e: e.tensor_copy(pa.rearrange("p a b -> p (a b)"), PS[:, 0:2048]), PE.mark())
        PE.wait(t_v)
        for h in range(8):
            for j in range(2):
                mm(PS[:, 2048 + 128 * h:2176 + 128 * h], va[:, j, 128 * h:128 * h + 128], pa[:, 2 * h + j, :],
                   j == 0, j == 1)
        V.step(lambda e, t=t: e.tensor_copy(XT[:, :, 128 * t:128 * t + 128],
                                            PS[:, 2048:3072].rearrange("p (h s) -> p h s", h=8)), PE.mark())
        fence()
    add_out()
    fence()

    swiglu(g2 + 16)
    swiglu(g2 + 24)

    top[0] = 0
    uu = room(2, 3072)
    vv = room(2, 3072)
    bb = room(2, 1024)
    wsp = room(8, 128)
    wst = room(8, 128)
    xs = vv[:, 0, 0:2048].rearrange("p (t n) -> p t n", t=2)
    junk = vv[:, 1, 0:1024]
    zb = room(2, 512)
    bsp = tiny(8)
    t_w = dma(G, "wsp", wsp, a["b_w_sp_2"][0].rearrange("g t s -> t g s"))
    t_bsp = dma(G, "bsp", rows[0:8, :], a["b_b_sp_2"][0])
    t_v = rms_scale(X[:, :, :], xs, junk)
    t_v = flip(xs, 8, XT[:, :, :], gc[:, g2 + 32:g2 + 40], t_v)
    for q in range(2):
        b = nextbank()
        PE.wait(t_w)
        for k in range(4):
            PE.put(lambda e, b=b, k=k, q=q: e.transpose(bank(b, 128, 128 * k), wsp[:, 4 * q + k, :], ident))
        to(None, b, 512, fn=lambda e, b=b, q=q: e.tensor_tensor(
            wst[:, 4 * q:4 * q + 4, :], bank(b).rearrange("p (k i) -> p k i", k=4),
            upper[:, 0, 0:128].unsqueeze(1).broadcast_to([128, 4, 128]), ALU.mult))
    b = nextbank()
    PE.wait(t_bsp)
    PE.put(lambda e, b=b: e.transpose(bank(b, 8), rows[0:8, :], ident[0:8, 0:8]))
    to(bsp, b, 8)
    fence()
    bread = [(V.sem, 0)] * 2

    def bias_piece(n, *parts):
        s = n % 2
        for k, src in enumerate(parts):
            t_p = dma(G, f"bp{s}", bb[:, s, 512 * k:512 * k + 512], src.broadcast_to([128, 512]), bread[s])
        return s, t_p

    zread = [(S.sem, 0)] * 2
    pieces = [(vv, 3072, c) for c in range(6)] + [(uu, 0, c) for c in range(6)]
    for n, (dst, base, c) in enumerate(pieces):
        s, t_p = bias_piece(n, a["b_b_in_2"][:, base + 512 * c:base + 512 * c + 512])
        i, w = unit()
        for t in range(2):
            b = rbank()
            mm_rows(b, XTv, t, w, 0, 512)
            tv = V.step(lambda e, b=b, t=t, s=s: e.tensor_tensor(zb[:, t, :], bank(b), bb[:, s, 0:512], ALU.add),
                        PE.mark(), t_p, zread[t])
            give(tv, b)
            zread[t] = S.step(lambda e, t=t, c=c, dst=dst: e.activation(dst[:, t, 512 * c:512 * c + 512], zb[:, t, :],
                                                                        ACT.Gelu_apprx_tanh), tv)
        bread[s] = tv
        done(i)
    bst = tiny(2 * 36)
    mv = tiny(4)
    for t in range(2):
        for c in range(6):
            V.step(lambda e, t=t, c=c: e.bn_stats(bst[:, 36 * t + 6 * c:36 * t + 6 * c + 6], vv[:, t, 512 * c:512 * c + 512]),
                   (S.sem, S.n))
        V.step(lambda e, t=t: e.bn_aggr(mv[:, 2 * t:2 * t + 2], bst[:, 36 * t:36 * t + 36]))
        V.step(lambda e, t=t: e.tensor_scalar(mv[:, 2 * t + 1:2 * t + 2], mv[:, 2 * t + 1:2 * t + 2], 1e-6, None, ALU.add))
        rsqrt(mv[:, 2 * t + 1:2 * t + 2], 1)
    for c in range(6):
        s, t_p = bias_piece(c, a["b_ln_g_2"][:, 512 * c:512 * c + 512], a["b_ln_b_2"][:, 512 * c:512 * c + 512])
        for t in range(2):
            vp = vv[:, t, 512 * c:512 * c + 512]
            V.step(lambda e, t=t, vp=vp: e.tensor_scalar(vp, vp, mv[:, 2 * t:2 * t + 1], mv[:, 2 * t + 1:2 * t + 2],
                                                         ALU.subtract, ALU.mult))
            V.step(lambda e, vp=vp, s=s: e.tensor_tensor(vp, vp, bb[:, s, 0:512], ALU.mult), t_p)
            bread[s] = V.step(lambda e, vp=vp, s=s: e.tensor_tensor(vp, vp, bb[:, s, 512:1024], ALU.add))
    PE.wait((V.sem, V.n))
    for t in range(2):
        for g in range(8):
            b = rbank()
            mm(bank(b, 384), wst[:, g, :], vv[:, t, 384 * g:384 * g + 384], True, True)
            up = uu[:, t, 384 * g:384 * g + 384]
            to(None, b, 384, fn=lambda e, b=b, g=g, up=up: e.scalar_tensor_tensor(
                up, bank(b, 384), bsp[:, g:g + 1], up, ALU.add, ALU.mult))
    fence()
    yT = arena[:, 6144:12288].rearrange("p (k s) -> p k s", k=24)
    t_v = flip(uu, 24, yT, None)
    take(4, 5, 6, 7)
    PE.wait(t_v)
    for c in range(6):
        i, w = unit()
        for t in range(2):
            for nn in range(2):
                for k in range(4):
                    kk = 4 * c + k
                    mm(bank(4 + 2 * t + nn), yT[:, kk, 128 * t:128 * t + 128],
                       w[:, k, 512 * nn:512 * nn + 512], kk == 0, kk == 23)
        done(i)
    for t in range(2):
        for nn in range(2):
            xv = X[:, t, 512 * nn:512 * nn + 512]
            b = 4 + 2 * t + nn
            to(None, b, 512, fn=lambda e, xv=xv, b=b: e.tensor_tensor(xv, bank(b), xv, ALU.add))
    fence()

    swiglu(g2 + 40)

    top[0] = 0
    xs = room(2, 1024)
    junk = room(1024)
    rms_scale(X[:, :, :], xs, junk)
    for t in range(2):
        t_v = V.step(lambda e, t=t: e.tensor_tensor(xs[:, t, :], xs[:, t, :], gfin[:, 1, :], ALU.mult))
    t_o = dma(SP, "o", out[0].rearrange("(t p) n -> p t n", p=128), xs, t_v)
    SP.wait(t_o)
    assert at["next"] == len(units), (at, len(units))


_NAMES = ["x", "mem", "norm_mix", "w_in", "b_gates", "conv_w", "conv_b", "att_sinks", "norm_att_out", "norm_ml_out",
          "w_out", "norm_cross", "norm_mem", "w_cq", "w_ckv", "w_co", "norm_ffn", "w_router_group", "b_router_group",
          "w_router_expert", "b_router_expert", "w_e_gate", "w_e_up", "w_e_down", "norm_final", "norm_g_2",
          "final_g_2", "ffn_w_in_2", "ffn_w_out_2", "rel_table_2", "a_w_in_2", "a_w_out_2", "b_w_in_2", "b_b_in_2",
          "b_ln_g_2", "b_ln_b_2", "b_w_sp_2", "b_b_sp_2", "b_w_out_2"]


def kernel(**inputs):
    import concourse.bacc as _bacc
    from concourse.bass_utils import run_bass_kernel_spmd as _run

    nc = _bacc.Bacc("TRN2", target_bir_lowering=False, num_devices=1)
    cst, hot = shape_constants()
    arrays, a = {}, {}
    for name in _NAMES + ["cst", "hot"]:
        v = np.ascontiguousarray({"cst": cst, "hot": hot}[name] if name in ("cst", "hot") else inputs[name])
        arrays["in_" + name] = v
        a[name] = nc.dram_tensor("in_" + name, v.shape, mybir.dt.from_np(v.dtype), kind="ExternalInput").ap()
    out = nc.dram_tensor("out_0", (1, 256, 1024), F32, kind="ExternalOutput").ap()
    build(nc, a, out)
    r = _run(nc, [arrays], core_ids=[0])
    return r.results[0]["out_0"]
```

```python
import numpy as np
import concourse.bass as bass
from concourse import mybir
from contextlib import ExitStack

F32 = mybir.dt.float32
F32R = mybir.dt.float32r
I32 = mybir.dt.int32
ALU = mybir.AluOpType
ACT = mybir.ActivationFunctionType
AX = mybir.AxisListType

NEG = -1.0e30
NONE = 100000
GONE = -3.0e38
RING = 5
SPLIT = 3
PART = 2048
CONST_AT = {"ident": (0, 128), "upper": (128, 512), "eye": (640, 512), "causal": (1152, 512),
            "iota": (1664, 32), "ones": (1696, 128), "slot": (1824, 4), "alibi": (1828, 2048)}
CONST_W = 3876
KEPT_W = 1828


def head_at(n):
    return 2 * (n % 4) + n // 4


def shape_constants():
    p = np.arange(128)[:, None]
    s = np.arange(256)[None, :]
    c = np.zeros((128, CONST_W), np.float32)

    def put(name, a):
        o, n = CONST_AT[name]
        c[:, o:o + n] = a.reshape(128, n)

    put("ident", np.eye(128))
    put("upper", np.stack([(p + 128 * j) <= s for j in range(2)], 1).astype(np.float32))
    put("eye", np.stack([(p + 128 * j) == s for j in range(2)], 1).astype(np.float32))
    dist = p + 128 - s
    ok = (dist >= 0) & (dist < 128)
    put("alibi", np.stack([np.where(ok, -(2.0 ** -(head_at(n) + 1)) * dist, NEG) for n in range(8)], 1))
    put("causal", np.stack([np.where(s <= p + 128 * t, 0.0, NEG) for t in range(2)], 1))
    put("iota", np.broadcast_to(np.arange(32), (128, 32)))
    put("slot", 128 * np.arange(4)[None, :] + p)
    put("ones", np.ones((128, 128)))
    hot = np.zeros((32, 512), np.float32)
    for j in range(256):
        d = 255 - j
        b = d if d < 16 else min(31, 16 + int(np.log(d / 16.0) / np.log(128.0) * 16))
        hot[b, j] = 1.0
    return c, hot


class Lane:

    def __init__(self, eng, sem, live=True):
        self.eng, self.sem, self.n, self.last, self.seen, self.live = eng, sem, 0, None, {}, live

    def wait(self, *tokens):
        for sem, value in tokens:
            if value > self.seen.get(sem.name, 0):
                self.seen[sem.name] = value
                if self.live:
                    self.eng.wait_ge(sem, value)

    def mark(self):
        if self.last is not None:
            if self.live:
                self.last.then_inc(self.sem, 1)
            self.last = None
            self.n += 1
        return (self.sem, self.n)

    def put(self, fn):
        self.last = fn(self.eng) if self.live else self

    def step(self, fn, *tokens):
        self.wait((self.sem, self.n), *tokens)
        if self.live:
            fn(self.eng).then_inc(self.sem, 1)
        self.n += 1
        return (self.sem, self.n)


def build(nc, a, out):
    with ExitStack() as ctx:
        assemble(nc, a, out, ctx)


def assemble(nc, a, out, ctx):
    def sem(name):
        return ctx.enter_context(nc.semaphore(name))

    def sb(name, shape):
        return ctx.enter_context(nc.sbuf_tensor(name, shape, F32))

    PE, V, S = Lane(nc.tensor, sem("s_pe")), Lane(nc.vector, sem("s_v")), Lane(nc.scalar, sem("s_s"))
    G, SP = Lane(nc.gpsimd, sem("s_g")), Lane(nc.sync, sem("s_sp"))
    dma_count = {}

    def dma(lane, name, dst, src, *tokens):
        if name not in dma_count:
            dma_count[name] = [sem("d_" + name), 0]
        lane.wait(*tokens)
        d = dma_count[name]
        d[1] += 16
        if lane.live:
            lane.eng.dma_start(dst, src).then_inc(d[0], 16)
        return (d[0], d[1])

    def dma_of(lane, name, fn, *tokens):
        if name not in dma_count:
            dma_count[name] = [sem("d_" + name), 0]
        lane.wait(*tokens)
        d = dma_count[name]
        d[1] += 16
        if lane.live:
            fn(lane.eng).then_inc(d[0], 16)
        return (d[0], d[1])

    def fence(*tokens):
        marks = [(V.sem, V.n), (S.sem, S.n), (G.sem, G.n), PE.mark()]
        for lane in (PE, V, S, G):
            lane.wait(*marks, *tokens)
        return marks

    cst = sb("cst", [128, KEPT_W])
    gc = sb("gc", [128, 128])
    rows = sb("rows", [128, 128])
    X = sb("X", [128, 2, 1024])
    xtmp = sb("xtmp", [128, 2, 512])
    small = sb("small", [128, 512])
    ring = sb("ring", [128, RING, PART])
    XTh = ctx.enter_context(nc.sbuf_tensor("XTh", [128, 8, 256], F32R))
    XTl = ctx.enter_context(nc.sbuf_tensor("XTl", [128, 8, 256], F32R))
    wh = ctx.enter_context(nc.sbuf_tensor("wh", [128, SPLIT, PART], F32R))
    wl = ctx.enter_context(nc.sbuf_tensor("wl", [128, SPLIT, PART], F32R))
    PS = ctx.enter_context(nc.psum_tensor("PS", [128, 4096], F32))
    lists = nc.dram_tensor("lists", (8192, 1), I32, kind="Internal").ap()
    xn_d = nc.dram_tensor("xn_d", (256, 1024), F32, kind="Internal").ap()
    y_d = nc.dram_tensor("y_d", (512, 1024), F32, kind="Internal").ap()
    toep = nc.dram_tensor("toep", (8, 128, 512), F32, kind="Internal").ap()

    def C(name):
        o, n = CONST_AT[name]
        return cst[:, o:o + n]

    ident = C("ident")
    upper = C("upper").rearrange("p (j s) -> p j s", j=2)
    eye = C("eye").rearrange("p (j s) -> p j s", j=2)
    causal = C("causal").rearrange("p (t s) -> p t s", t=2)
    iota = C("iota")
    ones = C("ones")

    space = {"stack": None, "count": 0}

    def phase(words):
        if space["stack"] is not None:
            space["stack"].close()
        space["stack"] = ctx.enter_context(ExitStack())
        space["count"] += 1
        space["arena"] = space["stack"].enter_context(nc.sbuf_tensor(f"arena{space['count']}", [128, words], F32))
        space["words"] = words
        space["at"] = 0

    def pieces_of(name, *dims):
        return [space["stack"].enter_context(nc.sbuf_tensor(f"{name}{x}{space['count']}", [128, *dims], F32R))
                for x in "hl"]

    def shaped(v, dims):
        if len(dims) == 2:
            v = v.rearrange("p (a b) -> p a b", a=dims[0])
        if len(dims) == 3:
            v = v.rearrange("p (a b c) -> p a b c", a=dims[0], b=dims[1])
        return v

    def room_at(o, *dims):
        n = 1
        for d in dims:
            n *= d
        assert o + n <= space["words"], (o + n, space["words"])
        return shaped(space["arena"][:, o:o + n], dims)

    def room(*dims):
        v = room_at(space["at"], *dims)
        n = 1
        for d in dims:
            n *= d
        space["at"] += n
        return v

    used = [0]

    def tiny(n):
        o = used[0]
        used[0] += n
        assert used[0] <= 512, used[0]
        return small[:, o:o + n]

    rel = [(PE.sem, 0)] * 8

    def bank(b, n=512, o=0):
        return PS[:, b * 512 + o:b * 512 + o + n]

    def take(*banks):
        for b in banks:
            PE.wait(rel[b])

    def give(token, *banks):
        for b in banks:
            rel[b] = token

    parts = []

    def cols(w, c0, c1):
        r = w.rearrange("(k p) n -> p k n", p=128)
        for k in (0, 4):
            parts.append((4, c1 - c0, [(0, c1 - c0, r[:, k:k + 4, c0:c1])]))

    def pair(w, c0, u0, n):
        r = w.rearrange("(k p) n -> p k n", p=128)
        for k in (0, 4):
            parts.append((4, 2 * n, [(0, n, r[:, k:k + 4, c0:c0 + n]), (n, 2 * n, r[:, k:k + 4, u0:u0 + n])]))

    def deep(w, r0, nk):
        for k in range(0, nk, 2):
            src = w[r0 + 128 * k:r0 + 128 * k + 256, :].rearrange("(k p) n -> p k n", p=128)
            parts.append((2, 1024, [(0, 1024, src)]))

    w_in = a["w_in"][0]
    cols(a["w_ckv"][0], 0, 512)
    cols(a["w_ckv"][0], 512, 1024)
    for c in range(0, 2824, 512):
        cols(w_in, c, min(c + 512, 2824))
    cols(a["w_out"][0], 0, 512)
    cols(a["w_out"][0], 512, 1024)
    cols(a["w_cq"][0], 0, 512)
    deep(a["w_co"][0], 0, 4)
    for e in range(32):
        cols(a["w_e_gate"][0, e], 0, 512)
        if e:
            deep(a["w_e_down"][0, e - 1], 0, 4)
        cols(a["w_e_up"][0, e], 0, 512)
    deep(a["w_e_down"][0, 31], 0, 4)

    def ffn_units(i, j):
        for c in range(11):
            pair(a["ffn_w_in_2"][i, j], 256 * c, 2816 + 256 * c, 256)
        for c in range(6):
            deep(a["ffn_w_out_2"][i, j], 512 * c, min(4, 22 - 4 * c))

    ffn_units(0, 0)
    for c in range(0, 3656, 512):
        cols(a["a_w_in_2"][0], c, min(c + 512, 3656))
    cols(a["a_w_out_2"][0], 0, 512)
    cols(a["a_w_out_2"][0], 512, 1024)
    ffn_units(0, 1)
    ffn_units(1, 0)
    for c in range(6):
        cols(a["b_w_in_2"][0], 3072 + 512 * c, 3584 + 512 * c)
    for c in range(6):
        cols(a["b_w_in_2"][0], 512 * c, 512 * c + 512)
    for c in range(6):
        deep(a["b_w_out_2"][0], 512 * c, 4)
    ffn_units(1, 1)

    loaded, ready, at = {}, {}, {"load": 0, "split": 0, "use": 0}

    def load_part(*tokens):
        i = at["load"]
        if i < len(parts):
            at["load"] += 1
            nk, w, srcs = parts[i]
            for c0, c1, src in srcs:
                dst = ring[:, i % RING, 0:nk * w].rearrange("p (k n) -> p k n", n=w)[:, :, c0:c1]
                loaded[i] = dma(SP, f"w{i % RING}", dst, src, *tokens)

    def split_part(*tokens):
        i = at["split"]
        if i < len(parts):
            at["split"] += 1
            n = parts[i][0] * parts[i][1]
            raw, h, l = ring[:, i % RING, 0:n], wh[:, i % SPLIT, 0:n], wl[:, i % SPLIT, 0:n]
            t_s = S.step(lambda e: e.activation(h, raw, ACT.Copy), loaded[i], *tokens)
            ready[i] = V.step(lambda e: e.tensor_tensor(l, raw, h.bitcast(F32), ALU.subtract), t_s)
            load_part(ready[i])

    def part():
        i = at["use"]
        at["use"] += 1
        nk, w, _ = parts[i]
        PE.wait(ready[i])
        return [x[:, i % SPLIT, 0:nk * w].rearrange("p (k n) -> p k n", n=w) for x in (wh, wl)]

    def done():
        split_part(PE.mark())

    phase(20300)
    mem = room(2, 1024)
    alibi_flat = room(2048)
    alibi = alibi_flat.rearrange("p (h s) -> p h s", h=8)
    t_mem = dma(SP, "m", mem, a["mem"][0].rearrange("(t p) n -> p t n", p=128))
    t_c = dma(SP, "c", cst[:, :], a["cst"][:, 0:KEPT_W])
    t_x = dma(SP, "x", X[:, :, :], a["x"][0].rearrange("(t p) n -> p t n", p=128))

    GAIN = {}
    row_at = 0
    t_r = None
    for name, src, n in (("mix", a["norm_mix"][0], 8), ("att", a["norm_att_out"][0], 4),
                         ("ml", a["norm_ml_out"][0], 4), ("cross", a["norm_cross"][0], 8),
                         ("mem", a["norm_mem"][0], 8), ("ffn", a["norm_ffn"][0], 8),
                         ("convb", a["conv_b"][0], 8)):
        t_r = dma(S, "r", rows[row_at:row_at + n, :], src.rearrange("(k p) -> k p", p=128))
        GAIN[name] = row_at
        row_at += n
    t_r = dma(S, "r", rows[row_at:row_at + 32, :], a["conv_w"][0].rearrange("w (k p) -> (w k) p", p=128))
    GAIN["convw"] = row_at
    row_at += 32
    t_r = dma(S, "r", rows[row_at:row_at + 48, :], a["norm_g_2"].rearrange("i j (k p) -> (i j k) p", p=128))
    GAIN["g2"] = row_at
    row_at += 48
    assert row_at == 128
    for _ in range(RING):
        load_part()
    for _ in range(SPLIT):
        split_part()

    sink = tiny(8)
    bgate = tiny(8)
    brout = tiny(36)
    sink_in = tiny(8)
    t_b = dma(S, "b", sink_in, a["att_sinks"].broadcast_to([128, 8]))
    t_b = dma(S, "b", bgate, a["b_gates"].broadcast_to([128, 8]))
    t_b = dma(S, "b", brout[:, 0:4], a["b_router_group"].broadcast_to([128, 4]))
    t_b = dma(S, "b", brout[:, 4:36], a["b_router_expert"].broadcast_to([128, 32]))
    t_b = dma(S, "b", alibi_flat, a["cst"][:, KEPT_W:CONST_W])
    hot = room_at(15000, 512)[0:32, :]
    frow = room_at(16000, 512)[0:8, :]
    rtab = tiny(8)
    t_b = dma(S, "b", hot, a["hot"])
    t_b = dma(S, "b", rtab[0:32, :], a["rel_table_2"])

    PE.wait(t_c, t_r)
    PE.put(lambda e: e.transpose(bank(7, 128), rows[:, :], ident))
    t_gc = V.step(lambda e: e.tensor_copy(gc[:, :], bank(7, 128)), PE.mark())
    give(t_gc, 7)

    def col(name, k=0, n=1):
        o = GAIN[name] + k
        return gc[:, o:o + n]

    mhalf = tiny(8)
    V.step(lambda e: e.memset(mhalf, -0.5))

    def rsqrt(x, n):
        t_g = G.step(lambda e: e.tensor_tensor(x, x, mhalf[:, 0:n], ALU.pow), (V.sem, V.n))
        V.wait(t_g)

    ss = tiny(2)
    rstd = tiny(2)

    def rms_scale(src, dst, junk, *tokens, width=1024):
        for t in range(2):
            t_ss = S.step(lambda e, t=t: e.activation(junk[:, 0:width], src[:, t, :], ACT.Square,
                                                      accum_out=ss[:, t:t + 1]), *tokens)
        V.step(lambda e: e.tensor_scalar(rstd, ss, 1.0 / width, 1e-6, ALU.mult, ALU.add), t_ss, *tokens)
        rsqrt(rstd, 2)
        for t in range(2):
            t_v = V.step(lambda e, t=t: e.tensor_scalar(dst[:, t, :], src[:, t, :], rstd[:, t:t + 1], None, ALU.mult))
        return t_v

    def cut(dst, src, n):
        h, l = dst
        t_s = S.step(lambda e: e.activation(h, src, ACT.Copy), n)
        return V.step(lambda e: e.tensor_tensor(l, src, h.bitcast(F32), ALU.subtract), t_s)

    def flip(src, nk, dst, gain, *tokens, banks=(0, 1, 2, 3)):
        PE.wait(*tokens)
        n = 0
        t_v = None
        for t in range(2):
            for k0 in range(0, nk, 4):
                b = banks[n % len(banks)]
                m = min(4, nk - k0)
                take(b)
                for k in range(m):
                    PE.put(lambda e: e.transpose(
                        bank(b, 128, 128 * k), src[:, t, 128 * (k0 + k):128 * (k0 + k + 1)], ident))
                view = bank(b, 128 * m).rearrange("p (k i) -> p k i", k=m)
                d = [x[:, k0:k0 + m, 128 * t:128 * t + 128] for x in dst]
                if gain is None:
                    t_v = cut(d, view, PE.mark())
                    give(t_v, b)
                else:
                    g = gain[:, k0:k0 + m].unsqueeze(2).broadcast_to([128, m, 128])
                    tmp = xtmp[:, n % 2, 0:128 * m].rearrange("p (k i) -> p k i", k=m)
                    t_m = V.step(lambda e: e.tensor_tensor(tmp, view, g, ALU.mult), PE.mark())
                    give(t_m, b)
                    t_v = cut(d, tmp, t_m)
                n += 1
        return t_v

    def mm(o, l, r, first, last):
        PE.put(lambda e: e.matmul(o, lhsT=l, rhs=r, start=first, stop=last))

    def mm3(o, lh, ll, rh, rl, first, last):
        mm(o, lh, rh, first, False)
        mm(o, lh, rl, False, False)
        mm(o, ll, rh, False, last)

    def use_rows(o, xt, kx, t, w, kw, c0, c1, first, last):
        xs_ = [x[:, kx, 128 * t:128 * t + 128] for x in xt]
        ws_ = [x[:, kw, c0:c1] for x in w]
        mm3(o, xs_[0], xs_[1], ws_[0], ws_[1], first, last)

    def rows_job(t, c0, c1, dst=None, fn=None):
        return ("rows", t, c0, c1, dst, fn)

    def cols_job(c0, dst, m=128, keep=128):
        return ("cols", c0, m, keep, dst, None)

    def project(xt, jobs, nparts=2):
        banks = [nextbank() for _ in jobs]
        for p in range(nparts):
            w = part()
            for b, job in zip(banks, jobs):
                for k in range(4):
                    kk, last = 4 * p + k, 4 * nparts - 1
                    if job[0] == "rows":
                        _, t, c0, c1, _, _ = job
                        use_rows(bank(b, c1 - c0), xt, kk, t, w, k, c0, c1, kk == 0, kk == last)
                    else:
                        _, c0, m, _, _, _ = job
                        o = PS[0:m, b * 512:b * 512 + 256]
                        mm3(o, w[0][:, k, c0:c0 + m], w[1][:, k, c0:c0 + m], xt[0][:, kk, :], xt[1][:, kk, :],
                            kk == 0, kk == last)
            done()
        for b, job in zip(banks, jobs):
            if job[0] == "rows":
                n, dst, fn = job[3] - job[2], job[4], job[5]
                give(V.step((lambda e: fn(e, b)) if fn else (lambda e: e.tensor_copy(dst, bank(b, n))), PE.mark()), b)
            else:
                q, dst = job[3], job[4]
                give(V.step(lambda e: e.tensor_copy(dst, PS[0:q, b * 512:b * 512 + 256]), PE.mark()), b)

    def bc(x, n, m):
        return x.unsqueeze(2).broadcast_to([128, n, m])

    xs = room(2, 1024)
    junk = room(1024)
    qT = room(4, 256)
    kT = room(256)
    kT2 = room(256)
    va = room(2, 128)
    qkT = room(8, 260)
    vm = room(2, 512)
    om = room(2, 512)
    gr = room(2, 8)
    mark_a = space["at"]
    kcT = room_at(mark_a + 5120, 4, 256)
    vc = room_at(mark_a + 6144, 2, 512)
    for o in range(2):
        V.step(lambda e: e.tensor_copy(sink[:, 4 * o:4 * o + 4],
                                       sink_in.rearrange("p (x o) -> p o x", o=2)[:, o, :]), t_b)
    V.step(lambda e: e.memset(qkT[:, :, 0:4], 0.0))

    PE.wait(t_b)
    take(7)
    PE.put(lambda e: e.matmul(PS[0:8, 3584:4096], lhsT=rtab[0:32, :], rhs=hot, start=True, stop=True))
    t_f = S.step(lambda e: e.activation(frow, PS[0:8, 3584:4096], ACT.Copy), PE.mark())
    give(t_f, 7)
    t_toep = dma(G, "toep", toep, frow.unsqueeze(1).broadcast_to([8, 128, 512]), t_f)

    XT = (XTh, XTl)
    rot = [0]

    def nextbank():
        b = rot[0] % 8
        rot[0] += 1
        take(b)
        return b

    def to(dst, b, n, o=0, fn=None):
        t = V.step(fn or (lambda e: e.tensor_copy(dst, bank(b, n, o))), PE.mark())
        give(t, b)
        return t

    t_v = rms_scale(mem, xs, junk, t_mem)
    t_mt = flip(xs, 8, XT, col("mem", 0, 8), t_v)
    t_v = rms_scale(X[:, :, :], xs, junk, t_x, t_mt)
    PE.wait(t_mt)
    project(XT, [cols_job(128 * c, kcT[:, c, :]) for c in range(4)])
    project(XT, [rows_job(t, 0, 512, vc[:, t, :]) for t in range(2)])
    V.wait(PE.mark())
    S.wait(PE.mark())
    t_xt = flip(xs, 8, XT, col("mix", 0, 8), t_v)
    PE.wait(t_xt)
    project(XT, [cols_job(128 * c, qT[:, c, :]) for c in range(4)])
    project(XT, [cols_job(0, kT)] + [rows_job(t, 128, 256, va[:, t, :]) for t in range(2)]
            + [cols_job(256 + 128 * c, qkT[:, c, 4:260]) for c in range(2)])
    t_k2 = dma(G, "k2", kT2[0:64, :], kT[64:128, :], (V.sem, V.n))
    t_k2 = dma(G, "k2", kT2[64:128, :], kT[0:64, :])
    project(XT, [cols_job(128 * c, qkT[:, 2 + c, 4:260]) for c in range(4)])
    project(XT, [cols_job(128 * c, qkT[:, 6 + c, 4:260]) for c in range(2)]
            + [rows_job(t, 256, 512, vm[:, t, 0:256]) for t in range(2)])
    project(XT, [rows_job(t, 0, 256, vm[:, t, 256:512]) for t in range(2)]
            + [rows_job(t, 256, 512, om[:, t, 0:256]) for t in range(2)])
    project(XT, [rows_job(t, 0, 256, om[:, t, 256:512]) for t in range(2)]
            + [rows_job(t, 256, 264, gr[:, t, :]) for t in range(2)])
    fence(t_k2, t_b, t_toep)

    L1 = room_at(0, 8, 256)
    L0 = room(8, 128)
    pT = room(24, 128)
    att = room(2, 512)
    for n in range(8):
        h = head_at(n)
        lo = 64 * (h % 2)
        kk = kT if (h // 4) == (h % 2) else kT2
        mm(PS[:, 256 * n:256 * n + 256], qT[lo:lo + 64, h // 2, 128:256], kk[lo:lo + 64, :], True, True)
        mm(PS[:, 2048 + 128 * n:2048 + 128 * n + 128], qT[lo:lo + 64, h // 2, 0:128], kk[lo:lo + 64, 0:128], True, True)
    t_sc = PE.mark()

    mx = tiny(16)
    dn = tiny(16)
    esk = tiny(16)
    LL = (L0, L1)
    SC = (PS[:, 2048:3072].rearrange("p (h s) -> p h s", h=8), PS[:, 0:2048].rearrange("p (h s) -> p h s", h=8))
    AB = (alibi[:, :, 128:256], alibi)
    for t in range(2):
        m8 = mx[:, 8 * t:8 * t + 8]
        tv = V.step(lambda e, t=t: e.scalar_tensor_tensor(LL[t], SC[t], 0.125, AB[t], ALU.mult, ALU.add), t_sc)
        V.step(lambda e, t=t, m8=m8: e.tensor_reduce(m8, LL[t], AX.X, ALU.max))
        V.step(lambda e, m8=m8: e.tensor_tensor(m8, m8, sink, ALU.max))
        V.step(lambda e, t=t, m8=m8: e.tensor_tensor(esk[:, 8 * t:8 * t + 8], sink, m8, ALU.subtract))
        tv = V.step(lambda e, t=t, m8=m8: e.tensor_tensor(LL[t], LL[t], bc(m8, 8, 128 * (t + 1)), ALU.subtract))
        S.step(lambda e, t=t: e.activation(LL[t], LL[t], ACT.Exp), tv)
        ts = S.step(lambda e, t=t: e.activation(esk[:, 8 * t:8 * t + 8], esk[:, 8 * t:8 * t + 8], ACT.Exp))
        d8 = dn[:, 8 * t:8 * t + 8]
        V.step(lambda e, t=t, d8=d8: e.tensor_reduce(d8, LL[t], AX.X, ALU.add), ts)
        V.step(lambda e, t=t, d8=d8: e.tensor_tensor(d8, d8, esk[:, 8 * t:8 * t + 8], ALU.add))
        V.step(lambda e, d8=d8: e.reciprocal(d8, d8))
    fence()
    n = 0
    for t in range(2):
        for h in range(8):
            for j in range(t + 1):
                PE.put(lambda e, n=n, t=t, h=h, j=j: e.transpose(PS[:, 128 * n:128 * n + 128],
                                                                 LL[t][:, h, 128 * j:128 * j + 128], ident))
                n += 1
                if n % 4 == 0:
                    b = n // 4 - 1
                    V.step(lambda e, b=b: e.tensor_copy(pT[:, 4 * b:4 * b + 4, :].rearrange("p a b -> p (a b)"), bank(b)),
                           PE.mark())
    PE.wait((V.sem, V.n))
    n = 0
    for t in range(2):
        for m in range(8):
            kv = 64 * (head_at(m) // 4)
            for j in range(t + 1):
                mm(bank(6 + t, 64, 64 * m), pT[:, n, :], va[:, j, kv:kv + 64], j == 0, j == t)
                n += 1
    for t in range(2):
        for o in range(2):
            V.step(lambda e: e.tensor_tensor(att[:, t, :].rearrange("p (x o d) -> p x o d", o=2, d=64)[:, :, o, :],
                                             bank(6 + t, 256, 256 * o).rearrange("p (h d) -> p h d", h=4),
                                             bc(dn[:, 8 * t + 4 * o:8 * t + 4 * o + 4], 4, 64), ALU.mult), PE.mark())
    t_v = rms_scale(att, att, junk, (V.sem, V.n), width=512)
    flip(att, 4, XT, col("att", 0, 4), t_v)
    fence()

    cv = room_at(0, 8, 256)
    space["at"] = mark_a
    R = room(2, 4, 256)
    tmp = room(256)
    AM0 = room(4, 128)
    AM1 = room_at(4096, 4, 256)
    sT = room(12, 128)
    hm = room_at(5120, 2, 512)
    assert space["at"] <= mark_a + 5120
    lf = tiny(16)
    gi = tiny(16)
    ga = tiny(16)
    for c in range(8):
        V.step(lambda e, c=c: e.tensor_scalar(cv[:, c, :], qkT[:, c, 1:257], col("convw", c), col("convb", c),
                                              ALU.mult, ALU.add))
        for j in range(1, 4):
            V.step(lambda e, c=c, j=j: e.scalar_tensor_tensor(cv[:, c, :], qkT[:, c, 1 + j:257 + j],
                                                              col("convw", 8 * j + c), cv[:, c, :], ALU.mult, ALU.add))
    t_cv = S.step(lambda e: e.activation(cv, cv, ACT.Silu), (V.sem, V.n))
    for t in range(2):
        V.step(lambda e, t=t: e.tensor_tensor(gi[:, 8 * t:8 * t + 8], gr[:, t, :], bgate, ALU.add))
    gi3 = gi.rearrange("p (t g) -> p t g", t=2)
    ipre = gi3[:, :, 0:4]
    fpre = gi3[:, :, 4:8]
    lf3 = lf[:, 0:8].rearrange("p (t g) -> p t g", t=2)
    nlf = lf[:, 8:16].rearrange("p (t g) -> p t g", t=2)
    ga3 = ga[:, 0:8].rearrange("p (t g) -> p t g", t=2)
    t_v = V.step(lambda e: e.scalar_tensor_tensor(ga3, fpre, -1.0, fpre, ALU.mult, ALU.max))
    S.step(lambda e: e.activation(ga3, ga3, ACT.Exp, scale=-1.0), t_v)
    t_s = S.step(lambda e: e.activation(ga3, ga3, ACT.Ln, bias=1.0))
    V.step(lambda e: e.tensor_scalar(lf3, fpre, 0.0, None, ALU.min))
    V.step(lambda e: e.tensor_tensor(lf3, lf3, ga3, ALU.subtract), t_s)
    V.step(lambda e: e.tensor_scalar(nlf, lf3, -1.0, None, ALU.mult))
    for j in range(2):
        for h in range(4):
            V.step(lambda e, j=j, h=h: e.tensor_scalar(tmp, eye[:, j, :], ipre[:, j, h:h + 1], None, ALU.mult))
            V.step(lambda e, j=j, h=h: e.scalar_tensor_tensor(R[:, j, h, :], upper[:, j, :], nlf[:, j, h:h + 1], tmp,
                                                              ALU.mult, ALU.add))
    PE.wait((V.sem, V.n))
    for hh in range(2):
        for j in range(2):
            mm(bank(hh), ones, R[:, j, 2 * hh:2 * hh + 2, :].rearrange("p a b -> p (a b)"), j == 0, j == 1)
    for t in range(2):
        for j in range(t + 1):
            mm(bank(2, 4, 4 * t), upper[:, j, 128 * t:128 * t + 128], lf3[:, j, :], j == 0, j == t)
    t_a = PE.mark()
    PE.wait(t_cv)
    for h in range(4):
        mm(bank(3, 128, 128 * h), cv[:, h, 0:128], cv[:, 4 + h, 0:128], True, True)
    for h in range(4):
        mm(PS[:, 2048 + 256 * h:2048 + 256 * h + 256], cv[:, h, 128:256], cv[:, 4 + h, :], True, True)
    t_q = PE.mark()
    A3 = PS[:, 0:1024].rearrange("p (h s) -> p h s", h=4)
    QK = (bank(3).rearrange("p (h s) -> p h s", h=4), PS[:, 2048:3072].rearrange("p (h s) -> p h s", h=4))
    AM = (AM0, AM1)
    M = tiny(8)
    em = tiny(8)
    for t in range(2):
        w1 = 128 * (t + 1)
        m4, e4, d4 = M[:, 4 * t:4 * t + 4], em[:, 4 * t:4 * t + 4], dn[:, 4 * t:4 * t + 4]
        V.step(lambda e, t=t, w1=w1: e.tensor_tensor(AM[t], A3[:, :, 0:w1],
                                                     causal[:, t, 0:w1].unsqueeze(1).broadcast_to([128, 4, w1]), ALU.add), t_a)
        V.step(lambda e, t=t, m4=m4: e.tensor_reduce(m4, AM[t], AX.X, ALU.max))
        V.step(lambda e, m4=m4: e.tensor_scalar(m4, m4, 0.0, None, ALU.max))
        V.step(lambda e, t=t, m4=m4, w1=w1: e.tensor_tensor(AM[t], AM[t], bc(m4, 4, w1), ALU.subtract))
        t_v = V.step(lambda e, t=t, m4=m4, e4=e4: e.tensor_tensor(e4, bank(2, 4, 4 * t), m4, ALU.add))
        S.step(lambda e, t=t: e.activation(AM[t], AM[t], ACT.Exp), t_v)
        t_s = S.step(lambda e, e4=e4: e.activation(e4, e4, ACT.Exp, scale=-1.0))
        V.step(lambda e, t=t: e.scalar_tensor_tensor(AM[t], QK[t], 128 ** -0.5, AM[t], ALU.mult, ALU.mult), t_s, t_q)
        V.step(lambda e, t=t, d4=d4: e.tensor_reduce(d4, AM[t], AX.X, ALU.add))
        V.step(lambda e, d4=d4: e.scalar_tensor_tensor(d4, d4, -1.0, d4, ALU.mult, ALU.max))
        V.step(lambda e, d4=d4, e4=e4: e.tensor_tensor(d4, d4, e4, ALU.max))
        V.step(lambda e, d4=d4: e.reciprocal(d4, d4))
    t_s = S.step(lambda e: e.activation(om, om, ACT.Tanh, scale=0.5))
    V.step(lambda e: e.tensor_scalar(om, om, 0.5, 0.5, ALU.mult, ALU.add), t_s)
    fence()
    n = 0
    for t in range(2):
        for h in range(4):
            for j in range(t + 1):
                PE.put(lambda e, n=n, t=t, h=h, j=j: e.transpose(PS[:, 128 * n:128 * n + 128],
                                                                 AM[t][:, h, 128 * j:128 * j + 128], ident))
                n += 1
                if n % 4 == 0:
                    b = n // 4 - 1
                    V.step(lambda e, b=b: e.tensor_copy(sT[:, 4 * b:4 * b + 4, :].rearrange("p a b -> p (a b)"), bank(b)),
                           PE.mark())
    PE.wait((V.sem, V.n))
    n = 0
    for t in range(2):
        for h in range(4):
            for j in range(t + 1):
                mm(bank(6 + t, 128, 128 * h), sT[:, n, :], vm[:, j, 128 * h:128 * h + 128], j == 0, j == t)
                n += 1
    sq = tiny(8)
    for t in range(2):
        hv = hm[:, t, :].rearrange("p (h d) -> p h d", h=4)
        s4 = sq[:, 4 * t:4 * t + 4]
        V.step(lambda e, t=t, hv=hv: e.tensor_tensor(hv, bank(6 + t).rearrange("p (h d) -> p h d", h=4),
                                                     bc(dn[:, 4 * t:4 * t + 4], 4, 128), ALU.mult), PE.mark())
        V.step(lambda e, t=t: e.tensor_tensor(hm[:, t, :], hm[:, t, :], om[:, t, :], ALU.mult))
        jv = junk[:, 0:512].rearrange("p (h d) -> p h d", h=4)
        V.step(lambda e, jv=jv, hv=hv: e.tensor_tensor(jv, hv, hv, ALU.mult))
        V.step(lambda e, jv=jv, s4=s4: e.tensor_reduce(s4, jv, AX.X, ALU.add))
        V.step(lambda e, s4=s4: e.tensor_scalar(s4, s4, 1.0 / 128, 1e-6, ALU.mult, ALU.add))
        rsqrt(s4, 4)
        V.step(lambda e, hv=hv, s4=s4: e.tensor_tensor(hv, hv, bc(s4, 4, 128), ALU.mult))
    t_v = flip(hm, 4, [x[:, 4:8, :] for x in XT], col("ml", 0, 4), (V.sem, V.n))
    PE.wait(t_v)

    def add_to_x(t, nn, b, scale=None):
        xv = X[:, t, 512 * nn:512 * nn + 512]
        if scale is None:
            return to(None, b, 512, fn=lambda e: e.tensor_tensor(xv, bank(b), xv, ALU.add))
        return to(None, b, 512, fn=lambda e: e.scalar_tensor_tensor(xv, bank(b), scale, xv, ALU.mult, ALU.add))

    def add_out():
        for nn in range(2):
            def plus(t):
                xv = X[:, t, 512 * nn:512 * nn + 512]
                return lambda e, b: e.tensor_tensor(xv, bank(b), xv, ALU.add)
            project(XT, [rows_job(t, 0, 512, fn=plus(t)) for t in range(2)])

    def deep_sum(xt, nk, first=True, last=True, k0=0):
        for p in range(nk // 2):
            w = part()
            for t in range(2):
                for nn in range(2):
                    for k in range(2):
                        kk = 2 * p + k
                        use_rows(bank(4 + 2 * t + nn), xt, k0 + kk, t, w, k, 512 * nn, 512 * nn + 512,
                                 first and kk == 0, last and kk == nk - 1)
            done()

    add_out()
    fence()

    xs = room_at(0, 2, 1024)
    junk = room_at(2048, 1024)
    space["at"] = mark_a
    Lc = room(4, 256)
    pcT = room(8, 128)
    qcT = room(4, 256)
    assert space["at"] <= mark_a + 5120
    t_v = rms_scale(X[:, :, :], xs, junk)
    t_v = flip(xs, 8, XT, col("cross", 0, 8), t_v)
    PE.wait(t_v)
    project(XT, [cols_job(128 * c, qcT[:, c, :]) for c in range(4)])
    for t in range(2):
        fence()
        for h in range(4):
            mm(PS[:, 256 * h:256 * h + 256], qcT[:, h, 128 * t:128 * t + 128], kcT[:, h, :], True, True)
        sc3 = PS[:, 0:1024].rearrange("p (h s) -> p h s", h=4)
        m4, d4 = mx[:, 0:4], dn[:, 0:4]
        V.step(lambda e, sc3=sc3, m4=m4: e.tensor_reduce(m4, sc3, AX.X, ALU.max), PE.mark())
        t_v = V.step(lambda e, sc3=sc3, m4=m4: e.tensor_tensor(Lc, sc3, bc(m4, 4, 256), ALU.subtract))
        t_s = S.step(lambda e: e.activation(Lc, Lc, ACT.Exp, scale=128 ** -0.5), t_v)
        V.step(lambda e, d4=d4: e.tensor_reduce(d4, Lc, AX.X, ALU.add), t_s)
        V.step(lambda e, d4=d4: e.reciprocal(d4, d4))
        t_v = V.step(lambda e, d4=d4: e.tensor_tensor(Lc, Lc, bc(d4, 4, 256), ALU.mult))
        PE.wait(t_v)
        for n in range(8):
            PE.put(lambda e, n=n: e.transpose(PS[:, 1024 + 128 * n:1152 + 128 * n],
                                              Lc[:, n // 2, 128 * (n % 2):128 * (n % 2) + 128], ident))
        t_v = V.step(lambda e: e.tensor_copy(pcT.rearrange("p a b -> p (a b)"), PS[:, 1024:2048]), PE.mark())
        PE.wait(t_v)
        for h in range(4):
            for j in range(2):
                mm(bank(4, 128, 128 * h), vc[:, j, 128 * h:128 * h + 128], pcT[:, 2 * h + j, :], j == 0, j == 1)
        cut([x[:, 0:4, 128 * t:128 * t + 128] for x in XT], bank(4).rearrange("p (h s) -> p h s", h=4), PE.mark())
    fence()
    deep_sum(XT, 4)
    for t in range(2):
        for nn in range(2):
            add_to_x(t, nn, 4 + 2 * t + nn)
    fence()

    phase(13056)
    W0 = room_at(0, 4096)
    W1 = room_at(12032, 1024)
    xs = room(2, 1024)
    junk = room(1024)
    gffn = room(1024)
    gfin = room(1024)
    t_gf = dma(S, "gf", gfin, a["norm_final"].rearrange("(a n) -> a n", a=1).broadcast_to([128, 1024]))
    t_gn = dma(S, "gn", gffn, a["norm_ffn"].broadcast_to([128, 1024]))
    wr = room(8, 36)
    rt = room(2, 36)
    gates = room(2, 32)
    wk = room(4, 2, 32)
    t_wr = dma(S, "wr", wr[:, :, 0:4], a["w_router_group"][0].rearrange("(k p) n -> p k n", p=128))
    t_wr = dma(S, "wr", wr[:, :, 4:36], a["w_router_expert"][0].rearrange("(k p) n -> p k n", p=128))
    wrh, wrl = pieces_of("wr", 8, 36)
    cut((wrh[:, :, :], wrl[:, :, :]), wr, t_wr)
    rms_scale(X[:, :, :], xs, junk)
    for t in range(2):
        t_v = V.step(lambda e: e.tensor_tensor(xs[:, t, :], xs[:, t, :], gffn, ALU.mult), t_gn)
    t_xn = dma(G, "xn", xn_d.rearrange("(t p) n -> p t n", p=128), xs, t_v)
    t_v = flip(xs, 8, XT, None, t_v)
    PE.wait(t_v)
    for t in range(2):
        b = nextbank()
        for k in range(8):
            use_rows(bank(b, 36), XT, k, t, (wrh, wrl), k, 0, 36, k == 0, k == 7)
        to(None, b, 36, fn=lambda e, t=t, b=b: e.tensor_tensor(rt[:, t, :], bank(b, 36), brout, ALU.add))
    st = tiny(16)
    g1, e1, g2_ = st[:, 0:2], st[:, 2:4], st[:, 4:6]
    gl = rt[:, :, 0:4]
    oh, ex = wk[:, 0, :, 0:4], wk[:, 1, :, 0:4]

    def first_hit(vals, n, hit, best, where):
        V.step(lambda e: e.tensor_reduce(best, vals, AX.X, ALU.max))
        V.step(lambda e: e.tensor_tensor(hit, vals, bc(best, 2, n), ALU.is_equal))
        io = iota[:, 0:n].unsqueeze(1).broadcast_to([128, 2, n])
        V.step(lambda e: e.tensor_scalar(hit, hit, -64.0, 64.0, ALU.mult, ALU.add))
        V.step(lambda e: e.tensor_tensor(hit, hit, io, ALU.add))
        V.step(lambda e: e.tensor_reduce(where, hit, AX.X, ALU.min))
        V.step(lambda e: e.tensor_tensor(hit, bc(where, 2, n), io, ALU.is_equal))

    idx = st[:, 6:8]
    first_hit(gl, 4, oh, g1, idx)
    t_v = V.step(lambda e: e.tensor_tensor(ex, gl, bc(g1, 2, 4), ALU.subtract))
    t_s = S.step(lambda e: e.activation(ex, ex, ACT.Exp), t_v)
    V.step(lambda e: e.tensor_reduce(g2_, ex, AX.X, ALU.add), t_s)
    V.step(lambda e: e.reciprocal(g2_, g2_))
    el = wk[:, 1, :, :]
    o1, o2 = wk[:, 2, :, :], wk[:, 3, :, :]
    off = wk[:, 0, :, 4:8]
    V.step(lambda e: e.tensor_scalar(off, oh, -NEG, NEG, ALU.mult, ALU.add))
    for t in range(2):
        e3 = el[:, t, :].rearrange("p (g x) -> p g x", g=4)
        r3 = rt[:, t, 4:36].rearrange("p (g x) -> p g x", g=4)
        V.step(lambda e, t=t, e3=e3, r3=r3: e.tensor_tensor(e3, r3, bc(oh[:, t, :], 4, 8), ALU.mult))
        V.step(lambda e, t=t, e3=e3: e.tensor_tensor(e3, e3, bc(off[:, t, :], 4, 8), ALU.add))
    first_hit(el, 32, o1, g1, idx)
    V.step(lambda e: e.scalar_tensor_tensor(el, o1, NEG, el, ALU.mult, ALU.add))
    first_hit(el, 32, o2, e1, idx)
    t_v = V.step(lambda e: e.tensor_tensor(e1, e1, g1, ALU.subtract))
    t_s = S.step(lambda e: e.activation(e1, e1, ACT.Exp), t_v)
    V.step(lambda e: e.tensor_scalar(g1, e1, 1.0, None, ALU.add), t_s)
    V.step(lambda e: e.reciprocal(g1, g1))
    V.step(lambda e: e.tensor_tensor(g1, g1, g2_, ALU.mult))
    V.step(lambda e: e.tensor_tensor(e1, e1, g1, ALU.mult))
    both = gates
    t_v = V.step(lambda e: e.tensor_tensor(both, o1, o2, ALU.add))
    PE.wait(t_v)
    take(0, 1)
    for t in range(2):
        for j in range(t + 1):
            mm(bank(0, 32, 32 * t), upper[:, j, 128 * t:128 * t + 128], both[:, j, :], j == 0, j == t)
    for j in range(2):
        mm(bank(1, 32), ones, both[:, j, :], j == 0, j == 1)
    Z = room(2, 32)
    ints = space["stack"].enter_context(nc.sbuf_tensor("ints", [128, 144], I32))
    none, val, dest, most = ints[:, 0:64], ints[:, 64:68], ints[:, 68:72], ints[:, 72:73]
    six, gix = ints[:, 80:112], ints[:, 112:144]
    df = tiny(6)
    V.step(lambda e: e.tensor_scalar(Z, bank(0, 64).rearrange("p (t x) -> p t x", t=2), 32.0, -32.0,
                                     ALU.mult, ALU.add), PE.mark())
    V.step(lambda e: e.tensor_tensor(Z, Z, iota.unsqueeze(1).broadcast_to([128, 2, 32]), ALU.add))
    for k, o in ((0, o1), (1, o2)):
        V.step(lambda e: e.tensor_tensor(o, o, Z, ALU.mult))
        V.step(lambda e: e.tensor_reduce(df[:, 2 * k:2 * k + 2], o, AX.X, ALU.add))
    V.step(lambda e: e.tensor_copy(dest, df[:, 0:4]))
    V.step(lambda e: e.tensor_copy(val, C("slot")))
    V.step(lambda e: e.tensor_reduce(df[:, 4:5], bank(1, 32), AX.X, ALU.max))
    V.step(lambda e: e.tensor_copy(most, df[:, 4:5]))
    t_v = V.step(lambda e: e.memset(none, NONE))
    t_l = dma(G, "li", lists.rearrange("(p c) a -> p (c a)", p=128), none, t_v)

    def indirect(name, out_, out_ix, in_, in_ix, bound, *tokens):
        return dma_of(G, name, lambda e: e.indirect_dma_start(
            out=out_, out_offset=None if out_ix is None else bass.IndirectOffsetOnAxis(ap=out_ix, axis=0),
            in_=in_, in_offset=None if in_ix is None else bass.IndirectOffsetOnAxis(ap=in_ix, axis=0),
            bounds_check=bound, oob_is_err=False), *tokens)

    for k in range(4):
        t_l2 = indirect("ls", lists, dest[:, k:k + 1], val[:, k:k + 1], None, 8191, t_l)
    rank = lists.rearrange("(r e) a -> r (e a)", e=32)

    def load_lists(G, r0, *tokens, name="ll"):
        return dma(G, name, six, rank[r0:r0 + 128, :], *tokens)

    def tokens_of(V, t_six):
        Zf = Z[:, 0, :]
        Zg = Z[:, 1, :]
        V.step(lambda e: e.tensor_copy(Zf, six), t_six)
        V.step(lambda e: e.tensor_scalar(Zg, Zf, 256.0, -256.0, ALU.is_ge, ALU.mult))
        V.step(lambda e: e.tensor_tensor(Zf, Zf, Zg, ALU.add))
        return V.step(lambda e: e.tensor_copy(gix, Zf))

    t_gix = tokens_of(V, load_lists(G, 0, t_l2))

    xg = room(3, 1024)
    yr = room(2, 1024)
    hs = room(512)
    hr = room(512)
    assert space["at"] <= 12032, space["at"]
    for b in range(3):
        t_z = V.step(lambda e: e.memset(xg[:, b, :], 0.0))
    fence(t_gix, t_xn)
    xgT = [pieces_of(f"xgT{x}", 8, 128) for x in range(2)]
    hT = [pieces_of(f"hT{x}", 4, 128) for x in range(2)]
    got = {}
    y_done = [(PE.sem, 0)] * 2

    def gather(e_, *tokens):
        if e_ < 32:
            got[e_] = indirect(f"xg{e_ % 3}", xg[:, e_ % 3, :], None, xn_d, gix[:, e_:e_ + 1], 255, *tokens)

    def turn_x(e_):
        PE.wait(got[e_])
        for k0 in (0, 4):
            b = 6 + k0 // 4
            take(b)
            for k in range(4):
                PE.put(lambda e: e.transpose(bank(b, 128, 128 * k), xg[:, e_ % 3, 128 * (k0 + k):128 * (k0 + k) + 128],
                                             ident))
            tc = cut([x[:, k0:k0 + 4, :] for x in xgT[e_ % 2]], bank(b).rearrange("p (k i) -> p k i", k=4), PE.mark())
            give(tc, b)
        gather(e_ + 3, PE.mark())
        return tc

    def expert_part(e_, b, p):
        w = part()
        for k in range(4):
            kk = 4 * p + k
            use_rows(bank(b), xgT[e_ % 2], kk, 0, w, k, 0, 512, kk == 0, kk == 7)
        done()

    def turn_h(e_, tv):
        take(2)
        PE.wait(tv)
        for k in range(4):
            PE.put(lambda e: e.transpose(bank(2, 128, 128 * k), hr[:, 128 * k:128 * k + 128], ident))
        tc = cut([x[:, :, :] for x in hT[e_ % 2]], bank(2).rearrange("p (k i) -> p k i", k=4), PE.mark())
        give(tc, 2)
        return tc

    def expert_down(e_, tc):
        take(4, 5)
        PE.wait(tc)
        for p in range(2):
            w = part()
            for nn in range(2):
                for k in range(2):
                    kk = 2 * p + k
                    use_rows(bank(4 + nn), hT[e_ % 2], kk, 0, w, k, 512 * nn, 512 * nn + 512, kk == 0, kk == 3)
            done()
        o = e_ % 2
        ta = S.step(lambda e: e.activation(yr[:, o, 0:512], bank(4), ACT.Copy), PE.mark(), y_done[o])
        tb = S.step(lambda e: e.activation(yr[:, o, 512:1024], bank(5), ACT.Copy))
        give(ta, 4)
        give(tb, 5)
        y_done[o] = indirect(f"yd{o}", y_d, six[:, e_:e_ + 1], yr[:, o, :], None, 511, tb)

    for e_ in range(3):
        gather(e_)
    tx = turn_x(0)
    tv = (PE.sem, 0)
    for e_ in range(32):
        take(0)
        PE.wait(tx)
        expert_part(e_, 0, 0)
        tc = turn_h(e_ - 1, tv) if e_ else None
        expert_part(e_, 0, 1)
        ts = S.step(lambda e: e.activation(hs, bank(0), ACT.Silu), PE.mark(), tv)
        give(ts, 0)
        if e_:
            expert_down(e_ - 1, tc)
        take(1)
        expert_part(e_, 1, 0)
        if e_ < 31:
            tx = turn_x(e_ + 1)
        expert_part(e_, 1, 1)
        tv = V.step(lambda e: e.tensor_tensor(hr, hs, bank(1), ALU.mult), ts, PE.mark())
        give(tv, 1)
    expert_down(31, turn_h(31, tv))
    fence(*y_done)
    SP.wait((V.sem, V.n), *y_done)

    osem = [sem("o_" + x) for x in ("pe", "v", "s", "g", "sp")]
    engines = (nc.tensor, nc.vector, nc.scalar, nc.gpsimd, nc.sync)

    def rest(live):
        oPE, oV, oS, oG, oSP = (Lane(e, q, n == live) for n, (e, q) in enumerate(zip(engines, osem)))
        for name in ("o_ll", "o_xg", "o_w", "o_yd"):
            if name in dma_count:
                dma_count[name][1] = 0
        xT_ = W1
        t_l = load_lists(oG, 128, name="o_ll")
        t_v = tokens_of(oV, t_l)
        oG.wait(t_v)
        free = (oPE.sem, 0)
        for e_ in range(32):
            t_x = dma_of(oG, "o_xg", lambda e: e.indirect_dma_start(
                out=xg[:, 0, :], out_offset=None, in_=xn_d,
                in_offset=bass.IndirectOffsetOnAxis(ap=gix[:, e_:e_ + 1], axis=0), bounds_check=255,
                oob_is_err=False), free)
            w_src = [a["w_e_gate"][0, e_].rearrange("(k p) n -> p k n", p=128),
                     a["w_e_up"][0, e_].rearrange("(k p) n -> p k n", p=128),
                     a["w_e_down"][0, e_].rearrange("(k p) n -> p k n", p=128)]
            oPE.wait(t_x, (oV.sem, oV.n), (oS.sem, oS.n))
            for k in range(8):
                oPE.put(lambda e: e.transpose(bank(6 + k // 4, 128, 128 * (k % 4)), xg[:, 0, 128 * k:128 * k + 128], ident))
            oV.step(lambda e: e.tensor_copy(xT_, PS[:, 3072:4096]), oPE.mark())
            for q in range(2):
                t_w = dma(oSP, "o_w", W0.rearrange("p (k n) -> p k n", k=8), w_src[q], oPE.mark(), free)
                oPE.wait(t_w, (oV.sem, oV.n))
                for k in range(8):
                    oPE.put(lambda e: e.matmul(bank(q), lhsT=xT_[:, 128 * k:128 * k + 128],
                                               rhs=W0[:, 512 * k:512 * k + 512], start=k == 0, stop=k == 7))
                oPE.mark()
            t_s = oS.step(lambda e: e.activation(hs, bank(0), ACT.Silu), (oPE.sem, oPE.n))
            t_v = oV.step(lambda e: e.tensor_tensor(hr, hs, bank(1), ALU.mult), t_s)
            oPE.wait(t_v)
            for k in range(4):
                oPE.put(lambda e: e.transpose(bank(2, 128, 128 * k), hr[:, 128 * k:128 * k + 128], ident))
            t_v = oV.step(lambda e: e.tensor_copy(xT_[:, 0:512], bank(2)), oPE.mark())
            t_w = dma(oSP, "o_w", W0.rearrange("p (k n) -> p k n", k=4), w_src[2], (oPE.sem, oPE.n))
            oPE.wait(t_w, t_v)
            for nn in range(2):
                for k in range(4):
                    oPE.put(lambda e: e.matmul(bank(4 + nn), lhsT=xT_[:, 128 * k:128 * k + 128],
                                               rhs=W0[:, 1024 * k + 512 * nn:1024 * k + 512 * nn + 512],
                                               start=k == 0, stop=k == 3))
            t_v = oV.step(lambda e: e.tensor_copy(yr[:, 0, :], PS[:, 2048:3072]), oPE.mark())
            free = dma_of(oG, "o_yd", lambda e: e.indirect_dma_start(
                out=y_d, out_offset=bass.IndirectOffsetOnAxis(ap=six[:, e_:e_ + 1], axis=0), in_=yr[:, 0, :],
                in_offset=None, bounds_check=511, oob_is_err=False), t_v)
            oV.wait(free)
            oPE.wait(free)
        for lane in (oPE, oV, oS, oG, oSP):
            lane.wait(free, (oPE.sem, oPE.n), (oV.sem, oV.n), (oS.sem, oS.n))

    def branch(n, eng):
        count = eng.value_load(most[0:1, 0:1])
        with eng.If(count > 128):
            rest(n)

    with nc.Block() as block:
        @block.tensor
        def _(eng):
            branch(0, eng)

        @block.vector
        def _(eng):
            branch(1, eng)

        @block.scalar
        def _(eng):
            branch(2, eng)

        @block.gpsimd
        def _(eng):
            branch(3, eng)

        @block.sync
        def _(eng):
            branch(4, eng)

    yy = room_at(7168, 4, 1024)
    t_y = dma(S, "yy", yy, y_d.rearrange("(k p) n -> p k n", p=128))
    for t in range(2):
        for k, g in ((0, g1), (1, e1)):
            V.step(lambda e: e.scalar_tensor_tensor(X[:, t, :], yy[:, 2 * k + t, :], g[:, t:t + 1], X[:, t, :],
                                                    ALU.mult, ALU.add), t_y)
    t_v = rms_scale(X[:, :, :], X[:, :, :], junk, (V.sem, V.n))
    for t in range(2):
        V.step(lambda e: e.tensor_tensor(X[:, t, :], X[:, t, :], gfin, ALU.mult), t_gf)
    fence()

    rot4 = [0]

    def rbank():
        b = rot4[0] % 4
        rot4[0] += 1
        take(b)
        return b

    def swiglu(gain_row):
        phase(5120)
        xs = room(2, 1024)
        junk = room(1024)
        hs = room(4, 256)
        hr = room(4, 256)
        hT = pieces_of("hT", 22, 256)
        t_v = rms_scale(X[:, :, :], xs, junk)
        t_v = flip(xs, 8, XT, gc[:, gain_row:gain_row + 8], t_v)
        PE.wait(t_v)
        hsr = [(V.sem, 0)] * 4
        hrr = [(PE.sem, 0)] * 4
        full = {}

        def turn(c):
            for t in range(2):
                b = nextbank()
                slot = 2 * (c % 2) + t
                PE.wait(full[(c, t)])
                for k in range(2):
                    PE.put(lambda e: e.transpose(bank(b, 128, 128 * k), hr[:, slot, 128 * k:128 * k + 128], ident))
                tp = PE.mark()
                hrr[slot] = tp
                tc = cut([x[:, 2 * c:2 * c + 2, 128 * t:128 * t + 128] for x in hT],
                         bank(b, 256).rearrange("p (k i) -> p k i", k=2), tp)
                give(tc, b)
            return tc

        for c in range(11):
            bs = (nextbank(), nextbank())
            for p in range(2):
                w = part()
                for t in range(2):
                    for k in range(4):
                        kk = 4 * p + k
                        use_rows(bank(bs[t]), XT, kk, t, w, k, 0, 512, kk == 0, kk == 7)
                done()
                if c and p == 0:
                    turn(c - 1)
            tp = PE.mark()
            for t in range(2):
                b, slot = bs[t], 2 * (c % 2) + t
                ts = S.step(lambda e: e.activation(hs[:, slot, :], bank(b, 256), ACT.Silu), tp, hsr[slot])
                tv = V.step(lambda e: e.tensor_tensor(hr[:, slot, :], hs[:, slot, :], bank(b, 256, 256), ALU.mult),
                            ts, tp, hrr[slot])
                give(tv, b)
                hsr[slot] = tv
                full[(c, t)] = tv
        tc = turn(10)
        take(4, 5, 6, 7)
        PE.wait(tc)
        deep_sum(hT, 22)
        for t in range(2):
            for nn in range(2):
                add_to_x(t, nn, 4 + 2 * t + nn, 0.5)
        fence()

    g2 = GAIN["g2"]
    swiglu(g2)

    phase(19200)
    qT = room(8, 256)
    kT = room(8, 256)
    va = room(2, 1024)
    qi = room(4, 256)
    ki = room(256)
    BT = room(2, 8, 256)
    la = space["at"]
    xs = room(2, 1024)
    junk = room(1024)
    space["at"] = la
    sc = room(256)
    w0 = room(256)
    w1_ = room(256)
    La = room(8, 256)
    pa = room(16, 128)
    wi = tiny(16)
    for t in range(2):
        src = bass.AP(tensor=toep.tensor, offset=255 - 128 * t, ap=[[511, 128], [65536, 8], [1, 256]])
        t_bt = dma(G, "bt", BT[:, t, :, :], src, t_toep)
    t_v = rms_scale(X[:, :, :], xs, junk)
    t_v = flip(xs, 8, XT, gc[:, g2 + 8:g2 + 16], t_v)
    PE.wait(t_v)
    for dst in (qT, kT):
        for u in range(2):
            project(XT, [cols_job(128 * c, dst[:, 4 * u + c, :]) for c in range(4)])
    for u in range(2):
        project(XT, [rows_job(t, 0, 512, va[:, t, 512 * u:512 * u + 512]) for t in range(2)])
    project(XT, [cols_job(128 * c, qi[:, c, :]) for c in range(4)])

    def gate(t):
        return lambda e, b: e.tensor_scalar(wi[:, 8 * t:8 * t + 8], bank(b, 8), 8 ** -0.5 / 8, None, ALU.mult)

    project(XT, [cols_job(0, ki[0:64, :], m=72, keep=64)] + [rows_job(t, 64, 72, fn=gate(t)) for t in range(2)])
    t_ki = dma(G, "ki", ki[64:128, :], ki[0:64, :], (V.sem, V.n))
    fence(t_ki, t_bt)
    best = tiny(8)
    for t in range(2):
        for n in range(8):
            h = head_at(n)
            lo = 64 * (h % 2)
            mm(PS[:, 256 * n:256 * n + 256], qi[lo:lo + 64, h // 2, 128 * t:128 * t + 128], ki[lo:lo + 64, :], True, True)
        t_i = PE.mark()
        for h in range(8):
            mm(PS[:, 2048 + 256 * h:2304 + 256 * h], qT[:, h, 128 * t:128 * t + 128], kT[:, h, :], True, True)
        t_q = PE.mark()
        for n in range(8):
            wcol = wi[:, 8 * t + head_at(n):8 * t + head_at(n) + 1]
            V.step(lambda e: e.tensor_scalar(w0, PS[:, 256 * n:256 * n + 256], 0.0, wcol, ALU.max, ALU.mult), t_i)
            if n == 0:
                V.step(lambda e, t=t: e.tensor_copy(sc, w0))
            else:
                V.step(lambda e: e.tensor_tensor(sc, sc, w0, ALU.add))
        V.step(lambda e, t=t: e.tensor_tensor(sc, sc, causal[:, t, :], ALU.add))
        cur = sc
        for r in range(8):
            nxt = w0 if r % 2 == 0 else w1_
            V.step(lambda e, cur=cur: e.max(best, cur))
            V.step(lambda e, cur=cur, nxt=nxt: e.match_replace(nxt, best, cur, GONE))
            cur = nxt
        V.step(lambda e, cur=cur: e.tensor_scalar(cur, cur, -2.0e38, None, ALU.is_gt))
        V.step(lambda e, cur=cur, t=t: e.scalar_tensor_tensor(cur, cur, NEG, causal[:, t, :], ALU.mult, ALU.add))
        V.step(lambda e, t=t: e.scalar_tensor_tensor(La, PS[:, 2048:4096].rearrange("p (h s) -> p h s", h=8),
                                                     128 ** -0.5, BT[:, t, :, :], ALU.mult, ALU.add), t_q)
        V.step(lambda e, cur=cur: e.tensor_tensor(La, La, cur.unsqueeze(1).broadcast_to([128, 8, 256]), ALU.add))
        m8, d8 = mx[:, 0:8], dn[:, 0:8]
        V.step(lambda e, m8=m8: e.tensor_reduce(m8, La, AX.X, ALU.max))
        t_v = V.step(lambda e, m8=m8: e.tensor_tensor(La, La, bc(m8, 8, 256), ALU.subtract))
        t_s = S.step(lambda e: e.activation(La, La, ACT.Exp), t_v)
        V.step(lambda e, d8=d8: e.tensor_reduce(d8, La, AX.X, ALU.add), t_s)
        V.step(lambda e, d8=d8: e.reciprocal(d8, d8))
        t_v = V.step(lambda e, d8=d8: e.tensor_tensor(La, La, bc(d8, 8, 256), ALU.mult))
        PE.wait(t_v)
        for n in range(16):
            PE.put(lambda e, n=n: e.transpose(PS[:, 128 * n:128 * n + 128],
                                              La[:, n // 2, 128 * (n % 2):128 * (n % 2) + 128], ident))
        t_v = V.step(lambda e: e.tensor_copy(pa.rearrange("p a b -> p (a b)"), PS[:, 0:2048]), PE.mark())
        PE.wait(t_v)
        for h in range(8):
            for j in range(2):
                mm(PS[:, 2048 + 128 * h:2176 + 128 * h], va[:, j, 128 * h:128 * h + 128], pa[:, 2 * h + j, :],
                   j == 0, j == 1)
        cut([x[:, :, 128 * t:128 * t + 128] for x in XT], PS[:, 2048:3072].rearrange("p (h s) -> p h s", h=8), PE.mark())
        fence()
    add_out()
    fence()

    swiglu(g2 + 16)
    swiglu(g2 + 24)

    phase(17408)
    uu = room(2, 3072)
    vv = room(2, 3072)
    bb = room(2, 1024)
    wsp = room(8, 128)
    wst = room(8, 128)
    xs = vv[:, 0, 0:2048].rearrange("p (t n) -> p t n", t=2)
    junk = vv[:, 1, 0:1024]
    zb = room(2, 512)
    bsp = tiny(8)
    t_w = dma(G, "wsp", wsp, a["b_w_sp_2"][0].rearrange("g t s -> t g s"))
    t_bsp = dma(G, "bsp", rows[0:8, :], a["b_b_sp_2"][0])
    t_v = rms_scale(X[:, :, :], xs, junk)
    t_v = flip(xs, 8, XT, gc[:, g2 + 32:g2 + 40], t_v)
    for q in range(2):
        b = nextbank()
        PE.wait(t_w)
        for k in range(4):
            PE.put(lambda e, b=b, k=k, q=q: e.transpose(bank(b, 128, 128 * k), wsp[:, 4 * q + k, :], ident))
        to(None, b, 512, fn=lambda e, b=b, q=q: e.tensor_tensor(
            wst[:, 4 * q:4 * q + 4, :], bank(b).rearrange("p (k i) -> p k i", k=4),
            upper[:, 0, 0:128].unsqueeze(1).broadcast_to([128, 4, 128]), ALU.mult))
    b = nextbank()
    PE.wait(t_bsp)
    PE.put(lambda e, b=b: e.transpose(bank(b, 8), rows[0:8, :], ident[0:8, 0:8]))
    to(bsp, b, 8)
    fence()
    bread = [(V.sem, 0)] * 2

    def bias_piece(n, *parts):
        s = n % 2
        for k, src in enumerate(parts):
            t_p = dma(G, f"bp{s}", bb[:, s, 512 * k:512 * k + 512], src.broadcast_to([128, 512]), bread[s])
        return s, t_p

    zread = [(S.sem, 0)] * 2
    pieces = [(vv, 3072, c) for c in range(6)] + [(uu, 0, c) for c in range(6)]
    for n, (dst, base, c) in enumerate(pieces):
        s, t_p = bias_piece(n, a["b_b_in_2"][:, base + 512 * c:base + 512 * c + 512])
        bs = (nextbank(), nextbank())
        for p in range(2):
            w = part()
            for t in range(2):
                for k in range(4):
                    kk = 4 * p + k
                    use_rows(bank(bs[t]), XT, kk, t, w, k, 0, 512, kk == 0, kk == 7)
            done()
        for t in range(2):
            b = bs[t]
            tv = V.step(lambda e, b=b, t=t, s=s: e.tensor_tensor(zb[:, t, :], bank(b), bb[:, s, 0:512], ALU.add),
                        PE.mark(), t_p, zread[t])
            give(tv, b)
            zread[t] = S.step(lambda e, t=t, c=c, dst=dst: e.activation(dst[:, t, 512 * c:512 * c + 512], zb[:, t, :],
                                                                        ACT.Gelu_apprx_tanh), tv)
        bread[s] = tv
    bst = tiny(2 * 36)
    mv = tiny(4)
    for t in range(2):
        for c in range(6):
            V.step(lambda e, t=t, c=c: e.bn_stats(bst[:, 36 * t + 6 * c:36 * t + 6 * c + 6], vv[:, t, 512 * c:512 * c + 512]),
                   (S.sem, S.n))
        V.step(lambda e, t=t: e.bn_aggr(mv[:, 2 * t:2 * t + 2], bst[:, 36 * t:36 * t + 36]))
        V.step(lambda e, t=t: e.tensor_scalar(mv[:, 2 * t + 1:2 * t + 2], mv[:, 2 * t + 1:2 * t + 2], 1e-6, None, ALU.add))
        rsqrt(mv[:, 2 * t + 1:2 * t + 2], 1)
    for c in range(6):
        s, t_p = bias_piece(c, a["b_ln_g_2"][:, 512 * c:512 * c + 512], a["b_ln_b_2"][:, 512 * c:512 * c + 512])
        for t in range(2):
            vp = vv[:, t, 512 * c:512 * c + 512]
            V.step(lambda e, t=t, vp=vp: e.tensor_scalar(vp, vp, mv[:, 2 * t:2 * t + 1], mv[:, 2 * t + 1:2 * t + 2],
                                                         ALU.subtract, ALU.mult))
            V.step(lambda e, vp=vp, s=s: e.tensor_tensor(vp, vp, bb[:, s, 0:512], ALU.mult), t_p)
            bread[s] = V.step(lambda e, vp=vp, s=s: e.tensor_tensor(vp, vp, bb[:, s, 512:1024], ALU.add))
    PE.wait((V.sem, V.n))
    for t in range(2):
        for g in range(8):
            b = rbank()
            mm(bank(b, 384), wst[:, g, :], vv[:, t, 384 * g:384 * g + 384], True, True)
            up = uu[:, t, 384 * g:384 * g + 384]
            to(None, b, 384, fn=lambda e, b=b, g=g, up=up: e.scalar_tensor_tensor(
                up, bank(b, 384), bsp[:, g:g + 1], up, ALU.add, ALU.mult))
    fence()
    space["stack"].close()
    space["stack"] = ctx.enter_context(ExitStack())
    y = space["stack"].enter_context(nc.sbuf_tensor("y", [128, 2, 3072], F32))
    yT = pieces_of("yT", 24, 256)
    t_v = flip(y, 24, yT, None)
    take(4, 5, 6, 7)
    PE.wait(t_v)
    deep_sum(yT, 24)
    for t in range(2):
        for nn in range(2):
            add_to_x(t, nn, 4 + 2 * t + nn)
    fence()

    swiglu(g2 + 40)

    phase(4096)
    xs = room(2, 1024)
    junk = room(1024)
    gfin = room(1024)
    t_gf = dma(S, "gf", gfin, a["final_g_2"].rearrange("(a n) -> a n", a=1).broadcast_to([128, 1024]))
    rms_scale(X[:, :, :], xs, junk)
    for t in range(2):
        t_v = V.step(lambda e: e.tensor_tensor(xs[:, t, :], xs[:, t, :], gfin, ALU.mult), t_gf)
    t_o = dma(SP, "o", out[0].rearrange("(t p) n -> p t n", p=128), xs, t_v)
    SP.wait(t_o)
    assert at["use"] == len(parts), (at, len(parts))


_NAMES = ["x", "mem", "norm_mix", "w_in", "b_gates", "conv_w", "conv_b", "att_sinks", "norm_att_out", "norm_ml_out",
          "w_out", "norm_cross", "norm_mem", "w_cq", "w_ckv", "w_co", "norm_ffn", "w_router_group", "b_router_group",
          "w_router_expert", "b_router_expert", "w_e_gate", "w_e_up", "w_e_down", "norm_final", "norm_g_2",
          "final_g_2", "ffn_w_in_2", "ffn_w_out_2", "rel_table_2", "a_w_in_2", "a_w_out_2", "b_w_in_2", "b_b_in_2",
          "b_ln_g_2", "b_ln_b_2", "b_w_sp_2", "b_b_sp_2", "b_w_out_2"]


def kernel(**inputs):
    import concourse.bacc as _bacc
    from concourse.bass_utils import run_bass_kernel_spmd as _run

    nc = _bacc.Bacc("TRN2", target_bir_lowering=False, num_devices=1)
    cst, hot = shape_constants()
    arrays, a = {}, {}
    for name in _NAMES + ["cst", "hot"]:
        v = np.ascontiguousarray({"cst": cst, "hot": hot}[name] if name in ("cst", "hot") else inputs[name])
        arrays["in_" + name] = v
        a[name] = nc.dram_tensor("in_" + name, v.shape, mybir.dt.from_np(v.dtype), kind="ExternalInput").ap()
    out = nc.dram_tensor("out_0", (1, 256, 1024), F32, kind="ExternalOutput").ap()
    build(nc, a, out)
    r = _run(nc, [arrays], core_ids=[0])
    return r.results[0]["out_0"]
```

```python
import numpy as np
import concourse.bass as bass
from concourse import mybir
from contextlib import ExitStack

F32 = mybir.dt.float32
F32R = mybir.dt.float32r
I32 = mybir.dt.int32
ALU = mybir.AluOpType
ACT = mybir.ActivationFunctionType
AX = mybir.AxisListType

NEG = -1.0e30
NONE = 100000
GONE = -3.0e38
RING = 5
SPLIT = 3
PART = 2048
CONST_AT = {"ident": (0, 128), "upper": (128, 512), "eye": (640, 512), "causal": (1152, 512),
            "iota": (1664, 32), "ones": (1696, 128), "slot": (1824, 4), "alibi": (1828, 2048)}
CONST_W = 3876
KEPT_W = 1828


def head_at(n):
    return 2 * (n % 4) + n // 4


def shape_constants():
    p = np.arange(128)[:, None]
    s = np.arange(256)[None, :]
    c = np.zeros((128, CONST_W), np.float32)

    def put(name, a):
        o, n = CONST_AT[name]
        c[:, o:o + n] = a.reshape(128, n)

    put("ident", np.eye(128))
    put("upper", np.stack([(p + 128 * j) <= s for j in range(2)], 1).astype(np.float32))
    put("eye", np.stack([(p + 128 * j) == s for j in range(2)], 1).astype(np.float32))
    dist = p + 128 - s
    ok = (dist >= 0) & (dist < 128)
    put("alibi", np.stack([np.where(ok, -(2.0 ** -(head_at(n) + 1)) * dist, NEG) for n in range(8)], 1))
    put("causal", np.stack([np.where(s <= p + 128 * t, 0.0, NEG) for t in range(2)], 1))
    put("iota", np.broadcast_to(np.arange(32), (128, 32)))
    put("slot", 128 * np.arange(4)[None, :] + p)
    put("ones", np.ones((128, 128)))
    hot = np.zeros((32, 512), np.float32)
    for j in range(256):
        d = 255 - j
        b = d if d < 16 else min(31, 16 + int(np.log(d / 16.0) / np.log(128.0) * 16))
        hot[b, j] = 1.0
    return c, hot


class Lane:

    def __init__(self, eng, sem, live=True):
        self.eng, self.sem, self.n, self.last, self.seen, self.live = eng, sem, 0, None, {}, live

    def wait(self, *tokens):
        for sem, value in tokens:
            if value > self.seen.get(sem.name, 0):
                self.seen[sem.name] = value
                if self.live:
                    self.eng.wait_ge(sem, value)

    def mark(self):
        if self.last is not None:
            if self.live:
                self.last.then_inc(self.sem, 1)
            self.last = None
            self.n += 1
        return (self.sem, self.n)

    def put(self, fn):
        self.last = fn(self.eng) if self.live else self

    def step(self, fn, *tokens):
        self.wait((self.sem, self.n), *tokens)
        if self.live:
            fn(self.eng).then_inc(self.sem, 1)
        self.n += 1
        return (self.sem, self.n)


def build(nc, a, out):
    with ExitStack() as ctx:
        assemble(nc, a, out, ctx)


def assemble(nc, a, out, ctx):
    def sem(name):
        return ctx.enter_context(nc.semaphore(name))

    def sb(name, shape):
        return ctx.enter_context(nc.sbuf_tensor(name, shape, F32))

    PE, V, S = Lane(nc.tensor, sem("s_pe")), Lane(nc.vector, sem("s_v")), Lane(nc.scalar, sem("s_s"))
    G, SP = Lane(nc.gpsimd, sem("s_g")), Lane(nc.sync, sem("s_sp"))
    dma_count = {}

    def dma(lane, name, dst, src, *tokens):
        if name not in dma_count:
            dma_count[name] = [sem("d_" + name), 0]
        lane.wait(*tokens)
        d = dma_count[name]
        d[1] += 16
        if lane.live:
            lane.eng.dma_start(dst, src).then_inc(d[0], 16)
        return (d[0], d[1])

    def dma_of(lane, name, fn, *tokens):
        if name not in dma_count:
            dma_count[name] = [sem("d_" + name), 0]
        lane.wait(*tokens)
        d = dma_count[name]
        d[1] += 16
        if lane.live:
            fn(lane.eng).then_inc(d[0], 16)
        return (d[0], d[1])

    def fence(*tokens):
        marks = [(V.sem, V.n), (S.sem, S.n), (G.sem, G.n), PE.mark()]
        for lane in (PE, V, S, G):
            lane.wait(*marks, *tokens)
        return marks

    cst = sb("cst", [128, KEPT_W])
    gc = sb("gc", [128, 128])
    rows = sb("rows", [128, 128])
    X = sb("X", [128, 2, 1024])
    xtmp = sb("xtmp", [128, 2, 512])
    small = sb("small", [128, 512])
    ring = sb("ring", [128, RING, PART])
    XTh = ctx.enter_context(nc.sbuf_tensor("XTh", [128, 8, 256], F32R))
    XTl = ctx.enter_context(nc.sbuf_tensor("XTl", [128, 8, 256], F32R))
    XT = (XTh, XTl)
    wh = ctx.enter_context(nc.sbuf_tensor("wh", [128, SPLIT, PART], F32R))
    wl = ctx.enter_context(nc.sbuf_tensor("wl", [128, SPLIT, PART], F32R))
    PS = ctx.enter_context(nc.psum_tensor("PS", [128, 4096], F32))
    lists = nc.dram_tensor("lists", (8192, 1), I32, kind="Internal").ap()
    xn_d = nc.dram_tensor("xn_d", (256, 1024), F32, kind="Internal").ap()
    y_d = nc.dram_tensor("y_d", (512, 1024), F32, kind="Internal").ap()
    toep = nc.dram_tensor("toep", (8, 128, 512), F32, kind="Internal").ap()

    def C(name):
        o, n = CONST_AT[name]
        return cst[:, o:o + n]

    ident = C("ident")
    upper = C("upper").rearrange("p (j s) -> p j s", j=2)
    eye = C("eye").rearrange("p (j s) -> p j s", j=2)
    causal = C("causal").rearrange("p (t s) -> p t s", t=2)
    iota = C("iota")
    ones = C("ones")

    space = {"stack": None, "count": 0}

    def phase(words):
        if space["stack"] is not None:
            space["stack"].close()
        space["stack"] = ctx.enter_context(ExitStack())
        space["count"] += 1
        space["arena"] = space["stack"].enter_context(nc.sbuf_tensor(f"arena{space['count']}", [128, words], F32))
        space["words"] = words
        space["at"] = 0

    def pieces_of(name, *dims):
        return [space["stack"].enter_context(nc.sbuf_tensor(f"{name}{x}{space['count']}", [128, *dims], F32R))
                for x in "hl"]

    def shaped(v, dims):
        if len(dims) == 2:
            v = v.rearrange("p (a b) -> p a b", a=dims[0])
        if len(dims) == 3:
            v = v.rearrange("p (a b c) -> p a b c", a=dims[0], b=dims[1])
        return v

    def room_at(o, *dims):
        n = 1
        for d in dims:
            n *= d
        assert o + n <= space["words"], (o + n, space["words"])
        return shaped(space["arena"][:, o:o + n], dims)

    def room(*dims):
        v = room_at(space["at"], *dims)
        n = 1
        for d in dims:
            n *= d
        space["at"] += n
        return v

    used = [0]

    def tiny(n):
        o = used[0]
        used[0] += n
        assert used[0] <= 512, used[0]
        return small[:, o:o + n]

    rel = [(PE.sem, 0)] * 8

    def bank(b, n=512, o=0):
        return PS[:, b * 512 + o:b * 512 + o + n]

    def take(*banks):
        for b in banks:
            PE.wait(rel[b])

    def give(token, *banks):
        for b in banks:
            rel[b] = token

    parts = []

    def cols(w, c0, c1):
        r = w.rearrange("(k p) n -> p k n", p=128)
        for k in (0, 4):
            parts.append((4, c1 - c0, [(0, c1 - c0, r[:, k:k + 4, c0:c1])]))

    def pair(w, c0, u0, n):
        r = w.rearrange("(k p) n -> p k n", p=128)
        for k in (0, 4):
            parts.append((4, 2 * n, [(0, n, r[:, k:k + 4, c0:c0 + n]), (n, 2 * n, r[:, k:k + 4, u0:u0 + n])]))

    def deep(w, r0, nk):
        for k in range(0, nk, 2):
            src = w[r0 + 128 * k:r0 + 128 * k + 256, :].rearrange("(k p) n -> p k n", p=128)
            parts.append((2, 1024, [(0, 1024, src)]))

    w_in = a["w_in"][0]
    cols(a["w_ckv"][0], 0, 512)
    cols(a["w_ckv"][0], 512, 1024)
    for c in (0, 512, 2560, 1024, 1536, 2048):
        cols(w_in, c, min(c + 512, 2824))
    for k in (0, 4):
        for c in (0, 512):
            r = a["w_out"][0].rearrange("(k p) n -> p k n", p=128)
            parts.append((4, 512, [(0, 512, r[:, k:k + 4, c:c + 512])]))
    cols(a["w_cq"][0], 0, 512)
    deep(a["w_co"][0], 0, 4)
    for e in range(32):
        cols(a["w_e_gate"][0, e], 0, 512)
        if e:
            deep(a["w_e_down"][0, e - 1], 0, 4)
        cols(a["w_e_up"][0, e], 0, 512)
    deep(a["w_e_down"][0, 31], 0, 4)

    def ffn_units(i, j):
        for c in range(11):
            pair(a["ffn_w_in_2"][i, j], 256 * c, 2816 + 256 * c, 256)
        for c in range(6):
            deep(a["ffn_w_out_2"][i, j], 512 * c, min(4, 22 - 4 * c))

    ffn_units(0, 0)
    for c in (3072, 3584, 0, 512, 1024, 1536, 2048, 2560):
        cols(a["a_w_in_2"][0], c, min(c + 512, 3656))
    cols(a["a_w_out_2"][0], 0, 512)
    cols(a["a_w_out_2"][0], 512, 1024)
    ffn_units(0, 1)
    ffn_units(1, 0)
    for c in range(6):
        cols(a["b_w_in_2"][0], 3072 + 512 * c, 3584 + 512 * c)
    for c in range(6):
        cols(a["b_w_in_2"][0], 512 * c, 512 * c + 512)
    for c in range(6):
        deep(a["b_w_out_2"][0], 512 * c, 4)
    ffn_units(1, 1)

    loaded, ready, at = {}, {}, {"load": 0, "split": 0, "use": 0}
    buffers = [(wh[:, i, :], wl[:, i, :]) for i in range(SPLIT)]
    held, retired = {}, []
    late = {}

    def load_part(*tokens):
        i = at["load"]
        if i < len(parts):
            at["load"] += 1
            nk, w, srcs = parts[i]
            for c0, c1, src in srcs:
                dst = ring[:, i % RING, 0:nk * w].rearrange("p (k n) -> p k n", n=w)[:, :, c0:c1]
                loaded[i] = dma(SP, f"w{i % RING}", dst, src, *tokens)

    def split_part(buf, *tokens):
        i = at["split"]
        if i < len(parts):
            at["split"] += 1
            n = parts[i][0] * parts[i][1]
            held[i] = buf
            raw, h, l = ring[:, i % RING, 0:n], buf[0][:, 0:n], buf[1][:, 0:n]
            t_s = S.step(lambda e: e.activation(h, raw, ACT.Copy), loaded[i], *tokens)
            ready[i] = V.step(lambda e: e.tensor_tensor(l, raw, h.bitcast(F32), ALU.subtract), t_s)
            load_part(ready[i])

    def part():
        i = at["use"]
        at["use"] += 1
        nk, w, _ = parts[i]
        PE.wait(ready[i], *late.pop(i, ()))
        return [x[:, 0:nk * w].rearrange("p (k n) -> p k n", n=w) for x in held[i]]

    def done(first=None):
        buf = held.pop(at["use"] - 1)
        read = PE.mark()
        res = first() if first else None
        if not any(buf is x for x in retired):
            split_part(buf, read)
        return res

    phase(20300)
    mem = room(2, 1024)
    alibi_flat = room(2048)
    alibi = alibi_flat.rearrange("p (h s) -> p h s", h=8)
    t_mem = dma(SP, "m", mem, a["mem"][0].rearrange("(t p) n -> p t n", p=128))
    t_c = dma(SP, "c", cst[:, :], a["cst"][:, 0:KEPT_W])
    GAIN = {}
    row_at = 0
    t_r = None
    for name, src, n in (("mix", a["norm_mix"][0], 8), ("att", a["norm_att_out"][0], 4),
                         ("ml", a["norm_ml_out"][0], 4), ("cross", a["norm_cross"][0], 8),
                         ("mem", a["norm_mem"][0], 8), ("ffn", a["norm_ffn"][0], 8),
                         ("convb", a["conv_b"][0], 8)):
        t_r = dma(S, "r", rows[row_at:row_at + n, :], src.rearrange("(k p) -> k p", p=128))
        GAIN[name] = row_at
        row_at += n
    t_r = dma(S, "r", rows[row_at:row_at + 32, :], a["conv_w"][0].rearrange("w (k p) -> (w k) p", p=128))
    GAIN["convw"] = row_at
    row_at += 32
    t_r = dma(S, "r", rows[row_at:row_at + 48, :], a["norm_g_2"].rearrange("i j (k p) -> (i j k) p", p=128))
    GAIN["g2"] = row_at
    row_at += 48
    assert row_at == 128
    load_part(t_r)
    load_part()
    t_x = dma(SP, "x", X[:, :, :], a["x"][0].rearrange("(t p) n -> p t n", p=128))
    for _ in range(RING - 2):
        load_part()

    sink = tiny(8)
    bgate = tiny(8)
    brout = tiny(36)
    sink_in = tiny(8)
    t_b = dma(S, "b", sink_in, a["att_sinks"].broadcast_to([128, 8]))
    t_b = dma(S, "b", bgate, a["b_gates"].broadcast_to([128, 8]))
    t_b = dma(S, "b", brout[:, 0:4], a["b_router_group"].broadcast_to([128, 4]))
    t_b = dma(S, "b", brout[:, 4:36], a["b_router_expert"].broadcast_to([128, 32]))
    t_b = dma(S, "b", alibi_flat, a["cst"][:, KEPT_W:CONST_W])
    hot = room_at(15000, 512)[0:32, :]
    frow = room_at(16000, 512)[0:8, :]
    rtab = tiny(8)
    t_b = dma(S, "b", hot, a["hot"])
    t_b = dma(S, "b", rtab[0:32, :], a["rel_table_2"])

    PE.wait(t_c, t_r)
    PE.put(lambda e: e.transpose(bank(7, 128), rows[:, :], ident))
    t_gc = V.step(lambda e: e.tensor_copy(gc[:, :], bank(7, 128)), PE.mark())
    give(t_gc, 7)

    def col(name, k=0, n=1):
        o = GAIN[name] + k
        return gc[:, o:o + n]

    mhalf = tiny(8)
    V.step(lambda e: e.memset(mhalf, -0.5))

    def rsqrt(x, n):
        t_g = G.step(lambda e: e.tensor_tensor(x, x, mhalf[:, 0:n], ALU.pow), (V.sem, V.n))
        V.wait(t_g)

    ss = tiny(2)
    rstd = tiny(2)

    def rms_scale(src, dst, junk, *tokens, width=1024):
        for t in range(2):
            t_ss = S.step(lambda e, t=t: e.activation(junk[:, 0:width], src[:, t, :], ACT.Square,
                                                      accum_out=ss[:, t:t + 1]), *tokens)
        V.step(lambda e: e.tensor_scalar(rstd, ss, 1.0 / width, 1e-6, ALU.mult, ALU.add), t_ss, *tokens)
        rsqrt(rstd, 2)
        for t in range(2):
            t_v = V.step(lambda e, t=t: e.tensor_scalar(dst[:, t, :], src[:, t, :], rstd[:, t:t + 1], None, ALU.mult))
        return t_v

    def cut(dst, src, n):
        h, l = dst
        t_s = S.step(lambda e: e.activation(h, src, ACT.Copy), n)
        return V.step(lambda e: e.tensor_tensor(l, src, h.bitcast(F32), ALU.subtract), t_s)

    def flip(src, nk, dst, gain, *tokens, banks=(0, 1, 2, 3)):
        PE.wait(*tokens)
        t_v, subtract = None, None
        for n, (k0, t) in enumerate([(k0, t) for k0 in range(0, nk, 4) for t in range(2)]):
            b = banks[n % len(banks)]
            m = min(4, nk - k0)
            take(b)
            for k in range(m):
                PE.put(lambda e: e.transpose(
                    bank(b, 128, 128 * k), src[:, t, 128 * (k0 + k):128 * (k0 + k + 1)], ident))
            view = bank(b, 128 * m).rearrange("p (k i) -> p k i", k=m)
            h, l = [x[:, k0:k0 + m, 128 * t:128 * t + 128] for x in dst]
            if gain is None:
                t_v = cut((h, l), view, PE.mark())
                give(t_v, b)
            else:
                g = gain[:, k0:k0 + m].unsqueeze(2).broadcast_to([128, m, 128])
                tmp = xtmp[:, n % 2, 0:128 * m].rearrange("p (k i) -> p k i", k=m)
                t_m = V.step(lambda e: e.tensor_tensor(tmp, view, g, ALU.mult), PE.mark())
                give(t_m, b)
                if subtract:
                    t_v = V.step(*subtract)
                t_s = S.step(lambda e: e.activation(h, tmp, ACT.Copy), t_m)
                subtract = (lambda e, l=l, h=h, tmp=tmp: e.tensor_tensor(l, tmp, h.bitcast(F32), ALU.subtract), t_s)
            if n == 2:
                half[0] = t_v
        if subtract:
            t_v = V.step(*subtract)
        return t_v

    half = [None]

    def start_rows(t_v):
        PE.wait(half[0])
        late[at["use"] + 1] = (t_v,)

    def mm(o, l, r, first, last):
        PE.put(lambda e: e.matmul(o, lhsT=l, rhs=r, start=first, stop=last))

    def mm3(o, lh, ll, rh, rl, first, last):
        mm(o, lh, rh, first, False)
        mm(o, lh, rl, False, False)
        mm(o, ll, rh, False, last)

    def use_rows(o, xt, kx, t, w, kw, c0, c1, first, last):
        xs_ = [x[:, kx, 128 * t:128 * t + 128] for x in xt]
        ws_ = [x[:, kw, c0:c1] for x in w]
        mm3(o, xs_[0], xs_[1], ws_[0], ws_[1], first, last)

    def rows_job(t, c0, c1, dst=None, fn=None):
        return ("rows", t, c0, c1, dst, fn)

    def cols_job(c0, dst, m=128, keep=128):
        return ("cols", c0, m, keep, dst, None)

    def project(xt, jobs, nparts=2):
        banks = [nextbank() for _ in jobs]
        for p in range(nparts):
            w = part()
            for b, job in zip(banks, jobs):
                for k in range(4):
                    kk, last = 4 * p + k, 4 * nparts - 1
                    if job[0] == "rows":
                        _, t, c0, c1, _, _ = job
                        use_rows(bank(b, c1 - c0), xt, kk, t, w, k, c0, c1, kk == 0, kk == last)
                    else:
                        _, c0, m, _, _, _ = job
                        o = PS[0:m, b * 512:b * 512 + 256]
                        mm3(o, w[0][:, k, c0:c0 + m], w[1][:, k, c0:c0 + m], xt[0][:, kk, :], xt[1][:, kk, :],
                            kk == 0, kk == last)
            done()
            if between and p < nparts - 1:
                run_stages()
        for b, job in zip(banks, jobs):
            if job[0] == "rows":
                n, dst, fn = job[3] - job[2], job[4], job[5]
                give(V.step((lambda e: fn(e, b)) if fn else (lambda e: e.tensor_copy(dst, bank(b, n))), PE.mark()), b)
            else:
                q, dst = job[3], job[4]
                give(V.step(lambda e: e.tensor_copy(dst, PS[0:q, b * 512:b * 512 + 256]), PE.mark()), b)

        if between:
            run_stages()

    def bc(x, n, m):
        return x.unsqueeze(2).broadcast_to([128, n, m])

    xs = room(2, 1024)
    junk = room(1024)
    qT = room(4, 256)
    kT = room(256)
    kT2 = room(256)
    va = room(2, 128)
    qkT = room(8, 260)
    vm = room(2, 512)
    om = room(2, 512)
    gr = room(2, 8)
    mark_a = space["at"]
    kcT = room_at(mark_a + 5120, 4, 256)
    vc = room_at(mark_a + 6144, 2, 512)
    V.step(lambda e: e.memset(qkT[:, :, 0:4], 0.0))

    rot = [0]
    rotate = [0, 1, 2, 3, 4, 5, 6, 7]
    between = []

    def run_stages():
        for stage in between.pop(0):
            stage()

    def nextbank():
        b = rotate[rot[0] % len(rotate)]
        rot[0] += 1
        take(b)
        return b

    def to(dst, b, n, o=0, fn=None):
        t = V.step(fn or (lambda e: e.tensor_copy(dst, bank(b, n, o))), PE.mark())
        give(t, b)
        return t

    t_v = rms_scale(mem, xs, junk, t_mem)
    t_mt = flip(xs, 8, XT, col("mem", 0, 8), t_v)
    for buf in buffers:
        split_part(buf)
    t_v = rms_scale(X[:, :, :], xs, junk, t_x, t_mt)
    PE.wait(t_mt)
    project(XT, [cols_job(128 * c, kcT[:, c, :]) for c in range(4)])
    project(XT, [rows_job(t, 0, 512, vc[:, t, :]) for t in range(2)])
    for o in range(2):
        V.step(lambda e: e.tensor_copy(sink[:, 4 * o:4 * o + 4],
                                       sink_in.rearrange("p (x o) -> p o x", o=2)[:, o, :]), t_b)
    PE.wait(t_b)
    take(7)
    PE.put(lambda e: e.matmul(PS[0:8, 3584:4096], lhsT=rtab[0:32, :], rhs=hot, start=True, stop=True))
    t_f = S.step(lambda e: e.activation(frow, PS[0:8, 3584:4096], ACT.Copy), PE.mark())
    give(t_f, 7)
    t_toep = dma(G, "toep", toep, frow.unsqueeze(1).broadcast_to([8, 128, 512]), t_f)
    V.wait(PE.mark())
    S.wait(PE.mark())
    t_xt = flip(xs, 8, XT, col("mix", 0, 8), t_v)
    start_rows(t_xt)
    project(XT, [cols_job(128 * c, qT[:, c, :]) for c in range(4)])
    project(XT, [cols_job(0, kT)] + [rows_job(t, 128, 256, va[:, t, :]) for t in range(2)]
            + [cols_job(256 + 128 * c, qkT[:, c, 4:260]) for c in range(2)])
    t_k2 = dma(G, "k2", kT2[0:64, :], kT[64:128, :], (V.sem, V.n))
    t_k2 = dma(G, "k2", kT2[64:128, :], kT[0:64, :])
    L1 = room_at(0, 8, 256)
    L0 = room(8, 128)
    att = room_at(mark_a, 2, 512)
    pT = room(16, 128)
    R = room(2, 4, 256)
    assert space["at"] <= mark_a + 5120
    cv = room_at(4096, 8, 256)
    mx = tiny(16)
    dn = tiny(16)
    esk = tiny(16)
    LL = (L0, L1)
    SC = [PS[:, 0:1024 * (t + 1)].rearrange("p (h s) -> p h s", h=8) for t in range(2)]
    AB = (alibi[:, :, 128:256], alibi)
    t_qk = (V.sem, V.n)

    def scores(t):
        w1 = 128 * (t + 1)
        take(*range(2 * (t + 1)))
        PE.wait(t_qk, t_k2)
        for n in range(8):
            h = head_at(n)
            lo = 64 * (h % 2)
            kk = kT if (h // 4) == (h % 2) else kT2
            mm(PS[:, w1 * n:w1 * n + w1], qT[lo:lo + 64, h // 2, 128 * t:128 * t + 128], kk[lo:lo + 64, 0:w1], True, True)
        m8, e8, d8 = [x[:, 8 * t:8 * t + 8] for x in (mx, esk, dn)]
        t_v = V.step(lambda e: e.scalar_tensor_tensor(LL[t], SC[t], 0.125, AB[t], ALU.mult, ALU.add), PE.mark())
        give(t_v, *range(2 * (t + 1)))
        V.step(lambda e: e.tensor_reduce(m8, LL[t], AX.X, ALU.max))
        V.step(lambda e: e.tensor_tensor(m8, m8, sink, ALU.max))
        V.step(lambda e: e.tensor_tensor(e8, sink, m8, ALU.subtract))
        t_v = V.step(lambda e: e.tensor_tensor(LL[t], LL[t], bc(m8, 8, w1), ALU.subtract))
        S.step(lambda e: e.activation(LL[t], LL[t], ACT.Exp), t_v)
        return S.step(lambda e: e.activation(e8, e8, ACT.Exp))

    def weights(t, t_s):
        e8, d8 = esk[:, 8 * t:8 * t + 8], dn[:, 8 * t:8 * t + 8]
        PE.wait(t_s)
        n = 0
        V.wait(t_toep)
        for h in range(8):
            for j in range(t + 1):
                b = (2, 3)[n // 4] if t == 0 else n // 4
                if n % 4 == 0:
                    take(b)
                PE.put(lambda e: e.transpose(bank(b, 128, 128 * (n % 4)), LL[t][:, h, 128 * j:128 * j + 128], ident))
                n += 1
                if n % 4 == 0:
                    t_p = V.step(lambda e: e.tensor_copy(pT[:, n - 4:n, :].rearrange("p a b -> p (a b)"), bank(b)),
                                 PE.mark())
                    give(t_p, b)
        V.step(lambda e: e.tensor_reduce(d8, LL[t], AX.X, ALU.add))
        V.step(lambda e: e.tensor_tensor(d8, d8, e8, ALU.add))
        V.step(lambda e: e.reciprocal(d8, d8))
        return t_p

    def values(t, t_p):
        take(0)
        PE.wait(t_p)
        n = 0
        for m in range(8):
            kv = 64 * (head_at(m) // 4)
            for j in range(t + 1):
                mm(bank(0, 64, 64 * m), pT[:, n, :], va[:, j, kv:kv + 64], j == 0, j == t)
                n += 1
        for o in range(2):
            t_v = V.step(lambda e: e.tensor_tensor(att[:, t, :].rearrange("p (x o d) -> p x o d", o=2, d=64)[:, :, o, :],
                                                   bank(0, 256, 256 * o).rearrange("p (h d) -> p h d", h=4),
                                                   bc(dn[:, 8 * t + 4 * o:8 * t + 4 * o + 4], 4, 64), ALU.mult),
                         PE.mark())
        give(t_v, 0)

    lf = tiny(16)
    gi = tiny(16)
    ga = tiny(16)
    gi3 = gi.rearrange("p (t g) -> p t g", t=2)
    ipre = gi3[:, :, 0:4]
    fpre = gi3[:, :, 4:8]
    lf3 = lf[:, 0:8].rearrange("p (t g) -> p t g", t=2)
    nlf = lf[:, 8:16].rearrange("p (t g) -> p t g", t=2)
    ga3 = ga[:, 0:8].rearrange("p (t g) -> p t g", t=2)

    def conv(*chunks):
        for c in chunks:
            V.step(lambda e: e.tensor_scalar(cv[:, c, :], qkT[:, c, 1:257], col("convw", c), col("convb", c),
                                             ALU.mult, ALU.add))
            for j in range(1, 4):
                V.step(lambda e: e.scalar_tensor_tensor(cv[:, c, :], qkT[:, c, 1 + j:257 + j],
                                                        col("convw", 8 * j + c), cv[:, c, :], ALU.mult, ALU.add))

    def gates_of():
        for t in range(2):
            t_v = V.step(lambda e: e.tensor_tensor(gi[:, 8 * t:8 * t + 8], gr[:, t, :], bgate, ALU.add))
        t_v = V.step(lambda e: e.scalar_tensor_tensor(ga3, fpre, -1.0, fpre, ALU.mult, ALU.max))
        S.step(lambda e: e.activation(ga3, ga3, ACT.Exp, scale=-1.0), t_v)
        return S.step(lambda e: e.activation(ga3, ga3, ACT.Ln, bias=1.0))

    def decays(t_s):
        V.step(lambda e: e.tensor_scalar(lf3, fpre, 0.0, None, ALU.min))
        V.step(lambda e: e.tensor_tensor(lf3, lf3, ga3, ALU.subtract), t_s)
        V.step(lambda e: e.tensor_scalar(nlf, lf3, -1.0, None, ALU.mult))
        G.wait((V.sem, V.n))
        by_head = junk.rearrange("p (h s) -> p h s", h=4)
        for j in range(2):
            G.step(lambda e: e.tensor_tensor(R[:, j], eye[:, j, :].unsqueeze(1).broadcast_to([128, 4, 256]),
                                             bc(ipre[:, j, :], 4, 256), ALU.mult))
            G.step(lambda e: e.tensor_tensor(by_head, upper[:, j, :].unsqueeze(1).broadcast_to([128, 4, 256]),
                                             bc(nlf[:, j, :], 4, 256), ALU.mult))
            t_g = G.step(lambda e: e.tensor_tensor(R[:, j], R[:, j], by_head, ALU.add))
        return t_g

    tok = {}

    def keep(name, fn):
        def stage():
            tok[name] = fn()
        return stage

    rotate[:] = [4, 5, 6, 7]
    between += [
        [keep("s0", lambda: scores(0))],
        [keep("g", gates_of), lambda: conv(0, 1)],
        [keep("p0", lambda: weights(0, tok["s0"]))],
        [lambda: values(0, tok["p0"]), keep("r", lambda: decays(tok["g"]))],
        [keep("s1", lambda: scores(1)), lambda: conv(2, 3)],
        [lambda: conv(4, 5)],
        [keep("p1", lambda: weights(1, tok["s1"])), lambda: conv(6, 7),
         keep("cv", lambda: S.step(lambda e: e.activation(cv, cv, ACT.Silu), (V.sem, V.n)))],
        [lambda: values(1, tok["p1"])],
    ]
    project(XT, [rows_job(t, 0, 256, om[:, t, 256:512]) for t in range(2)]
            + [rows_job(t, 256, 264, gr[:, t, :]) for t in range(2)])
    project(XT, [cols_job(128 * c, qkT[:, 2 + c, 4:260]) for c in range(4)])
    project(XT, [cols_job(128 * c, qkT[:, 6 + c, 4:260]) for c in range(2)]
            + [rows_job(t, 256, 512, vm[:, t, 0:256]) for t in range(2)])
    project(XT, [rows_job(t, 0, 256, vm[:, t, 256:512]) for t in range(2)]
            + [rows_job(t, 256, 512, om[:, t, 0:256]) for t in range(2)])
    assert not between
    rotate[:] = list(range(8))

    AM0 = room_at(1024, 4, 128)
    AM1 = room_at(0, 4, 256)
    sT = pT[:, 0:12, :]
    hm = room_at(2048, 2, 512)
    take(0, 1, 2, 3, 4, 5)
    PE.wait((V.sem, V.n), tok["r"], tok["cv"])
    for hh in range(2):
        for j in range(2):
            mm(bank(hh), ones, R[:, j, 2 * hh:2 * hh + 2, :].rearrange("p a b -> p (a b)"), j == 0, j == 1)
    for t in range(2):
        for j in range(t + 1):
            mm(bank(2, 4, 4 * t), upper[:, j, 128 * t:128 * t + 128], lf3[:, j, :], j == 0, j == t)
    t_a = PE.mark()
    for h in range(4):
        mm(bank(3, 128, 128 * h), cv[:, h, 0:128], cv[:, 4 + h, 0:128], True, True)
    for h in range(4):
        mm(PS[:, 2048 + 256 * h:2048 + 256 * h + 256], cv[:, h, 128:256], cv[:, 4 + h, :], True, True)
    t_q = PE.mark()
    t_v = rms_scale(att, att, junk, (V.sem, V.n), tok["r"], width=512)
    t_v = flip(att, 4, XT, col("att", 0, 4), t_v, banks=(6, 7))
    OUT = (6, 4)

    def out_half(nn):
        take(OUT[nn], OUT[nn] + 1)
        w = part()
        for t in range(2):
            for k in range(4):
                use_rows(bank(OUT[nn] + t), XT, k, t, w, k, 0, 512, k == 0, False)
        done()

    PE.wait(t_v)
    out_half(0)
    A3 = PS[:, 0:1024].rearrange("p (h s) -> p h s", h=4)
    QK = (bank(3).rearrange("p (h s) -> p h s", h=4), PS[:, 2048:3072].rearrange("p (h s) -> p h s", h=4))
    AM = (AM0, AM1)
    M = tiny(8)
    em = tiny(8)
    m4, e4, d4 = [[x[:, 4 * t:4 * t + 4] for t in range(2)] for x in (M, em, dn)]
    W = (128, 256)
    T = range(2)
    for t in T:
        t_v = V.step(lambda e: e.tensor_tensor(AM[t], A3[:, :, 0:W[t]],
                                               causal[:, t, 0:W[t]].unsqueeze(1).broadcast_to([128, 4, W[t]]), ALU.add),
                     t_a)
    give(t_v, 0, 1)
    for t in T:
        V.step(lambda e: e.tensor_reduce(m4[t], AM[t], AX.X, ALU.max))
        V.step(lambda e: e.tensor_scalar(m4[t], m4[t], 0.0, None, ALU.max))
        V.step(lambda e: e.tensor_tensor(AM[t], AM[t], bc(m4[t], 4, W[t]), ALU.subtract))
        t_v = V.step(lambda e: e.tensor_tensor(e4[t], bank(2, 4, 4 * t), m4[t], ALU.add))
        S.step(lambda e: e.activation(AM[t], AM[t], ACT.Exp), t_v)
        tok[("e", t)] = S.step(lambda e: e.activation(e4[t], e4[t], ACT.Exp, scale=-1.0))
    give(t_v, 2)
    t_s = S.step(lambda e: e.activation(om, om, ACT.Tanh, scale=0.5))
    n = 0
    for t in T:
        t_v = V.step(lambda e: e.scalar_tensor_tensor(AM[t], QK[t], 128 ** -0.5, AM[t], ALU.mult, ALU.mult),
                     tok[("e", t)], t_q)
        give(t_v, *((3,), (4, 5))[t])
        PE.wait(t_v)
        for h in range(4):
            for j in range(t + 1):
                b = n // 4
                if n % 4 == 0:
                    take(b)
                PE.put(lambda e: e.transpose(bank(b, 128, 128 * (n % 4)), AM[t][:, h, 128 * j:128 * j + 128], ident))
                n += 1
                if n % 4 == 0:
                    t_p = V.step(lambda e: e.tensor_copy(sT[:, n - 4:n, :].rearrange("p a b -> p (a b)"), bank(b)),
                                 PE.mark())
                    give(t_p, b)
        tok[("p", t)] = t_p
    out_half(1)
    n = 0
    for t in T:
        b = (3, 0)[t]
        take(b)
        PE.wait(tok[("p", t)])
        for h in range(4):
            for j in range(t + 1):
                mm(bank(b, 128, 128 * h), sT[:, n, :], vm[:, j, 128 * h:128 * h + 128], j == 0, j == t)
                n += 1
        tok[("h", t)] = PE.mark()
    V.step(lambda e: e.tensor_scalar(om, om, 0.5, 0.5, ALU.mult, ALU.add), t_s)
    for t in T:
        V.step(lambda e: e.tensor_reduce(d4[t], AM[t], AX.X, ALU.add))
        V.step(lambda e: e.scalar_tensor_tensor(d4[t], d4[t], -1.0, d4[t], ALU.mult, ALU.max))
        V.step(lambda e: e.tensor_tensor(d4[t], d4[t], e4[t], ALU.max))
        V.step(lambda e: e.reciprocal(d4[t], d4[t]))
    sq = tiny(8)
    jv = junk.rearrange("p (t h d) -> p t h d", t=2, h=4)
    for t in T:
        hv = hm[:, t, :].rearrange("p (h d) -> p h d", h=4)
        t_v = V.step(lambda e: e.tensor_tensor(hv, bank((3, 0)[t]).rearrange("p (h d) -> p h d", h=4),
                                               bc(d4[t], 4, 128), ALU.mult), tok[("h", t)])
        give(t_v, (3, 0)[t])
        V.step(lambda e: e.tensor_tensor(hm[:, t, :], hm[:, t, :], om[:, t, :], ALU.mult))
        V.step(lambda e: e.tensor_tensor(jv[:, t], hv, hv, ALU.mult))
        V.step(lambda e: e.tensor_reduce(sq[:, 4 * t:4 * t + 4], jv[:, t], AX.X, ALU.add))
    V.step(lambda e: e.tensor_scalar(sq, sq, 1.0 / 128, 1e-6, ALU.mult, ALU.add))
    rsqrt(sq, 8)
    for t in T:
        hv = hm[:, t, :].rearrange("p (h d) -> p h d", h=4)
        t_v = V.step(lambda e: e.tensor_tensor(hv, hv, bc(sq[:, 4 * t:4 * t + 4], 4, 128), ALU.mult))
    t_v = flip(hm, 4, [x[:, 4:8, :] for x in XT], col("ml", 0, 4), t_v)
    PE.wait(t_v)

    def add_to_x(t, nn, b, scale=None):
        xv = X[:, t, 512 * nn:512 * nn + 512]
        if scale is None:
            return to(None, b, 512, fn=lambda e: e.tensor_tensor(xv, bank(b), xv, ALU.add))
        return to(None, b, 512, fn=lambda e: e.scalar_tensor_tensor(xv, bank(b), scale, xv, ALU.mult, ALU.add))

    def add_out():
        for nn in range(2):
            def plus(t):
                xv = X[:, t, 512 * nn:512 * nn + 512]
                return lambda e, b: e.tensor_tensor(xv, bank(b), xv, ALU.add)
            project(XT, [rows_job(t, 0, 512, fn=plus(t)) for t in range(2)])

    def deep_sum(xt, nk, last_rows=None):
        for p in range(nk // 2):
            w = part()
            if p == nk // 2 - 1 and last_rows:
                PE.wait(t_last)
            for t in range(2):
                for nn in range(2):
                    for k in range(2):
                        kk = 2 * p + k
                        use_rows(bank(4 + 2 * t + nn), xt, kk, t, w, k, 512 * nn, 512 * nn + 512, kk == 0, kk == nk - 1)
            done()
            if p == 0 and last_rows:
                t_last = last_rows()

    give((V.sem, V.n), 0, 1, 2, 3)
    for nn in range(2):
        w = part()
        for t in range(2):
            for k in range(4):
                use_rows(bank(OUT[nn] + t), XT, 4 + k, t, w, k, 0, 512, False, k == 3)
        done()
        for t in range(2):
            add_to_x(t, nn, OUT[nn] + t)
    fence()

    xs = room_at(0, 2, 1024)
    junk = room_at(2048, 1024)
    space["at"] = mark_a
    Lc = room(2, 4, 256)
    pcT = room(2, 8, 128)
    qcT = room(4, 256)
    assert space["at"] <= mark_a + 5120
    t_v = rms_scale(X[:, :, :], xs, junk)
    t_v = flip(xs, 8, XT, col("cross", 0, 8), t_v)
    start_rows(t_v)
    project(XT, [cols_job(128 * c, qcT[:, c, :]) for c in range(4)])
    fence()
    sc3, m4, d4, t_x = {}, {}, {}, {}
    for t in T:
        for h in range(4):
            mm(PS[:, 1024 * t + 256 * h:1024 * t + 256 * h + 256], qcT[:, h, 128 * t:128 * t + 128], kcT[:, h, :],
               True, True)
        sc3[t] = PS[:, 1024 * t:1024 * t + 1024].rearrange("p (h s) -> p h s", h=4)
        m4[t], d4[t] = mx[:, 4 * t:4 * t + 4], dn[:, 4 * t:4 * t + 4]
        V.step(lambda e: e.tensor_reduce(m4[t], sc3[t], AX.X, ALU.max), PE.mark())
        t_v = V.step(lambda e: e.tensor_tensor(Lc[:, t], sc3[t], bc(m4[t], 4, 256), ALU.subtract))
        t_x[t] = S.step(lambda e: e.activation(Lc[:, t], Lc[:, t], ACT.Exp, scale=128 ** -0.5), t_v)
    for t in T:
        V.step(lambda e: e.tensor_reduce(d4[t], Lc[:, t], AX.X, ALU.add), t_x[t])
        V.step(lambda e: e.reciprocal(d4[t], d4[t]))
        t_v = V.step(lambda e: e.tensor_tensor(Lc[:, t], Lc[:, t], bc(d4[t], 4, 256), ALU.mult))
        PE.wait(t_v)
        for n in range(8):
            PE.put(lambda e: e.transpose(PS[:, 2048 + 1024 * t + 128 * n:2176 + 1024 * t + 128 * n],
                                         Lc[:, t, n // 2, 128 * (n % 2):128 * (n % 2) + 128], ident))
        t_x[t] = S.step(lambda e: e.activation(pcT[:, t].rearrange("p a b -> p (a b)"),
                                               PS[:, 2048 + 1024 * t:3072 + 1024 * t], ACT.Copy), PE.mark())
    for t in T:
        PE.wait(t_x[t])
        for h in range(4):
            for j in range(2):
                mm(bank(t, 128, 128 * h), vc[:, j, 128 * h:128 * h + 128], pcT[:, t, 2 * h + j, :], j == 0, j == 1)
        cut([x[:, 0:4, 128 * t:128 * t + 128] for x in XT], bank(t).rearrange("p (h s) -> p h s", h=4), PE.mark())
    fence()
    deep_sum(XT, 4)
    for t in range(2):
        for nn in range(2):
            add_to_x(t, nn, 4 + 2 * t + nn)
    fence()

    phase(9952)
    W0 = room_at(0, 4096)
    xs = room(2, 1024)
    junk = room(1024)
    gffn = room(1024)
    gfin = room(1024)
    t_gf = dma(S, "gf", gfin, a["norm_final"].rearrange("(a n) -> a n", a=1).broadcast_to([128, 1024]))
    t_gn = dma(S, "gn", gffn, a["norm_ffn"].broadcast_to([128, 1024]))
    spent = space["at"]
    wr = room(8, 36)
    rt = room(2, 36)
    gates = room(2, 32)
    wk = room(4, 2, 32)
    t_wr = dma(S, "wr", wr[:, :, 0:4], a["w_router_group"][0].rearrange("(k p) n -> p k n", p=128))
    t_wr = dma(S, "wr", wr[:, :, 4:36], a["w_router_expert"][0].rearrange("(k p) n -> p k n", p=128))
    wrh, wrl = pieces_of("wr", 8, 36)
    rms_scale(X[:, :, :], xs, junk)
    for t in range(2):
        t_v = V.step(lambda e: e.tensor_tensor(xs[:, t, :], xs[:, t, :], gffn, ALU.mult), t_gn)
    t_xn = dma(G, "xn", xn_d.rearrange("(t p) n -> p t n", p=128), xs, t_v)
    t_v = flip(xs, 8, XT, None, t_v)
    PE.wait(t_v, cut((wrh[:, :, :], wrl[:, :, :]), wr, t_wr))
    for t in range(2):
        b = nextbank()
        for k in range(8):
            use_rows(bank(b, 36), XT, k, t, (wrh, wrl), k, 0, 36, k == 0, k == 7)
        to(None, b, 36, fn=lambda e, t=t, b=b: e.tensor_tensor(rt[:, t, :], bank(b, 36), brout, ALU.add))
    st = tiny(16)
    g1, e1, g2_ = st[:, 0:2], st[:, 2:4], st[:, 4:6]
    gl = rt[:, :, 0:4]
    oh, ex = wk[:, 0, :, 0:4], wk[:, 1, :, 0:4]

    def first_hit(vals, n, hit, best, where):
        V.step(lambda e: e.tensor_reduce(best, vals, AX.X, ALU.max))
        V.step(lambda e: e.tensor_tensor(hit, vals, bc(best, 2, n), ALU.is_equal))
        io = iota[:, 0:n].unsqueeze(1).broadcast_to([128, 2, n])
        V.step(lambda e: e.tensor_scalar(hit, hit, -64.0, 64.0, ALU.mult, ALU.add))
        V.step(lambda e: e.tensor_tensor(hit, hit, io, ALU.add))
        V.step(lambda e: e.tensor_reduce(where, hit, AX.X, ALU.min))
        V.step(lambda e: e.tensor_tensor(hit, bc(where, 2, n), io, ALU.is_equal))

    idx = st[:, 6:8]
    first_hit(gl, 4, oh, g1, idx)
    t_v = V.step(lambda e: e.tensor_tensor(ex, gl, bc(g1, 2, 4), ALU.subtract))
    t_s = S.step(lambda e: e.activation(ex, ex, ACT.Exp), t_v)
    V.step(lambda e: e.tensor_reduce(g2_, ex, AX.X, ALU.add), t_s)
    V.step(lambda e: e.reciprocal(g2_, g2_))
    el = wk[:, 1, :, :]
    o1, o2 = wk[:, 2, :, :], wk[:, 3, :, :]
    off = wk[:, 0, :, 4:8]
    V.step(lambda e: e.tensor_scalar(off, oh, -NEG, NEG, ALU.mult, ALU.add))
    for t in range(2):
        e3 = el[:, t, :].rearrange("p (g x) -> p g x", g=4)
        r3 = rt[:, t, 4:36].rearrange("p (g x) -> p g x", g=4)
        V.step(lambda e, t=t, e3=e3, r3=r3: e.tensor_tensor(e3, r3, bc(oh[:, t, :], 4, 8), ALU.mult))
        V.step(lambda e, t=t, e3=e3: e.tensor_tensor(e3, e3, bc(off[:, t, :], 4, 8), ALU.add))
    first_hit(el, 32, o1, g1, idx)
    V.step(lambda e: e.scalar_tensor_tensor(el, o1, NEG, el, ALU.mult, ALU.add))
    first_hit(el, 32, o2, e1, idx)
    t_v = V.step(lambda e: e.tensor_tensor(e1, e1, g1, ALU.subtract))
    t_s = S.step(lambda e: e.activation(e1, e1, ACT.Exp), t_v)
    V.step(lambda e: e.tensor_scalar(g1, e1, 1.0, None, ALU.add), t_s)
    V.step(lambda e: e.reciprocal(g1, g1))
    V.step(lambda e: e.tensor_tensor(g1, g1, g2_, ALU.mult))
    V.step(lambda e: e.tensor_tensor(e1, e1, g1, ALU.mult))
    both = gates
    t_v = V.step(lambda e: e.tensor_tensor(both, o1, o2, ALU.add))
    PE.wait(t_v)
    take(0, 1)
    for t in range(2):
        for j in range(t + 1):
            mm(bank(0, 32, 32 * t), upper[:, j, 128 * t:128 * t + 128], both[:, j, :], j == 0, j == t)
    for j in range(2):
        mm(bank(1, 32), ones, both[:, j, :], j == 0, j == 1)
    Z = room_at(spent, 2, 32)
    ints = space["stack"].enter_context(nc.sbuf_tensor("ints", [128, 144], I32))
    none, val, dest, most = ints[:, 0:64], ints[:, 64:68], ints[:, 68:72], ints[:, 72:73]
    six, gix = ints[:, 80:112], ints[:, 112:144]
    df = tiny(6)
    V.step(lambda e: e.tensor_scalar(Z, bank(0, 64).rearrange("p (t x) -> p t x", t=2), 32.0, -32.0,
                                     ALU.mult, ALU.add), PE.mark())
    V.step(lambda e: e.tensor_tensor(Z, Z, iota.unsqueeze(1).broadcast_to([128, 2, 32]), ALU.add))
    for k, o in ((0, o1), (1, o2)):
        V.step(lambda e: e.tensor_tensor(o, o, Z, ALU.mult))
        V.step(lambda e: e.tensor_reduce(df[:, 2 * k:2 * k + 2], o, AX.X, ALU.add))
    V.step(lambda e: e.tensor_copy(dest, df[:, 0:4]))
    V.step(lambda e: e.tensor_copy(val, C("slot")))
    V.step(lambda e: e.tensor_reduce(df[:, 4:5], bank(1, 32), AX.X, ALU.max))
    V.step(lambda e: e.tensor_copy(most, df[:, 4:5]))
    t_v = V.step(lambda e: e.memset(none, NONE))
    t_l = dma(G, "li", lists.rearrange("(p c) a -> p (c a)", p=128), none, t_v)

    def indirect(name, out_, out_ix, in_, in_ix, bound, *tokens):
        return dma_of(G, name, lambda e: e.indirect_dma_start(
            out=out_, out_offset=None if out_ix is None else bass.IndirectOffsetOnAxis(ap=out_ix, axis=0),
            in_=in_, in_offset=None if in_ix is None else bass.IndirectOffsetOnAxis(ap=in_ix, axis=0),
            bounds_check=bound, oob_is_err=False), *tokens)

    for k in range(4):
        t_l2 = indirect("ls", lists, dest[:, k:k + 1], val[:, k:k + 1], None, 8191, t_l)
    rank = lists.rearrange("(r e) a -> r (e a)", e=32)

    def load_lists(G, r0, *tokens, name="ll"):
        return dma(G, name, six, rank[r0:r0 + 128, :], *tokens)

    def tokens_of(V, t_six):
        Zf = Z[:, 0, :]
        Zg = Z[:, 1, :]
        V.step(lambda e: e.tensor_copy(Zf, six), t_six)
        V.step(lambda e: e.tensor_scalar(Zg, Zf, 256.0, -256.0, ALU.is_ge, ALU.mult))
        V.step(lambda e: e.tensor_tensor(Zf, Zf, Zg, ALU.add))
        return V.step(lambda e: e.tensor_copy(gix, Zf))

    t_gix = tokens_of(V, load_lists(G, 0, t_l2))

    xg = [room(1024), room_at(0, 1024), room_at(1024, 1024)]
    yr = room(2, 1024)
    hs = room(512)
    hr = room(512)
    assert space["at"] <= 9952, space["at"]
    for b in range(3):
        t_z = V.step(lambda e: e.memset(xg[b], 0.0), t_xn)
    fence(t_gix, t_xn)
    xgT = [pieces_of(f"xgT{x}", 8, 128) for x in range(2)]
    hT = [pieces_of(f"hT{x}", 4, 128) for x in range(2)]
    more = tuple(x[:, :] for x in pieces_of("more", PART))
    split_part(more)
    got = {}
    y_done = [(PE.sem, 0)] * 2

    def gather(e_, *tokens):
        if e_ < 32:
            got[e_] = indirect(f"xg{e_ % 3}", xg[e_ % 3], None, xn_d, gix[:, e_:e_ + 1], 255, *tokens)

    def turn_x(e_):
        PE.wait(got[e_])
        for k0 in (0, 4):
            b = 6 + k0 // 4
            take(b)
            for k in range(4):
                PE.put(lambda e: e.transpose(bank(b, 128, 128 * k), xg[e_ % 3][:, 128 * (k0 + k):128 * (k0 + k) + 128],
                                             ident))
            tc = cut([x[:, k0:k0 + 4, :] for x in xgT[e_ % 2]], bank(b).rearrange("p (k i) -> p k i", k=4), PE.mark())
            give(tc, b)
        gather(e_ + 3, PE.mark())
        return tc

    def expert_part(e_, b, p, first=None):
        w = part()
        for k in range(4):
            kk = 4 * p + k
            use_rows(bank(b), xgT[e_ % 2], kk, 0, w, k, 0, 512, kk == 0, kk == 7)
        return done(first)

    def turn_h(e_, tv):
        take(2)
        PE.wait(tv)
        for k in range(4):
            PE.put(lambda e: e.transpose(bank(2, 128, 128 * k), hr[:, 128 * k:128 * k + 128], ident))
        tc = cut([x[:, :, :] for x in hT[e_ % 2]], bank(2).rearrange("p (k i) -> p k i", k=4), PE.mark())
        give(tc, 2)
        return tc

    def expert_down(e_, tc):
        def store():
            o = e_ % 2
            ta = S.step(lambda e: e.activation(yr[:, o, 0:512], bank(4), ACT.Copy), PE.mark(), y_done[o])
            tb = S.step(lambda e: e.activation(yr[:, o, 512:1024], bank(5), ACT.Copy))
            give(ta, 4)
            give(tb, 5)
            y_done[o] = indirect(f"yd{o}", y_d, six[:, e_:e_ + 1], yr[:, o, :], None, 511, tb)

        take(4, 5)
        PE.wait(tc)
        for p in range(2):
            w = part()
            for nn in range(2):
                for k in range(2):
                    kk = 2 * p + k
                    use_rows(bank(4 + nn), hT[e_ % 2], kk, 0, w, k, 512 * nn, 512 * nn + 512, kk == 0, kk == 3)
            done(store if p else None)

    for e_ in range(3):
        gather(e_)
    tx = turn_x(0)
    tv = (PE.sem, 0)
    for e_ in range(32):
        if e_ == 31:
            retired.append(more)
        take(0)
        PE.wait(tx)
        tc = expert_part(e_, 0, 0, (lambda: turn_h(e_ - 1, tv)) if e_ else None)
        ts = expert_part(e_, 0, 1, lambda: S.step(lambda e: e.activation(hs, bank(0), ACT.Silu), PE.mark(), tv))
        give(ts, 0)
        if e_:
            expert_down(e_ - 1, tc)
        take(1)
        tx = expert_part(e_, 1, 0, (lambda: turn_x(e_ + 1)) if e_ < 31 else None)
        tv = expert_part(e_, 1, 1, lambda: V.step(lambda e: e.tensor_tensor(hr, hs, bank(1), ALU.mult), ts, PE.mark()))
        give(tv, 1)
    expert_down(31, turn_h(31, tv))
    assert not any(x is more for x in held.values())
    marks = fence(*y_done)
    SP.wait(*marks, *y_done)

    osem = [sem("o_" + x) for x in ("pe", "v", "s", "g", "sp")]
    engines = (nc.tensor, nc.vector, nc.scalar, nc.gpsimd, nc.sync)

    def rest(live):
        oPE, oV, oS, oG, oSP = (Lane(e, q, n == live) for n, (e, q) in enumerate(zip(engines, osem)))
        for name in ("o_ll", "o_xg", "o_w", "o_yd"):
            if name in dma_count:
                dma_count[name][1] = 0
        xT_ = yr[:, 1, :]
        t_l = load_lists(oG, 128, name="o_ll")
        t_v = tokens_of(oV, t_l)
        oG.wait(t_v)
        free = (oPE.sem, 0)
        for e_ in range(32):
            t_x = dma_of(oG, "o_xg", lambda e: e.indirect_dma_start(
                out=xg[0], out_offset=None, in_=xn_d,
                in_offset=bass.IndirectOffsetOnAxis(ap=gix[:, e_:e_ + 1], axis=0), bounds_check=255,
                oob_is_err=False), free)
            w_src = [a["w_e_gate"][0, e_].rearrange("(k p) n -> p k n", p=128),
                     a["w_e_up"][0, e_].rearrange("(k p) n -> p k n", p=128),
                     a["w_e_down"][0, e_].rearrange("(k p) n -> p k n", p=128)]
            oPE.wait(t_x, (oV.sem, oV.n), (oS.sem, oS.n))
            for k in range(8):
                oPE.put(lambda e: e.transpose(bank(6 + k // 4, 128, 128 * (k % 4)), xg[0][:, 128 * k:128 * k + 128], ident))
            oV.step(lambda e: e.tensor_copy(xT_, PS[:, 3072:4096]), oPE.mark())
            for q in range(2):
                t_w = dma(oSP, "o_w", W0.rearrange("p (k n) -> p k n", k=8), w_src[q], oPE.mark(), free)
                oPE.wait(t_w, (oV.sem, oV.n))
                for k in range(8):
                    oPE.put(lambda e: e.matmul(bank(q), lhsT=xT_[:, 128 * k:128 * k + 128],
                                               rhs=W0[:, 512 * k:512 * k + 512], start=k == 0, stop=k == 7))
                oPE.mark()
            t_s = oS.step(lambda e: e.activation(hs, bank(0), ACT.Silu), (oPE.sem, oPE.n))
            t_v = oV.step(lambda e: e.tensor_tensor(hr, hs, bank(1), ALU.mult), t_s)
            oPE.wait(t_v)
            for k in range(4):
                oPE.put(lambda e: e.transpose(bank(2, 128, 128 * k), hr[:, 128 * k:128 * k + 128], ident))
            t_v = oV.step(lambda e: e.tensor_copy(xT_[:, 0:512], bank(2)), oPE.mark())
            t_w = dma(oSP, "o_w", W0.rearrange("p (k n) -> p k n", k=4), w_src[2], (oPE.sem, oPE.n))
            oPE.wait(t_w, t_v)
            for nn in range(2):
                for k in range(4):
                    oPE.put(lambda e: e.matmul(bank(4 + nn), lhsT=xT_[:, 128 * k:128 * k + 128],
                                               rhs=W0[:, 1024 * k + 512 * nn:1024 * k + 512 * nn + 512],
                                               start=k == 0, stop=k == 3))
            t_v = oV.step(lambda e: e.tensor_copy(yr[:, 0, :], PS[:, 2048:3072]), oPE.mark())
            free = dma_of(oG, "o_yd", lambda e: e.indirect_dma_start(
                out=y_d, out_offset=bass.IndirectOffsetOnAxis(ap=six[:, e_:e_ + 1], axis=0), in_=yr[:, 0, :],
                in_offset=None, bounds_check=511, oob_is_err=False), t_v)
            oV.wait(free)
            oPE.wait(free)
        for lane in (oPE, oV, oS, oG, oSP):
            lane.wait(free, (oPE.sem, oPE.n), (oV.sem, oV.n), (oS.sem, oS.n))

    def branch(n, eng):
        count = eng.value_load(most[0:1, 0:1])
        with eng.If(count > 128):
            rest(n)

    with nc.Block() as block:
        @block.tensor
        def _(eng):
            branch(0, eng)

        @block.vector
        def _(eng):
            branch(1, eng)

        @block.scalar
        def _(eng):
            branch(2, eng)

        @block.gpsimd
        def _(eng):
            branch(3, eng)

        @block.sync
        def _(eng):
            branch(4, eng)

    yy = room_at(5120, 4, 1024)
    t_y = dma(S, "yy", yy, y_d.rearrange("(k p) n -> p k n", p=128))
    for t in range(2):
        for k, g in ((0, g1), (1, e1)):
            V.step(lambda e: e.scalar_tensor_tensor(X[:, t, :], yy[:, 2 * k + t, :], g[:, t:t + 1], X[:, t, :],
                                                    ALU.mult, ALU.add), t_y)
    t_v = rms_scale(X[:, :, :], X[:, :, :], junk, (V.sem, V.n))
    for t in range(2):
        V.step(lambda e: e.tensor_tensor(X[:, t, :], X[:, t, :], gfin, ALU.mult), t_gf)
    fence()

    rot4 = [0]

    def rbank():
        b = rot4[0] % 4
        rot4[0] += 1
        take(b)
        return b

    def swiglu(gain_row):
        phase(5120)
        xs = room(2, 1024)
        junk = room(1024)
        hs = room(4, 256)
        hr = room(4, 256)
        hT = pieces_of("hT", 22, 256)
        t_v = rms_scale(X[:, :, :], xs, junk)
        t_v = flip(xs, 8, XT, gc[:, gain_row:gain_row + 8], t_v)
        start_rows(t_v)
        hsr = [(V.sem, 0)] * 4
        hrr = [(PE.sem, 0)] * 4
        full = {}

        def turn(c):
            for t in range(2):
                b = nextbank()
                slot = 2 * (c % 2) + t
                PE.wait(full[(c, t)])
                for k in range(2):
                    PE.put(lambda e: e.transpose(bank(b, 128, 128 * k), hr[:, slot, 128 * k:128 * k + 128], ident))
                tp = PE.mark()
                hrr[slot] = tp
                tc = cut([x[:, 2 * c:2 * c + 2, 128 * t:128 * t + 128] for x in hT],
                         bank(b, 256).rearrange("p (k i) -> p k i", k=2), tp)
                give(tc, b)
            return tc

        def product(c, bs):
            tp = PE.mark()
            for t in range(2):
                b, slot = bs[t], 2 * (c % 2) + t
                ts = S.step(lambda e: e.activation(hs[:, slot, :], bank(b, 256), ACT.Silu), tp, hsr[slot])
                tv = V.step(lambda e: e.tensor_tensor(hr[:, slot, :], hs[:, slot, :], bank(b, 256, 256), ALU.mult),
                            ts, tp, hrr[slot])
                give(tv, b)
                hsr[slot] = tv
                full[(c, t)] = tv

        for c in range(11):
            bs = (nextbank(), nextbank())
            for p in range(2):
                w = part()
                for t in range(2):
                    for k in range(4):
                        kk = 4 * p + k
                        use_rows(bank(bs[t]), XT, kk, t, w, k, 0, 512, kk == 0, kk == 7)
                if p == 0:
                    done()
                    if c:
                        tc = turn(c - 1)
                else:
                    done(lambda: product(c, bs))
        rotate[:] = [0, 1, 2, 3]
        take(4, 5, 6, 7)
        PE.wait(tc)
        deep_sum(hT, 22, lambda: turn(10))
        rotate[:] = list(range(8))
        for t in range(2):
            for nn in range(2):
                add_to_x(t, nn, 4 + 2 * t + nn, 0.5)
        fence()

    g2 = GAIN["g2"]
    swiglu(g2)

    phase(20736)
    qT = room(8, 256)
    kT = room(8, 256)
    va = room(2, 1024)
    qi = room(4, 256)
    ki = room(256)
    BT = room(2, 8, 256)
    la = space["at"]
    xs = room(2, 1024)
    junk = room(1024)
    space["at"] = la
    sc = room(2, 256)
    w0 = room(256)
    w1_ = room(256)
    La = room(2, 8, 256)
    pa = room(2, 2048)
    wi = tiny(16)
    for t in range(2):
        src = bass.AP(tensor=toep.tensor, offset=255 - 128 * t, ap=[[511, 128], [65536, 8], [1, 256]])
        t_bt = dma(G, "bt", BT[:, t, :, :], src, t_toep)
    t_v = rms_scale(X[:, :, :], xs, junk)
    t_v = flip(xs, 8, XT, gc[:, g2 + 8:g2 + 16], t_v)
    start_rows(t_v)
    project(XT, [cols_job(128 * c, qi[:, c, :]) for c in range(4)])

    def gate(t):
        return lambda e, b: e.tensor_scalar(wi[:, 8 * t:8 * t + 8], bank(b, 8), 8 ** -0.5 / 8, None, ALU.mult)

    project(XT, [cols_job(0, ki[0:64, :], m=72, keep=64)] + [rows_job(t, 64, 72, fn=gate(t)) for t in range(2)])
    t_qi = (V.sem, V.n)
    t_ki = dma(G, "ki", ki[64:128, :], ki[0:64, :], t_qi)
    best = tiny(8)

    def index(t, half):
        take(0, 1)
        PE.wait(t_qi, t_ki)
        for i in range(4):
            h = head_at(4 * half + i)
            lo = 64 * (h % 2)
            mm(PS[:, 256 * i:256 * i + 256], qi[lo:lo + 64, h // 2, 128 * t:128 * t + 128], ki[lo:lo + 64, :], True, True)
        for i in range(4):
            wcol = wi[:, 8 * t + head_at(4 * half + i):8 * t + head_at(4 * half + i) + 1]
            first = half == 0 and i == 0
            o = sc[:, t, :] if first else w0
            t_v = V.step(lambda e: e.tensor_scalar(o, PS[:, 256 * i:256 * i + 256], 0.0, wcol, ALU.max, ALU.mult),
                         PE.mark())
            if not first:
                V.step(lambda e: e.tensor_tensor(sc[:, t, :], sc[:, t, :], w0, ALU.add))
        give(t_v, 0, 1)

    def choose(t):
        V.step(lambda e: e.tensor_tensor(sc[:, t, :], sc[:, t, :], causal[:, t, :], ALU.add))
        cur = sc[:, t, :]
        for r in range(8):
            nxt = w0 if r % 2 == 0 else w1_
            V.step(lambda e: e.max(best, cur))
            V.step(lambda e: e.match_replace(nxt, best, cur, GONE))
            cur = nxt
        V.step(lambda e: e.tensor_scalar(cur, cur, -2.0e38, None, ALU.is_gt))
        V.step(lambda e: e.scalar_tensor_tensor(sc[:, t, :], cur, NEG, causal[:, t, :], ALU.mult, ALU.add))

    rotate[:] = [2, 3, 4, 5, 6, 7]
    between += [
        [lambda: index(0, 0)],
        [lambda: index(0, 1)],
        [lambda: choose(0)],
        [lambda: index(1, 0)],
        [lambda: index(1, 1)],
        [lambda: choose(1)],
    ] + [[]] * 6
    for dst in (qT, kT):
        for u in range(2):
            project(XT, [cols_job(128 * c, dst[:, 4 * u + c, :]) for c in range(4)])
    for u in range(2):
        project(XT, [rows_job(t, 0, 512, va[:, t, 512 * u:512 * u + 512]) for t in range(2)])
    assert not between
    rotate[:] = list(range(8))
    fence(t_ki, t_bt)
    sc4 = [PS[:, 2048 * t:2048 * t + 2048].rearrange("p (h s) -> p h s", h=8) for t in T]
    m8, d8 = [[x[:, 8 * t:8 * t + 8] for t in T] for x in (mx, dn)]
    for t in T:
        for h in range(8):
            mm(sc4[t][:, h, :], qT[:, h, 128 * t:128 * t + 128], kT[:, h, :], True, True)
        V.step(lambda e: e.scalar_tensor_tensor(La[:, t], sc4[t], 128 ** -0.5, BT[:, t, :, :], ALU.mult, ALU.add),
               PE.mark())
    t_x = {}
    for t in T:
        V.step(lambda e: e.tensor_tensor(La[:, t], La[:, t], sc[:, t, :].unsqueeze(1).broadcast_to([128, 8, 256]),
                                         ALU.add))
        V.step(lambda e: e.tensor_reduce(m8[t], La[:, t], AX.X, ALU.max))
        t_v = V.step(lambda e: e.tensor_tensor(La[:, t], La[:, t], bc(m8[t], 8, 256), ALU.subtract))
        t_x[t] = S.step(lambda e: e.activation(La[:, t], La[:, t], ACT.Exp), t_v)
    for t in T:
        V.step(lambda e: e.tensor_reduce(d8[t], La[:, t], AX.X, ALU.add), t_x[t])
        V.step(lambda e: e.reciprocal(d8[t], d8[t]))
        t_v = V.step(lambda e: e.tensor_tensor(La[:, t], La[:, t], bc(d8[t], 8, 256), ALU.mult))
        PE.wait(t_v)
        for n in range(16):
            PE.put(lambda e: e.transpose(PS[:, 2048 * t + 128 * n:2048 * t + 128 * n + 128],
                                         La[:, t, n // 2, 128 * (n % 2):128 * (n % 2) + 128], ident))
        t_x[t] = S.step(lambda e: e.activation(pa[:, t, :], PS[:, 2048 * t:2048 * t + 2048], ACT.Copy), PE.mark())
    PE.wait(t_x[0])
    for t in T:
        PE.wait(t_x[t])
        for h in range(8):
            for j in range(2):
                mm(PS[:, 1024 * t + 128 * h:1024 * t + 128 * h + 128], va[:, j, 128 * h:128 * h + 128],
                   pa[:, t, 128 * (2 * h + j):128 * (2 * h + j) + 128], j == 0, j == 1)
        cut([x[:, :, 128 * t:128 * t + 128] for x in XT],
            PS[:, 1024 * t:1024 * t + 1024].rearrange("p (h s) -> p h s", h=8), PE.mark())
    fence()
    add_out()
    fence()

    swiglu(g2 + 16)
    swiglu(g2 + 24)

    phase(19456)
    uu = room(2, 3072)
    vv = room(2, 3072)
    bb = room(4, 1024)
    wsp = room(8, 128)
    wst = room(8, 128)
    xs = vv[:, 0, 0:2048].rearrange("p (t n) -> p t n", t=2)
    junk = vv[:, 1, 0:1024]
    zb = room(2, 512)
    bsp = tiny(8)
    t_w = dma(G, "wsp", wsp, a["b_w_sp_2"][0].rearrange("g t s -> t g s"))
    t_bsp = dma(G, "bsp", rows[0:8, :], a["b_b_sp_2"][0])
    t_v = rms_scale(X[:, :, :], xs, junk)
    t_v = flip(xs, 8, XT, gc[:, g2 + 32:g2 + 40], t_v)
    for q in range(2):
        b = nextbank()
        PE.wait(t_w)
        for k in range(4):
            PE.put(lambda e, b=b, k=k, q=q: e.transpose(bank(b, 128, 128 * k), wsp[:, 4 * q + k, :], ident))
        to(None, b, 512, fn=lambda e, b=b, q=q: e.tensor_tensor(
            wst[:, 4 * q:4 * q + 4, :], bank(b).rearrange("p (k i) -> p k i", k=4),
            upper[:, 0, 0:128].unsqueeze(1).broadcast_to([128, 4, 128]), ALU.mult))
    b = nextbank()
    PE.wait(t_bsp)
    PE.put(lambda e, b=b: e.transpose(bank(b, 8), rows[0:8, :], ident[0:8, 0:8]))
    to(bsp, b, 8)
    start_rows(t_v)
    bread = [(V.sem, 0)] * 4
    lin, gain, shift = a["b_b_in_2"], a["b_ln_g_2"], a["b_ln_b_2"]
    LN_AFTER = {6: (0,), 7: (1,), 8: (2, 3), 9: (4,), 10: (5,)}
    bias_rows = [(lin[:, 3072 + 512 * c:3584 + 512 * c],) for c in range(6)]
    for c in range(6):
        bias_rows.append((lin[:, 512 * c:512 * c + 512],))
        bias_rows += [(gain[:, 512 * x:512 * x + 512], shift[:, 512 * x:512 * x + 512]) for x in LN_AFTER.get(6 + c, ())]
    fetched = []

    def fetch():
        n = len(fetched)
        if n < len(bias_rows):
            s = n % 4
            for k, src in enumerate(bias_rows[n]):
                t_p = dma(G, f"bp{s}", bb[:, s, 512 * k:512 * k + 512], src.broadcast_to([128, 512]), bread[s])
            fetched.append(t_p)

    def bias_piece():
        n = turns[0]
        turns[0] += 1
        fetch()
        return n % 4, fetched[n]

    fetch()
    fetch()
    zread = [(S.sem, 0)] * 2
    bst = tiny(2 * 36)
    mv = tiny(4)
    turns = [0]

    def normed(c):
        s, t_p = bias_piece()
        for t in range(2):
            vp = vv[:, t, 512 * c:512 * c + 512]
            t_n = V.step(lambda e: e.tensor_scalar(vp, vp, mv[:, 2 * t:2 * t + 1], mv[:, 2 * t + 1:2 * t + 2],
                                                   ALU.subtract, ALU.mult))
            G.step(lambda e: e.tensor_tensor(vp, vp, bb[:, s, 0:512], ALU.mult), t_p, t_n)
            bread[s] = G.step(lambda e: e.tensor_tensor(vp, vp, bb[:, s, 512:1024], ALU.add))

    pieces = [(vv, 3072, c) for c in range(6)] + [(uu, 0, c) for c in range(6)]
    for n, (dst, base, c) in enumerate(pieces):
        s, t_p = bias_piece()
        bs = (nextbank(), nextbank())
        for p in range(2):
            w = part()
            for t in range(2):
                for k in range(4):
                    kk = 4 * p + k
                    use_rows(bank(bs[t]), XT, kk, t, w, k, 0, 512, kk == 0, kk == 7)
            done()
        for t in range(2):
            b = bs[t]
            tv = V.step(lambda e: e.tensor_tensor(zb[:, t, :], bank(b), bb[:, s, 0:512], ALU.add),
                        PE.mark(), t_p, zread[t])
            give(tv, b)
            zread[t] = S.step(lambda e: e.activation(dst[:, t, 512 * c:512 * c + 512], zb[:, t, :],
                                                     ACT.Gelu_apprx_tanh), tv)
        bread[s] = tv
        if n < 6:
            for t in range(2):
                V.step(lambda e: e.bn_stats(bst[:, 36 * t + 6 * c:36 * t + 6 * c + 6],
                                            vv[:, t, 512 * c:512 * c + 512]), zread[t])
        if n == 5:
            for t in range(2):
                V.step(lambda e: e.bn_aggr(mv[:, 2 * t:2 * t + 2], bst[:, 36 * t:36 * t + 36]))
                V.step(lambda e: e.tensor_scalar(mv[:, 2 * t + 1:2 * t + 2], mv[:, 2 * t + 1:2 * t + 2], 1e-6, None,
                                                 ALU.add))
                rsqrt(mv[:, 2 * t + 1:2 * t + 2], 1)
        for x in LN_AFTER.get(n, ()):
            normed(x)
    PE.wait((V.sem, V.n), (G.sem, G.n))
    V.wait((S.sem, S.n))
    for t in range(2):
        for g in range(8):
            b = rbank()
            mm(bank(b, 384), wst[:, g, :], vv[:, t, 384 * g:384 * g + 384], True, True)
            up = uu[:, t, 384 * g:384 * g + 384]
            to(None, b, 384, fn=lambda e, b=b, g=g, up=up: e.scalar_tensor_tensor(
                up, bank(b, 384), bsp[:, g:g + 1], up, ALU.add, ALU.mult))
    fence()
    space["stack"].close()
    space["stack"] = ctx.enter_context(ExitStack())
    y = space["stack"].enter_context(nc.sbuf_tensor("y", [128, 2, 3072], F32))
    yT = pieces_of("yT", 24, 256)
    t_v = flip(y, 24, yT, None)
    take(4, 5, 6, 7)
    PE.wait(t_v)
    deep_sum(yT, 24)
    for t in range(2):
        for nn in range(2):
            add_to_x(t, nn, 4 + 2 * t + nn)
    fence()

    swiglu(g2 + 40)

    phase(4096)
    xs = room(2, 1024)
    junk = room(1024)
    gfin = room(1024)
    t_gf = dma(S, "gf", gfin, a["final_g_2"].rearrange("(a n) -> a n", a=1).broadcast_to([128, 1024]))
    rms_scale(X[:, :, :], xs, junk)
    for t in range(2):
        t_v = V.step(lambda e: e.tensor_tensor(xs[:, t, :], xs[:, t, :], gfin, ALU.mult), t_gf)
    t_o = dma(SP, "o", out[0].rearrange("(t p) n -> p t n", p=128), xs, t_v)
    SP.wait(t_o)
    assert at["use"] == len(parts), (at, len(parts))


_NAMES = ["x", "mem", "norm_mix", "w_in", "b_gates", "conv_w", "conv_b", "att_sinks", "norm_att_out", "norm_ml_out",
          "w_out", "norm_cross", "norm_mem", "w_cq", "w_ckv", "w_co", "norm_ffn", "w_router_group", "b_router_group",
          "w_router_expert", "b_router_expert", "w_e_gate", "w_e_up", "w_e_down", "norm_final", "norm_g_2",
          "final_g_2", "ffn_w_in_2", "ffn_w_out_2", "rel_table_2", "a_w_in_2", "a_w_out_2", "b_w_in_2", "b_b_in_2",
          "b_ln_g_2", "b_ln_b_2", "b_w_sp_2", "b_b_sp_2", "b_w_out_2"]


def kernel(**inputs):
    import concourse.bacc as _bacc
    from concourse.bass_utils import run_bass_kernel_spmd as _run

    nc = _bacc.Bacc("TRN2", target_bir_lowering=False, num_devices=1)
    cst, hot = shape_constants()
    arrays, a = {}, {}
    for name in _NAMES + ["cst", "hot"]:
        v = np.ascontiguousarray({"cst": cst, "hot": hot}[name] if name in ("cst", "hot") else inputs[name])
        arrays["in_" + name] = v
        a[name] = nc.dram_tensor("in_" + name, v.shape, mybir.dt.from_np(v.dtype), kind="ExternalInput").ap()
    out = nc.dram_tensor("out_0", (1, 256, 1024), F32, kind="ExternalOutput").ap()
    build(nc, a, out)
    r = _run(nc, [arrays], core_ids=[0])
    return r.results[0]["out_0"]
```
